# Optimizing a Trainium2 kernel written in Bass

```python
import jax, jax.numpy as jnp
from jax import lax
import numpy as np

D_MODEL = 1024
BATCH = 1
SEQ = 256
DEPTH = 2
DEC_BATCH = 1
DEC_SEQ = 32
PAST_LEN = 128

CHUNK = 64
EPS = 1e-6
ROPE_THETA = 10000.0
NEG = -1e30
A_HEADS = 8
A_KV_HEADS = 2
A_GROUP = A_HEADS // A_KV_HEADS
A_HEAD_DIM = 64
WINDOW = 128
WIN_CHUNKS = WINDOW // CHUNK
A_SCALE = A_HEAD_DIM ** -0.5
B_HEADS = 8
B_NOPE = 64
B_ROPE = 32
B_V = 64
B_QK = B_NOPE + B_ROPE
Q_LORA = 256
KV_LORA = 128
B_SCALE = B_QK ** -0.5
Q_BLOCK = 128
MIX_WIDTH = A_HEADS * A_HEAD_DIM + B_HEADS * B_V
S0 = A_HEADS * A_HEAD_DIM
S1 = S0 + A_KV_HEADS * A_HEAD_DIM
S2 = S1 + A_KV_HEADS * A_HEAD_DIM
S3 = S2 + Q_LORA
S4 = S3 + KV_LORA
IN_WIDTH = S4 + B_ROPE
D_FF = 2816
N_EXPERTS = 8
TOP_K = 2
N_DENSE = (DEPTH + 1) // 2
N_MOE = DEPTH // 2

kernel_name = 'hybrid_swa_sink_mla_streaming_step'

def rms_norm(x, g):
    xf = x.astype(jnp.float32)
    y = xf * lax.rsqrt(jnp.mean(xf * xf, axis=-1, keepdims=True) + EPS)
    return (y * g.astype(jnp.float32)).astype(x.dtype)

def rope(x, pos):
    half = x.shape[-1] // 2
    inv = ROPE_THETA ** (-(jnp.arange(half, dtype=jnp.float32) / half))
    ang = pos.astype(jnp.float32)[:, None] * inv[None, :]
    cos = jnp.cos(ang)[:, None, :]
    sin = jnp.sin(ang)[:, None, :]
    xf = x.astype(jnp.float32)
    x1, x2 = xf[..., :half], xf[..., half:]
    return jnp.concatenate([x1 * cos - x2 * sin, x2 * cos + x1 * sin], axis=-1).astype(x.dtype)

def project(h, pos, w_in, a_q_norm, a_k_norm, b_cq_norm, b_w_uq, b_ckv_norm, b_qn_norm, b_qr_norm, b_kr_norm):
    B, T, _ = h.shape
    z = jnp.einsum('btd,de->bte', h, w_in)
    q_a = rope(rms_norm(z[..., :S0].reshape(B, T, A_HEADS, A_HEAD_DIM), a_q_norm), pos)
    k_a = rope(rms_norm(z[..., S0:S1].reshape(B, T, A_KV_HEADS, A_HEAD_DIM), a_k_norm), pos)
    v_a = z[..., S1:S2].reshape(B, T, A_KV_HEADS, A_HEAD_DIM)
    cq = rms_norm(z[..., S2:S3], b_cq_norm)
    q_b = jnp.einsum('btc,ce->bte', cq, b_w_uq).reshape(B, T, B_HEADS, B_QK)
    q_nope = rms_norm(q_b[..., :B_NOPE], b_qn_norm)
    q_rope = rope(rms_norm(q_b[..., B_NOPE:], b_qr_norm), pos)
    ckv = rms_norm(z[..., S3:S4], b_ckv_norm)
    k_rope = rope(rms_norm(z[..., S4:], b_kr_norm)[:, :, None, :], pos)[:, :, 0, :]
    return q_a, k_a, v_a, q_nope, q_rope, ckv, k_rope

def sink_attend(q, k, v, valid, sinks):
    s = jnp.einsum('bnqkgd,bnskd->bnkgqs', q, k).astype(jnp.float32) * A_SCALE
    s = jnp.where(valid[None, :, None, None, None, :], s, NEG)
    sink = sinks.astype(jnp.float32).reshape(A_KV_HEADS, A_GROUP)[None, None, :, :, None, None]
    sink = jnp.broadcast_to(sink, s.shape[:-1] + (1,))
    p = jax.nn.softmax(jnp.concatenate([s, sink], axis=-1), axis=-1)[..., :-1].astype(v.dtype)
    return jnp.einsum('bnkgqs,bnskd->bnqkgd', p, v)

def swa_prompt(q_a, k_a, v_a, sinks):
    B, T = q_a.shape[:2]
    nC = T // CHUNK
    q = q_a.reshape(B, nC, CHUNK, A_KV_HEADS, A_GROUP, A_HEAD_DIM)

    def band(x):
        xp = jnp.pad(x, ((0, 0), (WINDOW, 0), (0, 0), (0, 0)))
        xp = xp.reshape(B, nC + WIN_CHUNKS, CHUNK, A_KV_HEADS, A_HEAD_DIM)
        return jnp.concatenate([xp[:, j:j + nC] for j in range(WIN_CHUNKS + 1)], axis=2)

    key_chunk_off = jnp.arange((WIN_CHUNKS + 1) * CHUNK)[None, :] // CHUNK
    valid = jnp.arange(nC)[:, None] + key_chunk_off - WIN_CHUNKS >= 0
    o = sink_attend(q, band(k_a), band(v_a), valid, sinks)
    return o.reshape(B, T, A_HEADS * A_HEAD_DIM)

def swa_sample(q_a, k_a, v_a, cache_k, cache_v, sinks):
    B, T = q_a.shape[:2]
    k = jnp.concatenate([cache_k, k_a], axis=1)[:, None]
    v = jnp.concatenate([cache_v, v_a], axis=1)[:, None]
    q = q_a.reshape(B, 1, T, A_KV_HEADS, A_GROUP, A_HEAD_DIM)
    valid = jnp.ones((1, k.shape[2]), dtype=bool)
    o = sink_attend(q, k, v, valid, sinks)
    return o.reshape(B, T, A_HEADS * A_HEAD_DIM)

def mla_kv(ckv, w_ukv, kn_norm):
    B, T, _ = ckv.shape
    kv = jnp.einsum('btc,ce->bte', ckv, w_ukv).reshape(B, T, B_HEADS, B_NOPE + B_V)
    return rms_norm(kv[..., :B_NOPE], kn_norm), kv[..., B_NOPE:]

def mla_scores(qn, qr, kn, kr):
    s = jnp.einsum('bqhd,bkhd->bhqk', qn, kn) + jnp.einsum('bqhd,bkd->bhqk', qr, kr)
    return s.astype(jnp.float32) * B_SCALE

def mla_prompt(q_nope, q_rope, ckv, k_rope, w_ukv, kn_norm):
    B, T = q_nope.shape[:2]
    nB = T // Q_BLOCK
    k_nope, v = mla_kv(ckv, w_ukv, kn_norm)
    key_chunk = jnp.arange(T) // CHUNK

    def block(args):
        i, qn, qr = args
        s = mla_scores(qn, qr, k_nope, k_rope)
        q_chunk = (i * Q_BLOCK + jnp.arange(Q_BLOCK)) // CHUNK
        s = jnp.where(key_chunk[None, :] <= q_chunk[:, None], s, NEG)
        p = jax.nn.softmax(s, axis=-1).astype(v.dtype)
        return jnp.einsum('bhqk,bkhd->bqhd', p, v)

    qn_b = q_nope.reshape(B, nB, Q_BLOCK, B_HEADS, B_NOPE).transpose(1, 0, 2, 3, 4)
    qr_b = q_rope.reshape(B, nB, Q_BLOCK, B_HEADS, B_ROPE).transpose(1, 0, 2, 3, 4)
    o = lax.map(block, (jnp.arange(nB), qn_b, qr_b))
    return o.transpose(1, 0, 2, 3, 4).reshape(B, T, B_HEADS * B_V)

def mla_sample(q_nope, q_rope, ckv, k_rope, cache_ckv, cache_kr, w_ukv, kn_norm):
    B, T = q_nope.shape[:2]
    k_nope, v = mla_kv(jnp.concatenate([cache_ckv, ckv], axis=1), w_ukv, kn_norm)
    kr = jnp.concatenate([cache_kr, k_rope], axis=1)
    p = jax.nn.softmax(mla_scores(q_nope, q_rope, k_nope, kr), axis=-1).astype(v.dtype)
    return jnp.einsum('bhqk,bkhd->bqhd', p, v).reshape(B, T, B_HEADS * B_V)

def token_mix(h, pos, cache, w_in, a_q_norm, a_k_norm, a_sinks, b_cq_norm, b_w_uq, b_ckv_norm,
              b_w_ukv, b_qn_norm, b_qr_norm, b_kn_norm, b_kr_norm, w_o):
    q_a, k_a, v_a, q_nope, q_rope, ckv, k_rope = project(
        h, pos, w_in, a_q_norm, a_k_norm, b_cq_norm, b_w_uq, b_ckv_norm, b_qn_norm, b_qr_norm, b_kr_norm)
    if cache is None:
        o_a = swa_prompt(q_a, k_a, v_a, a_sinks)
        o_b = mla_prompt(q_nope, q_rope, ckv, k_rope, b_w_ukv, b_kn_norm)
        new = (k_a[:, -WINDOW:], v_a[:, -WINDOW:], ckv, k_rope)
    else:
        ck, cv, cc, cr = cache
        o_a = swa_sample(q_a, k_a, v_a, ck, cv, a_sinks)
        o_b = mla_sample(q_nope, q_rope, ckv, k_rope, cc, cr, b_w_ukv, b_kn_norm)
        new = (k_a, v_a, ckv, k_rope)
    o = jnp.concatenate([o_a, o_b], axis=-1)
    return jnp.einsum('btm,md->btd', o, w_o), new

def swiglu(h, wg, wu, wd):
    g = jnp.einsum('btd,df->btf', h, wg)
    u = jnp.einsum('btd,df->btf', h, wu)
    return jnp.einsum('btf,fd->btd', jax.nn.silu(g) * u, wd)

def moe(h, router, wg, wu, wd):
    logits = jnp.einsum('btd,de->bte', h, router).astype(jnp.float32)
    vals, idx = lax.top_k(logits, TOP_K)
    gates = jax.nn.softmax(vals, axis=-1)
    comb = jnp.sum(jax.nn.one_hot(idx, N_EXPERTS, dtype=jnp.float32) * gates[..., None], axis=-2)
    out = jnp.zeros_like(h)
    for e in range(N_EXPERTS):
        out = out + comb[..., e:e + 1].astype(h.dtype) * swiglu(h, wg[e], wu[e], wd[e])
    return out

def channel_mix(h, l, ffn_w_gate, ffn_w_up, ffn_w_down, moe_router, moe_w_gate, moe_w_up, moe_w_down):
    i = l // 2
    if l % 2 == 0:
        return swiglu(h, ffn_w_gate[i], ffn_w_up[i], ffn_w_down[i])
    return moe(h, moe_router[i], moe_w_gate[i], moe_w_up[i], moe_w_down[i])

def setup_inputs(seed: int = 0) -> dict:
    key = jax.random.key(seed)
    ks = jax.random.split(key, 28)
    f32 = jnp.float32

    def nrm(k, shape, scale):
        return jax.random.normal(k, shape, f32) * scale

    def gain(k, shape):
        return 1.0 + 0.1 * jax.random.normal(k, shape, f32)

    return {
        'x_prompt': nrm(ks[0], (BATCH, SEQ, D_MODEL), 1.0),
        'x_sample': nrm(ks[1], (DEC_BATCH, DEC_SEQ, D_MODEL), 1.0),
        'cache_swa_k': nrm(ks[2], (DEPTH, DEC_BATCH, WINDOW, A_KV_HEADS, A_HEAD_DIM), 1.0),
        'cache_swa_v': nrm(ks[3], (DEPTH, DEC_BATCH, WINDOW, A_KV_HEADS, A_HEAD_DIM), 1.0),
        'cache_mla_ckv': nrm(ks[4], (DEPTH, DEC_BATCH, PAST_LEN, KV_LORA), 1.0),
        'cache_mla_krope': nrm(ks[5], (DEPTH, DEC_BATCH, PAST_LEN, B_ROPE), 1.0),
        'ln_attn': gain(ks[6], (DEPTH, D_MODEL)),
        'w_in': nrm(ks[7], (DEPTH, D_MODEL, IN_WIDTH), D_MODEL ** -0.5),
        'a_q_norm': gain(ks[8], (DEPTH, A_HEAD_DIM)),
        'a_k_norm': gain(ks[9], (DEPTH, A_HEAD_DIM)),
        'a_sinks': nrm(ks[10], (DEPTH, A_HEADS), 0.5),
        'b_cq_norm': gain(ks[11], (DEPTH, Q_LORA)),
        'b_w_uq': nrm(ks[12], (DEPTH, Q_LORA, B_HEADS * B_QK), Q_LORA ** -0.5),
        'b_ckv_norm': gain(ks[13], (DEPTH, KV_LORA)),
        'b_w_ukv': nrm(ks[14], (DEPTH, KV_LORA, B_HEADS * (B_NOPE + B_V)), KV_LORA ** -0.5),
        'b_qn_norm': gain(ks[15], (DEPTH, B_NOPE)),
        'b_qr_norm': gain(ks[16], (DEPTH, B_ROPE)),
        'b_kn_norm': gain(ks[17], (DEPTH, B_NOPE)),
        'b_kr_norm': gain(ks[18], (DEPTH, B_ROPE)),
        'w_o': nrm(ks[19], (DEPTH, MIX_WIDTH, D_MODEL), MIX_WIDTH ** -0.5),
        'ln_ffn': gain(ks[20], (DEPTH, D_MODEL)),
        'ffn_w_gate': nrm(ks[21], (N_DENSE, D_MODEL, D_FF), D_MODEL ** -0.5),
        'ffn_w_up': nrm(ks[22], (N_DENSE, D_MODEL, D_FF), D_MODEL ** -0.5),
        'ffn_w_down': nrm(ks[23], (N_DENSE, D_FF, D_MODEL), D_FF ** -0.5),
        'moe_router': nrm(ks[24], (N_MOE, D_MODEL, N_EXPERTS), D_MODEL ** -0.5),
        'moe_w_gate': nrm(ks[25], (N_MOE, N_EXPERTS, D_MODEL, D_FF), D_MODEL ** -0.5),
        'moe_w_up': nrm(ks[26], (N_MOE, N_EXPERTS, D_MODEL, D_FF), D_MODEL ** -0.5),
        'moe_w_down': nrm(ks[27], (N_MOE, N_EXPERTS, D_FF, D_MODEL), D_FF ** -0.5),
    }

def reference(x_prompt, x_sample, cache_swa_k, cache_swa_v, cache_mla_ckv, cache_mla_krope,
              ln_attn, w_in, a_q_norm, a_k_norm, a_sinks, b_cq_norm, b_w_uq, b_ckv_norm, b_w_ukv,
              b_qn_norm, b_qr_norm, b_kn_norm, b_kr_norm, w_o, ln_ffn,
              ffn_w_gate, ffn_w_up, ffn_w_down, moe_router, moe_w_gate, moe_w_up, moe_w_down):
    pos_p = jnp.arange(x_prompt.shape[1], dtype=jnp.int32)
    pos_s = PAST_LEN + jnp.arange(x_sample.shape[1], dtype=jnp.int32)
    xp, xs = x_prompt, x_sample
    pk, pv, pc, pr = [], [], [], []
    sk, sv, sc, sr = [], [], [], []
    for l in range(DEPTH):
        lw = (w_in[l], a_q_norm[l], a_k_norm[l], a_sinks[l], b_cq_norm[l], b_w_uq[l], b_ckv_norm[l],
              b_w_ukv[l], b_qn_norm[l], b_qr_norm[l], b_kn_norm[l], b_kr_norm[l], w_o[l])
        fw = (ffn_w_gate, ffn_w_up, ffn_w_down, moe_router, moe_w_gate, moe_w_up, moe_w_down)
        o, new_p = token_mix(rms_norm(xp, ln_attn[l]), pos_p, None, *lw)
        xp = xp + o
        xp = xp + channel_mix(rms_norm(xp, ln_ffn[l]), l, *fw)
        cache = (cache_swa_k[l], cache_swa_v[l], cache_mla_ckv[l], cache_mla_krope[l])
        o, new_s = token_mix(rms_norm(xs, ln_attn[l]), pos_s, cache, *lw)
        xs = xs + o
        xs = xs + channel_mix(rms_norm(xs, ln_ffn[l]), l, *fw)
        pk.append(new_p[0]); pv.append(new_p[1]); pc.append(new_p[2]); pr.append(new_p[3])
        sk.append(new_s[0]); sv.append(new_s[1]); sc.append(new_s[2]); sr.append(new_s[3])
    return (xp, xs, jnp.stack(pk), jnp.stack(pv), jnp.stack(pc), jnp.stack(pr),
            jnp.stack(sk), jnp.stack(sv), jnp.stack(sc), jnp.stack(sr))


_drawn_inputs = setup_inputs


def setup_inputs(seed=0):
    import zlib

    import numpy as np

    out = dict(_drawn_inputs(seed))
    spreads = {}
    factors = {'a_sinks': 8.0, 'b_qr_norm': 2.721}
    for name, (base, spread) in spreads.items():
        noise = np.random.default_rng([zlib.crc32(name.encode()), seed]).standard_normal(out[name].shape)
        drawn = base * np.exp(spread * noise) if base else spread * noise
        out[name] = __import__('jax').numpy.asarray(drawn.astype(out[name].dtype))
    for name, factor in factors.items():
        out[name] = (out[name] * factor).astype(out[name].dtype)
    return out
```

```python
from contextlib import ExitStack

import concourse.bass as bass
from concourse import mybir

F32 = mybir.dt.float32
I32 = mybir.dt.int32
U32 = mybir.dt.uint32
ALU = mybir.AluOpType
ACT = mybir.ActivationFunctionType
AX_X = mybir.AxisListType.X

P = 128
D = 1024
KD = D // P
SEQ, DEC = 256, 32
TOK = SEQ + DEC
ROWS = [P, P, DEC]
TOFF = [0, P, 2 * P]
CHUNK, WINDOW = 64, 128
HEADS, KVH, HD = 8, 2, 64
GRP = HEADS // KVH
NOPE, ROPE, VD, QK = 64, 32, 64, 96
QL, KL = 256, 128
S0, S1, S2 = HEADS * HD, HEADS * HD + KVH * HD, HEADS * HD + 2 * KVH * HD
S3, S4 = S2 + QL, S2 + QL + KL
IN_W = S4 + ROPE
DFF = 2816
FT = DFF // P
NE = 8
DEPTH = 2
EPS = 1e-6
A_SCALE, B_SCALE = HD ** -0.5, QK ** -0.5
KEYS = 4
KOFF = [0, 128, 256, 384]
NKEY = 416
KROWS = [P, P, P, DEC]
KT_OF_TILE = [0, 1, 3]
KEYS_OF = [(0, 1), (0, 2), (2, 4)]
SLOTS = P
ROUNDS = (TOK + SLOTS - 1) // SLOTS
NJ = NE * ROUNDS
CW = 512
CHUNKS = (DFF + CW - 1) // CW
WIDTH = [min(CW, DFF - CW * c) for c in range(CHUNKS)]
RING = 9
SLOT_W = 2048
ABSENT = 1000.0

CONST = {}
_at = 0
for _name, _w in (("ident", P), ("upper", P), ("ones", P), ("iota", P), ("c64", 2 * HD), ("s64", 2 * HD),
                  ("c32", 2 * ROPE), ("s32", 2 * ROPE), ("mask0", P), ("mask1a", 2 * P), ("mask1b", 2 * P),
                  ("inv_a", 13), ("inv_b", 16), ("eps", 1)):
    CONST[_name] = (_at, _w)
    _at += _w
CONST_W = _at

GAIN = {}
_at = 0
for _name, _w in (("a_q_norm", HD), ("a_k_norm", HD), ("b_cq_norm", QL), ("b_ckv_norm", KL), ("b_qn_norm", NOPE),
                  ("b_qr_norm", ROPE), ("b_kn_norm", NOPE), ("b_kr_norm", ROPE), ("a_sinks", HEADS)):
    GAIN[_name] = (_at, _w)
    _at += _w
GAIN_W = _at

ITEMS = [("q", 0), ("k", 0), ("q", 1), ("k", 1), ("k", 2), ("q", 2), ("k", 3)]
GROUPS = [(typ, t, hg) for typ in "ab" for t in range(3) for hg in range(2)]


def weight_plan():
    plan = []
    for layer in range(DEPTH):
        plan += [("in", layer, c, h) for c in range(2) for h in range(2)] + [("in", layer, 2, 0)]
        plan += [("uq", layer), ("ukv", layer)]
        plan += [("wo", layer, c, h) for c in range(2) for h in range(2)]
        plan += [None] * (-len(plan) % RING)
        if layer == 0:
            plan += [(m, c, h) for c in range(CHUNKS) for m in ("gate", "up") for h in range(2)]
            plan += [("down", c, g) for c in range(2) for g in range(6)]
            plan += [None] * (-len(plan) % RING)
    return plan


def expert_plan():
    order = []
    for c in range(CHUNKS + 2):
        if c < CHUNKS:
            order += [(m, c, h) for m in ("gate", "up") for h in range(2)]
        if c >= 2:
            order += [("down", c - 2, h) for h in range(2)]
    return order


def psum_plan():
    jobs = []
    for l in range(DEPTH):
        jobs += [("h", l, t) for t in range(3)]
        for t in range(3):
            jobs += [("za", l, t), ("zc", l, t)]
        jobs += [("tc", l)] + [("tq", l, t) for t in range(3)]
        for i in range(len(ITEMS) + 1):
            if i < len(ITEMS):
                jobs.append(("item", l, i))
            if i >= 1:
                jobs.append(("titem", l, i - 1))
        for g in range(len(GROUPS) + 2):
            if g < len(GROUPS):
                jobs.append(("s", l, g))
            if 1 <= g <= len(GROUPS):
                jobs.append(("p", l, g - 1))
            if g >= 2:
                jobs.append(("o", l, g - 2))
        jobs += [("to", l, t) for t in range(3)]
        for d in range(KD + 1):
            if d < KD:
                jobs.append(("wo", l, d))
            if d >= 1:
                jobs.append(("ty", l, d - 1))
        jobs += [("hf", l, t) for t in range(3)]
        if l == 0:
            jobs += [("gu", f) for f in range(FT)]
            for d in range(KD + 1):
                if d < KD:
                    jobs.append(("dn", d))
                if d >= 1:
                    jobs.append(("tz", d - 1))
        else:
            jobs += [("router",), ("pos",)]
    return jobs


def build(nc, a, out, consts):
    plan = weight_plan()
    slot_of, fills_before, ready_at = {}, {}, {}
    fills = [0] * RING
    for n, key in enumerate(plan):
        if key is not None:
            slot_of[key] = n % RING
            fills_before[key] = fills[n % RING]
            fills[n % RING] += 1
            ready_at[key] = 16 * fills[n % RING]
    base_fills = list(fills)
    assert len(plan) % RING == 0
    EXPERT = expert_plan()
    unit = {key: u for u, key in enumerate(EXPERT)}
    per_expert = len(EXPERT) // RING
    assert len(EXPERT) % RING == 0
    jobs = {key: n for n, key in enumerate(psum_plan())}

    with ExitStack() as ctx:
        def sb(name, shape, dt=F32):
            return ctx.enter_context(nc.sbuf_tensor(name, shape, dt))

        def sem(name):
            return ctx.enter_context(nc.semaphore(name))

        ring = sb("ring", [P, RING, SLOT_W])
        cst = sb("cst", [P, CONST_W])
        gains = sb("gains", [P, DEPTH, GAIN_W])
        ln_rows = sb("ln_rows", [4 * KD, P])
        ln_cols = sb("ln_cols", [P, 4 * KD])
        xres = sb("xres", [P, 3, D])
        xn = sb("xn", [P, 3, D])
        hT = sb("hT", [P, KD, TOK])
        ssx = sb("ssx", [P, 3])
        rtx = sb("rtx", [P, 3])
        rsx = sb("rsx", [P, 3])

        arena_w = 19400
        arena = sb("arena", [P, arena_w])
        used = {"attn": 0, "ffn": 0}

        def carve(phase, *shape):
            n = 1
            for s in shape:
                n *= s
            at = used[phase]
            used[phase] += n
            assert used[phase] <= arena_w, (phase, used[phase])
            v = arena[:, at:at + n]
            if len(shape) == 2:
                v = v.rearrange("p (a b) -> p a b", a=shape[0])
            elif len(shape) == 3:
                v = v.rearrange("p (a b c) -> p a b c", a=shape[0], b=shape[1])
            return v

        scratch_at = used["attn"]
        sq = carve("attn", IN_W)
        sqb = carve("attn", HEADS * QK)
        qa = carve("attn", 2, S0)
        cqn = carve("attn", 2, QL)
        tmp1 = carve("attn", S1)
        tmp2 = carve("attn", S1)
        scratch_end = used["attn"]
        used["attn"] = scratch_at
        sp_ = carve("attn", 2, 4, 2 * P)
        pT = carve("attn", 2, 4, 2 * P)
        assert used["attn"] <= scratch_end
        used["attn"] = scratch_end
        v_sb = carve("attn", 3, KVH * HD)
        ka = carve("attn", 3, KVH * HD)
        ckv = carve("attn", 3, KL)
        kr = carve("attn", 3, ROPE)
        tmp0 = carve("attn", S1)
        rt0 = carve("attn", ROPE * HEADS)
        rt1 = carve("attn", ROPE * HEADS)
        rt2 = carve("attn", ROPE * HEADS)
        st = carve("attn", 16)
        sr = carve("attn", 16)
        rs = carve("attn", 16)
        qTa = carve("attn", GRP, TOK)
        kTa = carve("attn", NKEY)
        cqT = carve("attn", 2, TOK)
        ckvT = carve("attn", NKEY)
        qkb = carve("attn", 2, HEADS * QK)
        vb = carve("attn", KEYS, HEADS * VD)
        qTb = carve("attn", HEADS, TOK)
        kTb = carve("attn", HEADS, NKEY)
        mx = carve("attn", 2, 4)
        mm = carve("attn", 2, 4)
        nb = carve("attn", 2, 4)
        dsk = carve("attn", 2, 4)
        es = carve("attn", 2, 4)
        rsum = carve("attn", 2, 4)
        den = carve("attn", 2, 4)
        rden = carve("attn", 2, 4)
        rot = {}
        for name, w in (("a_q_norm", HD), ("a_k_norm", HD), ("b_qr_norm", ROPE), ("b_kr_norm", ROPE)):
            rot[name] = (sb("rc_" + name, [P, DEPTH, 2, w]), sb("rs_" + name, [P, DEPTH, 2, w]), w)

        kc, vc, ckvc, krc = (sb("cache_" + n, [P, DEPTH, w]) for n, w in (("k", KVH * HD), ("v", KVH * HD), ("ckv", KL), ("kr", ROPE)))
        wr = sb("wr", [P, KD, NE])
        yT = sb("yT", [P, 2, TOK])
        sg = carve("ffn", 2, TOK)
        aT = carve("ffn", FT, TOK)
        moe0 = used["ffn"]
        used["ffn"] = 0
        lg = carve("ffn", 3, NE)
        mx8 = carve("ffn", 3, NE)
        idf = carve("ffn", 3, NE)
        oh1 = carve("ffn", 3, NE)
        oh2 = carve("ffn", 3, NE)
        member = carve("ffn", 3, NE)
        dlt = carve("ffn", 3, 4)
        gate = carve("ffn", 3, NJ)
        gtmp = carve("ffn", 3, NE)
        posn = carve("ffn", 3, NJ)
        possel = carve("ffn", 3, NJ)
        cnt = carve("ffn", 16)
        pick = carve("ffn", 3, SLOTS)
        pickg = carve("ffn", 3, SLOTS)
        pgT = carve("ffn", 3, P)
        xgT = carve("ffn", KD, SLOTS)
        sgm = carve("ffn", 2, CW)
        act_m = carve("ffn", 2, CW)
        aTm = carve("ffn", 2, CW // P, SLOTS)
        ysb = carve("ffn", D)
        used["ffn"] = max(used["ffn"], moe0)
        idx8 = sb("idx8", [P, 3, NE], U32)
        nround = sb("nround", [1, 1], I32)
        ps = ctx.enter_context(nc.psum_tensor("ps", [P, 8, 512], F32))

        loaded_x = sem("loaded_x")
        loaded_c = sem("loaded_c")
        loaded_ln = sem("loaded_ln")
        loaded_g = sem("loaded_g")
        loaded_cache = sem("loaded_cache")
        w_ready = [sem(f"w_ready{i}") for i in range(RING)]
        w_used = [sem(f"w_used{i}") for i in range(RING)]
        bank_full = [sem(f"bank_full{i}") for i in range(4)]
        bank_free = [sem(f"bank_free{i}") for i in range(4)]
        ln_done = sem("ln_done")
        ln_evac = sem("ln_evac")
        rot_ready = sem("rot_ready")
        sumsq_x = sem("sumsq_x")
        root_x = sem("root_x")
        xn_ready = sem("xn_ready")
        dve_step = sem("dve_step")
        squares_z = sem("squares_z")
        mean_z = sem("mean_z")
        root_z = sem("root_z")
        rows_ready = sem("rows_ready")
        squares_i = sem("squares_i")
        mean_i = sem("mean_i")
        root_i = sem("root_i")
        item_ready = sem("item_ready")
        negmax_ready = sem("negmax_ready")
        exp_ready = sem("exp_ready")
        silu_ready = sem("silu_ready")
        pair_diff = sem("pair_diff")
        pair_exp = sem("pair_exp")
        member_ready = sem("member_ready")
        plan_ready = sem("plan_ready")
        stored = sem("stored")
        pick_ready = sem("pick_ready")
        gathered = sem("gathered")
        gathered_out = sem("gathered_out")
        gu_full = [sem("gu_full0"), sem("gu_full1")]
        silu_done = sem("silu_done")
        gu_free = [sem("gu_free0"), sem("gu_free1")]
        pickT_full = sem("pickT_full")
        pickT_free = sem("pickT_free")
        aT_full = sem("aT_full")
        aT_free = sem("aT_free")
        y_full = sem("y_full")
        y_free = sem("y_free")
        sc_full = sem("sc_full")
        sc_free = sem("sc_free")
        moe_done = sem("moe_done")

        def C(name, rows=P):
            at, w = CONST[name]
            return cst[0:rows, at:at + w]

        def G(name, l, rows=P):
            at, w = GAIN[name]
            return gains[0:rows, l, at:at + w]

        def pair(key, rows=P):
            p = jobs[key] % 4
            return ps[0:rows, 2 * p:2 * p + 2, :].rearrange("p a b -> p (a b)")

        def slot(key, n, w):
            s = slot_of[key]
            return ring[:, s, 0:n * w].rearrange("p (n w) -> p n w", n=n)

        def wait_full(eng, key):
            eng.wait_ge(bank_full[jobs[key] % 4], jobs[key] // 4 + 1)

        def wait_out(eng, key):
            eng.wait_ge(bank_free[jobs[key] % 4], jobs[key] // 4 + 1)

        def wait_room(eng, key):
            if jobs[key] >= 4:
                eng.wait_ge(bank_free[jobs[key] % 4], jobs[key] // 4)

        def full(ins, key):
            ins.then_inc(bank_full[jobs[key] % 4], 1)

        def free(ins, key):
            ins.then_inc(bank_free[jobs[key] % 4], 1)

        def norm_no(l, w, t):
            return 3 * (2 * l + w) + t + 1

        def bc(v, n):
            return v.unsqueeze(2).to_broadcast([v.shape[0], v.shape[1], n])

        def bh(v, n):
            return v.unsqueeze(1).to_broadcast([v.shape[0], n, v.shape[1]])

        GAINS_IN = 16 * len(GAIN) * DEPTH
        CACHES_IN = 16 * (1 + 4 * DEPTH)

        block = ctx.enter_context(nc.Block())

        @block.sync
        def _(sp):
            for t in range(2):
                sp.dma_start(xres[:, t, :], a["x_prompt"][0, t * P:(t + 1) * P, :]).then_inc(loaded_x, 16)
            sp.dma_start(xres[0:DEC, 2, :], a["x_sample"][0]).then_inc(loaded_x, 16)
            sp.dma_start(cst[:, :], consts).then_inc(loaded_c, 16)

            def source(key):
                kind = key[0]
                if kind == "in":
                    _, l, c, h = key
                    w = a["w_in"][l].rearrange("(k p) n -> p k n", p=P)
                    return (w[:, 4 * h:4 * h + 4, 512 * c:512 * c + 512], 4, 512) if c < 2 else (w[:, :, 1024:IN_W], 8, IN_W - 1024)
                if kind == "uq":
                    return a["b_w_uq"][key[1]].rearrange("(k p) n -> p k n", p=P), 2, HEADS * QK
                if kind == "ukv":
                    return a["b_w_ukv"][key[1]].rearrange("(k p) n -> p k n", p=P), 1, HEADS * (NOPE + VD)
                if kind == "wo":
                    _, l, c, h = key
                    return a["w_o"][l].rearrange("(k p) n -> p k n", p=P)[:, 4 * h:4 * h + 4, 512 * c:512 * c + 512], 4, 512
                if kind in ("gate", "up"):
                    _, c, h = key
                    w = a["ffn_w_" + kind][0].rearrange("(k p) n -> p k n", p=P)
                    return w[:, 4 * h:4 * h + 4, CW * c:CW * c + WIDTH[c]], 4, WIDTH[c]
                _, c, g = key
                n = min(4, FT - 4 * g)
                return a["ffn_w_down"][0].rearrange("(k p) n -> p k n", p=P)[:, 4 * g:4 * g + n, 512 * c:512 * c + 512], n, 512

            for key in plan:
                if key is None:
                    continue
                if fills_before[key]:
                    sp.wait_ge(w_used[slot_of[key]], fills_before[key])
                src, n, w = source(key)
                sp.dma_start(slot(key, n, w), src).then_inc(w_ready[slot_of[key]], 16)

            def load_expert(j, e):
                for u, (kind, c, h) in enumerate(EXPERT):
                    s = u % RING
                    sp.wait_ge(w_used[s], j * per_expert + (base_fills[s] + u // RING))
                    if kind != "down":
                        n, wd = 4, WIDTH[c]
                        src = a["moe_w_" + kind][0, bass.ds(e, 1)].rearrange("o (k p) n -> p (o k) n", p=P)[:, 4 * h:4 * h + 4, CW * c:CW * c + wd]
                    else:
                        n, wd = WIDTH[c] // P // 2, D
                        k0 = 4 * c + n * h
                        src = a["moe_w_down"][0, bass.ds(e, 1)].rearrange("o (k p) n -> p (o k) n", p=P)[:, k0:k0 + n, :]
                    sp.dma_start(ring[:, s, 0:n * wd].rearrange("p (n w) -> p n w", n=n), src).then_inc(w_ready[s], 16)

            with sp.Fori(0, NE) as e:
                load_expert(e, e)
            sp.wait_ge(plan_ready, 1)
            rounds = sp.value_load(nround[0:1, 0:1], min_val=1, max_val=ROUNDS)
            with sp.If(rounds > 1):
                with sp.Fori(1, rounds) as r:
                    with sp.Fori(0, NE) as e:
                        load_expert(r * NE + e, e)

        @block.gpsimd
        def _(pool):
            pool.dma_start(wr[:, :, :], a["moe_router"][0].rearrange("(k p) e -> p k e", p=P)).then_inc(loaded_cache, 16)
            for l in range(DEPTH):
                pool.dma_start(kc[:, l, :], a["cache_swa_k"][l, 0].rearrange("s h d -> s (h d)")).then_inc(loaded_cache, 16)
                pool.dma_start(vc[:, l, :], a["cache_swa_v"][l, 0].rearrange("s h d -> s (h d)")).then_inc(loaded_cache, 16)
                pool.dma_start(ckvc[:, l, :], a["cache_mla_ckv"][l, 0]).then_inc(loaded_cache, 16)
                pool.dma_start(krc[:, l, :], a["cache_mla_krope"][l, 0]).then_inc(loaded_cache, 16)
            pool.wait_ge(loaded_g, GAINS_IN)
            pool.wait_ge(loaded_c, 16)
            for l in range(DEPTH):
                for name, (rc, rsn, w) in rot.items():
                    cc = C("c64" if w == HD else "c32").rearrange("p (c w) -> p c w", c=2)
                    ss = C("s64" if w == HD else "s32").rearrange("p (c w) -> p c w", c=2)
                    g = G(name, l)
                    hw = w // 2
                    pool.tensor_tensor(rc[:, l], cc, bh(g, 2), ALU.mult)
                    pool.tensor_tensor(rsn[:, l, :, 0:hw], ss[:, :, 0:hw], bh(g[:, hw:w], 2), ALU.mult)
                    pool.tensor_tensor(rsn[:, l, :, hw:w], ss[:, :, hw:w], bh(g[:, 0:hw], 2), ALU.mult).then_inc(rot_ready, 1)

            for l in range(DEPTH):
                pool.wait_ge(rows_ready, 3 * l + 3)
                for t in range(3):
                    rows = ROWS[t]
                    if t < 2:
                        o_c, o_r = out["ckv_p"][l, 0, t * P:(t + 1) * P, :], out["kr_p"][l, 0, t * P:(t + 1) * P, :]
                    else:
                        o_c, o_r = out["ckv_s"][l, 0], out["kr_s"][l, 0]
                    pool.dma_start(o_c, ckv[0:rows, t, :]).then_inc(stored, 16)
                    pool.dma_start(o_r, kr[0:rows, t, :]).then_inc(stored, 16)
                for t, o_k, o_v in ((1, out["k_p"], out["v_p"]), (2, out["k_s"], out["v_s"])):
                    rows = ROWS[t]
                    pool.dma_start(o_k[l, 0].rearrange("s h d -> s (h d)"), ka[0:rows, t, :]).then_inc(stored, 16)
                    pool.dma_start(o_v[l, 0].rearrange("s h d -> s (h d)"), v_sb[0:rows, t, :]).then_inc(stored, 16)

            pool.wait_ge(moe_done, 1)
            for t in range(2):
                pool.dma_start(out["y_p"][0, t * P:(t + 1) * P, :], xres[:, t, :]).then_inc(stored, 16)
            pool.dma_start(out["y_s"][0], xres[0:DEC, 2, :]).then_inc(stored, 16)
            pool.wait_ge(stored, 16 * (DEPTH * 10 + 3))

        @block.scalar
        def _(act):
            A = nc.scalar.activation
            act.dma_start(ln_rows[0:2 * KD, :], a["ln_attn"].rearrange("l (k p) -> (l k) p", p=P)).then_inc(loaded_ln, 16)
            act.dma_start(ln_rows[2 * KD:4 * KD, :], a["ln_ffn"].rearrange("l (k p) -> (l k) p", p=P)).then_inc(loaded_ln, 16)
            for l in range(DEPTH):
                for name, (at, w) in GAIN.items():
                    act.dma_start(gains[:, l, at:at + w], a[name][l:l + 1, :].to_broadcast([P, w])).then_inc(loaded_g, 16)

            def norm(l, w):
                for t in range(3):
                    r = ROWS[t]
                    if w == 0 and l == 0:
                        act.wait_ge(loaded_x, 16 * 3)
                        act.wait_ge(loaded_c, 16)
                    elif w == 1:
                        wait_out(act, ("ty", l, KD - 1))
                    else:
                        wait_out(act, ("tz", KD - 1))
                    A(xn[0:r, t, :], xres[0:r, t, :], ACT.Square, accum_out=ssx[0:r, t:t + 1]).then_inc(sumsq_x, 1)
                for t in range(3):
                    r = ROWS[t]
                    act.wait_ge(sumsq_x, norm_no(l, w, t))
                    A(rtx[0:r, t:t + 1], ssx[0:r, t:t + 1], ACT.Sqrt, bias=C("eps", r), scale=1.0 / D).then_inc(root_x, 1)

            for l in range(DEPTH):
                norm(l, 0)
                for t in range(3):
                    r = ROWS[t]
                    wait_full(act, ("za", l, t))
                    za = pair(("za", l, t), r)
                    n = 3 * l + t
                    if n:
                        act.wait_ge(mean_z, n)
                    if l == 1 and t == 0:
                        act.wait_ge(stored, 16 * 10)
                    A(sq[0:r, 0:512], za[:, 0:512], ACT.Square)
                    A(sq[0:r, 512:S1], za[:, 512:S1], ACT.Square)
                    A(v_sb[0:r, t, :], za[:, S1:S2], ACT.Copy)
                    A(sq[0:r, S2:S3], za[:, S2:S3], ACT.Square)
                    wait_full(act, ("zc", l, t))
                    A(sq[0:r, S3:IN_W], pair(("zc", l, t), r)[:, 0:IN_W - S3], ACT.Square).then_inc(squares_z, 1)
                    act.wait_ge(mean_z, n + 1)
                    A(sr[0:r, 0:13], st[0:r, 0:13], ACT.Sqrt, bias=C("eps", r)).then_inc(root_z, 1)
                wait_full(act, ("tc", l))
                pc = pair(("tc", l))
                A(kTa[:, KOFF[2]:KOFF[2] + P], pc[:, 0:P], ACT.Copy)
                free(A(ckvT[:, KOFF[2]:KOFF[2] + P], pc[:, P:2 * P], ACT.Copy), ("tc", l))
                for t in range(3):
                    r, k0 = ROWS[t], KOFF[KT_OF_TILE[t]]
                    wait_full(act, ("tq", l, t))
                    v = pair(("tq", l, t)).rearrange("p (i c) -> p i c", c=P)
                    A(qTa[:, :, TOFF[t]:TOFF[t] + r], v[:, 0:4, 0:r], ACT.Copy)
                    A(kTa[:, k0:k0 + r], v[:, 4, 0:r], ACT.Copy)
                    A(cqT[:, :, TOFF[t]:TOFF[t] + r], v[:, 5:7, 0:r], ACT.Copy)
                    free(A(ckvT[:, k0:k0 + r], v[:, 7, 0:r], ACT.Copy), ("tq", l, t))
                for i in range(len(ITEMS) + 1):
                    if i < len(ITEMS):
                        kind, t = ITEMS[i]
                        r = ROWS[t] if kind == "q" else KROWS[t]
                        n = len(ITEMS) * l + i
                        wait_full(act, ("item", l, i))
                        v = pair(("item", l, i), r)
                        if n:
                            act.wait_ge(mean_i, n)
                        if kind == "q":
                            A(sqb[0:r, 0:512], v[:, 0:512], ACT.Square)
                            A(sqb[0:r, 512:768], v[:, 512:768], ACT.Square).then_inc(squares_i, 1)
                        else:
                            kv = v.rearrange("p (h c) -> p h c", h=HEADS)
                            A(vb[0:r, t, :].rearrange("p (h c) -> p h c", h=HEADS), kv[:, :, NOPE:NOPE + VD], ACT.Copy)
                            A(sqb[0:r, 0:512].rearrange("p (h c) -> p h c", h=HEADS), kv[:, :, 0:NOPE], ACT.Square)\
                                .then_inc(squares_i, 1)
                        act.wait_ge(mean_i, n + 1)
                        w = 16 if kind == "q" else 8
                        A(sr[0:r, 0:w], st[0:r, 0:w], ACT.Sqrt, bias=C("eps", r),
                          scale=1.0 if kind == "q" else 1.0 / NOPE).then_inc(root_i, 1)
                    if i >= 1:
                        kind, t = ITEMS[i - 1]
                        r = ROWS[t] if kind == "q" else KROWS[t]
                        wait_full(act, ("titem", l, i - 1))
                        v = pair(("titem", l, i - 1), QK).rearrange("p (h c) -> p h c", h=HEADS)[:, :, 0:r]
                        dst = qTb[0:QK, :, TOFF[t]:TOFF[t] + r] if kind == "q" else kTb[0:QK, :, KOFF[t]:KOFF[t] + r]
                        free(A(dst, v, ACT.Copy), ("titem", l, i - 1))
                for g in range(len(GROUPS) + 1):
                    if g < len(GROUPS):
                        typ, t, hg = GROUPS[g]
                        r = ROWS[t]
                        b = g % 2
                        nk = sum(KROWS[KEYS_OF[t][0]:KEYS_OF[t][1]])
                        act.wait_ge(negmax_ready, len(GROUPS) * l + g + 1)
                        if typ == "a":
                            A(es[0:r, b, :], dsk[0:r, b, :], ACT.Exp)
                        for i in range(4):
                            ins = A(sp_[0:r, b, i, 0:nk], sp_[0:r, b, i, 0:nk], ACT.Exp, bias=nb[0:r, b, i:i + 1],
                                    scale=A_SCALE if typ == "a" else B_SCALE, accum_out=rsum[0:r, b, i:i + 1])
                        ins.then_inc(exp_ready, 1)
                    if g >= 1:
                        typ, t, hg = GROUPS[g - 1]
                        r, b = ROWS[t], (g - 1) % 2
                        key = ("p", l, g - 1)
                        wait_full(act, key)
                        v = pair(key).rearrange("p (h k c) -> p h k c", h=4, k=2)
                        dst = pT[:, b].rearrange("p h (k c) -> p h k c", k=2)
                        if t == 0:
                            free(A(dst[:, :, 0, 0:r], v[:, :, 0, 0:r], ACT.Copy), key)
                        elif t == 1:
                            free(A(dst[:, :, :, 0:r], v[:, :, :, 0:r], ACT.Copy), key)
                        else:
                            A(dst[:, :, 0, 0:r], v[:, :, 0, 0:r], ACT.Copy)
                            free(A(dst[0:DEC, :, 1, 0:r], v[0:DEC, :, 1, 0:r], ACT.Copy), key)
                for t in range(3):
                    r = ROWS[t]
                    wait_full(act, ("to", l, t))
                    v = pair(("to", l, t)).rearrange("p (k c) -> p k c", k=KD)
                    free(A(hT[:, :, TOFF[t]:TOFF[t] + r], v[:, :, 0:r], ACT.Copy), ("to", l, t))
                for d in range(KD):
                    wait_full(act, ("wo", l, d))
                    if d >= 2:
                        wait_full(act, ("ty", l, d - 2))
                    free(A(yT[:, d % 2, :], pair(("wo", l, d))[:, 0:TOK], ACT.Copy), ("wo", l, d))
                norm(l, 1)
                if l == 0:
                    act.wait_ge(stored, 16 * 10)
                    for f in range(FT):
                        wait_full(act, ("gu", f))
                        if f >= 2:
                            wait_out(act, ("gu", f - 2))
                        A(sg[:, f % 2, :], pair(("gu", f))[:, 0:TOK], ACT.Silu).then_inc(silu_ready, 1)
                    for d in range(KD):
                        wait_full(act, ("dn", d))
                        if d >= 2:
                            wait_full(act, ("tz", d - 2))
                        elif d < 2:
                            wait_full(act, ("ty", 0, KD - 2 + d))
                        free(A(yT[:, d % 2, :], pair(("dn", d))[:, 0:TOK], ACT.Copy), ("dn", d))

            act.wait_ge(pair_diff, 1)
            for t in range(3):
                ins = A(dlt[0:ROWS[t], t, 1:2], dlt[0:ROWS[t], t, 0:1], ACT.Exp)
            ins.then_inc(pair_exp, 1)
            act.wait_ge(plan_ready, 1)
            rounds = act.value_load(nround[0:1, 0:1], min_val=1, max_val=ROUNDS)
            with act.Fori(0, rounds) as r_:
                with act.Fori(0, NE) as e:
                    j = r_ * NE + e
                    for c in range(CHUNKS + 1):
                        if c < CHUNKS:
                            q = c % 2
                            act.wait_ge(gu_full[q], j * 3 + (c // 2 + 1))
                            A(sgm[:, q, 0:WIDTH[c]], ps[:, 2 * (1 - q), 0:WIDTH[c]], ACT.Silu).then_inc(silu_done, 1)
                        if c >= 1:
                            b, w = (c - 1) % 2, WIDTH[c - 1] // P
                            act.wait_ge(aT_full, j * CHUNKS + c)
                            A(aTm[:, b, 0:w, :], ps[:, 5 if b == 0 else 4, 0:w * P].rearrange("p (k c) -> p k c", k=w),
                              ACT.Copy).then_inc(aT_free, 1)
                    act.wait_ge(y_full, j + 1)
                    A(ysb[:, 0:512], ps[:, 6, :], ACT.Copy)
                    A(ysb[:, 512:1024], ps[:, 7, :], ACT.Copy).then_inc(y_free, 1)

        @block.vector
        def _(dve):
            V = nc.vector
            steps = [0]

            def link(ins):
                steps[0] += 1
                ins.then_inc(dve_step, 1)
                dve.wait_ge(dve_step, steps[0])

            dve.wait_ge(ln_done, 1)
            V.tensor_copy(ln_cols[:, :], ps[:, 0, 0:4 * KD]).then_inc(ln_evac, 1)
            dve.wait_ge(ln_evac, 1)

            def norm(l, w):
                for t in range(3):
                    r = ROWS[t]
                    dve.wait_ge(root_x, norm_no(l, w, t))
                    link(V.reciprocal(rsx[0:r, t:t + 1], rtx[0:r, t:t + 1]))
                    V.tensor_scalar(xn[0:r, t, :], xres[0:r, t, :], rsx[0:r, t:t + 1], None, ALU.mult).then_inc(xn_ready, 1)
                for t in range(3):
                    r = ROWS[t]
                    key = ("hf" if w else "h", l, t)
                    wait_full(dve, key)
                    c0 = KD * (2 * w + l)
                    v = pair(key).rearrange("p (k c) -> p k c", k=KD)[:, :, 0:r]
                    free(V.tensor_tensor(hT[:, :, TOFF[t]:TOFF[t] + r], v, bc(ln_cols[:, c0:c0 + KD], r), ALU.mult), key)

            def rotate(dst, src, name, l, t, heads, t1, t2, perm=False):
                rc, rsn, w = rot[name]
                r, cls, hw = ROWS[t], min(t, 1), w // 2
                x = src.rearrange("p (h w) -> p h w", h=heads) if len(src.shape) == 2 else src
                u = t1[0:r, 0:heads * w].rearrange("p (h w) -> p h w", h=heads)
                v = t2[0:r, 0:heads * w].rearrange("p (h w) -> p h w", h=heads)
                V.tensor_tensor(u, x, bh(rc[0:r, l, cls, :], heads), ALU.mult)
                V.tensor_tensor(v[:, :, 0:hw], x[:, :, hw:w], bh(rsn[0:r, l, cls, 0:hw], heads), ALU.mult)
                link(V.tensor_tensor(v[:, :, hw:w], x[:, :, 0:hw], bh(rsn[0:r, l, cls, hw:w], heads), ALU.mult))
                if perm:
                    u = u.rearrange("p (g i) w -> p g i w", g=KVH)
                    v = v.rearrange("p (g i) w -> p g i w", g=KVH)
                    dst = dst.rearrange("p (i g w) -> p g i w", g=KVH, i=GRP)
                    for g in range(KVH):
                        ins = V.tensor_tensor(dst[:, g], u[:, g], v[:, g], ALU.add)
                    return ins
                return V.tensor_tensor(dst, u, v, ALU.add)

            for l in range(DEPTH):
                norm(l, 0)
                if l == 0:
                    dve.wait_ge(rot_ready, 4 * DEPTH)
                for t in range(3):
                    r = ROWS[t]
                    dve.wait_ge(squares_z, 3 * l + t + 1)
                    V.reduce_sum(st[0:r, 0:10], sq[0:r, 0:S1].rearrange("p (h w) -> p h w", w=HD), AX_X)
                    V.reduce_sum(st[0:r, 10:11], sq[0:r, S2:S3], AX_X)
                    V.reduce_sum(st[0:r, 11:12], sq[0:r, S3:S4], AX_X)
                    link(V.reduce_sum(st[0:r, 12:13], sq[0:r, S4:IN_W], AX_X))
                    V.tensor_tensor(st[0:r, 0:13], st[0:r, 0:13], C("inv_a", r), ALU.mult).then_inc(mean_z, 1)
                    dve.wait_ge(root_z, 3 * l + t + 1)
                    link(V.reciprocal(rs[0:r, 0:13], sr[0:r, 0:13]))
                    za, zc = pair(("za", l, t), r), pair(("zc", l, t), r)
                    if t == 2:
                        wait_full(dve, ("tq", l, 0))
                    if t == 0 and l == 1:
                        dve.wait_ge(stored, 16 * 10)
                    V.tensor_tensor(tmp0[0:r, :].rearrange("p (h w) -> p h w", w=HD), za[:, 0:S1].rearrange("p (h w) -> p h w", w=HD),
                                    bc(rs[0:r, 0:10], HD), ALU.mult)
                    free(V.scalar_tensor_tensor(out=cqn[0:r, t % 2, :], in0=za[:, S2:S3], scalar=rs[0:r, 10:11],
                                                in1=G("b_cq_norm", l, r), op0=ALU.mult, op1=ALU.mult), ("za", l, t))
                    V.scalar_tensor_tensor(out=ckv[0:r, t, :], in0=zc[:, 0:KL], scalar=rs[0:r, 11:12],
                                           in1=G("b_ckv_norm", l, r), op0=ALU.mult, op1=ALU.mult)
                    free(V.tensor_scalar(rt0[0:r, 0:ROPE], zc[:, KL:KL + ROPE], rs[0:r, 12:13], None, ALU.mult), ("zc", l, t))
                    wait_out(dve, ("zc", l, t))
                    rotate(qa[0:r, t % 2, :], tmp0[0:r, 0:S0], "a_q_norm", l, t, HEADS, tmp1, tmp2, perm=True)
                    rotate(ka[0:r, t, :].rearrange("p (h w) -> p h w", h=KVH), tmp0[0:r, S0:S1], "a_k_norm", l, t, KVH,
                           tmp1[:, S0:S1], tmp2[:, S0:S1])
                    rotate(kr[0:r, t, :].rearrange("p (h w) -> p h w", h=1), rt0[0:r, 0:ROPE], "b_kr_norm", l, t, 1,
                           rt1, rt2).then_inc(rows_ready, 1)
                dve.wait_ge(rows_ready, 3 * l + 3)

                for i, (kind, t) in enumerate(ITEMS):
                    r = ROWS[t] if kind == "q" else KROWS[t]
                    n = len(ITEMS) * l + i
                    v = pair(("item", l, i), r)
                    dve.wait_ge(squares_i, n + 1)
                    if kind == "q":
                        s3 = sqb[0:r, :].rearrange("p (h w) -> p h w", h=HEADS)
                        V.reduce_sum(st[0:r, 0:8], s3[:, :, 0:NOPE], AX_X)
                        link(V.reduce_sum(st[0:r, 8:16], s3[:, :, NOPE:QK], AX_X))
                        V.tensor_tensor(st[0:r, :], st[0:r, :], C("inv_b", r), ALU.mult).then_inc(mean_i, 1)
                    else:
                        V.reduce_sum(st[0:r, 0:8], sqb[0:r, 0:512].rearrange("p (h w) -> p h w", h=HEADS), AX_X).then_inc(mean_i, 1)
                    dve.wait_ge(root_i, n + 1)
                    w = 16 if kind == "q" else 8
                    link(V.reciprocal(rs[0:r, 0:w], sr[0:r, 0:w]))
                    if i >= 2:
                        wait_full(dve, ("titem", l, i - 2))
                    dst = qkb[0:r, i % 2, :].rearrange("p (h w) -> p h w", h=HEADS)
                    nope = tmp0[0:r, 0:512].rearrange("p (h w) -> p h w", h=HEADS)
                    if kind == "q":
                        x = v[:, 0:768].rearrange("p (h w) -> p h w", h=HEADS)
                        xr = rt0[0:r, :].rearrange("p (h w) -> p h w", h=HEADS)
                        V.tensor_tensor(nope, x[:, :, 0:NOPE], bc(rs[0:r, 0:8], NOPE), ALU.mult)
                        free(V.tensor_tensor(xr, x[:, :, NOPE:QK], bc(rs[0:r, 8:16], ROPE), ALU.mult), ("item", l, i))
                        wait_out(dve, ("item", l, i))
                        V.tensor_tensor(dst[:, :, 0:NOPE], nope, bh(G("b_qn_norm", l, r), HEADS), ALU.mult)
                        rotate(dst[:, :, NOPE:QK], rt0[0:r, :], "b_qr_norm", l, t, HEADS, rt1, rt2).then_inc(item_ready, 1)
                    else:
                        x = v.rearrange("p (h w) -> p h w", h=HEADS)
                        free(V.tensor_tensor(nope, x[:, :, 0:NOPE], bc(rs[0:r, 0:8], NOPE), ALU.mult), ("item", l, i))
                        wait_out(dve, ("item", l, i))
                        V.tensor_tensor(dst[:, :, 0:NOPE], nope, bh(G("b_kn_norm", l, r), HEADS), ALU.mult)
                        if t == 2:
                            dve.wait_ge(loaded_cache, CACHES_IN)
                        own = krc[:, l, :] if t == 2 else kr[0:r, min(t, 2), :]
                        V.tensor_copy(dst[:, :, NOPE:QK], bh(own, HEADS)).then_inc(item_ready, 1)

                for g in range(len(GROUPS) + 2):
                    if g < len(GROUPS):
                        typ, t, hg = GROUPS[g]
                        r, b = ROWS[t], g % 2
                        nk = sum(KROWS[KEYS_OF[t][0]:KEYS_OF[t][1]])
                        key = ("s", l, g)
                        wait_full(dve, key)
                        if g >= 2:
                            wait_full(dve, ("p", l, g - 2))
                        src = pair(key, r).rearrange("p (h c) -> p h c", h=4)[:, :, 0:nk]
                        dst = sp_[0:r, b, :, 0:nk]
                        if t == 2:
                            free(V.tensor_copy(dst, src), key)
                        else:
                            m = C("mask0" if t == 0 else "mask1" + typ, r)
                            free(V.tensor_tensor(dst, src, bh(m, 4), ALU.add), key)
                        wait_out(dve, key)
                        link(V.reduce_max(mx[0:r, b, :], dst, AX_X))
                        if typ == "a":
                            sink = G("a_sinks", l, r)[:, 4 * hg:4 * hg + 4]
                            link(V.scalar_tensor_tensor(out=mm[0:r, b, :], in0=mx[0:r, b, :], scalar=A_SCALE, in1=sink,
                                                        op0=ALU.mult, op1=ALU.max))
                            V.tensor_scalar(nb[0:r, b, :], mm[0:r, b, :], -1.0, None, ALU.mult)
                            V.tensor_tensor(dsk[0:r, b, :], sink, mm[0:r, b, :], ALU.subtract).then_inc(negmax_ready, 1)
                        else:
                            V.tensor_scalar(nb[0:r, b, :], mx[0:r, b, :], -B_SCALE, None, ALU.mult).then_inc(negmax_ready, 1)
                    if 1 <= g <= len(GROUPS):
                        typ, t, hg = GROUPS[g - 1]
                        r, b = ROWS[t], (g - 1) % 2
                        dve.wait_ge(exp_ready, len(GROUPS) * l + g)
                        if typ == "a":
                            link(V.tensor_tensor(den[0:r, b, :], rsum[0:r, b, :], es[0:r, b, :], ALU.add))
                            link(V.reciprocal(rden[0:r, b, :], den[0:r, b, :]))
                        else:
                            link(V.reciprocal(rden[0:r, b, :], rsum[0:r, b, :]))
                    if g >= 2:
                        typ, t, hg = GROUPS[g - 2]
                        r, b = ROWS[t], (g - 2) % 2
                        key = ("o", l, g - 2)
                        wait_full(dve, key)
                        c0 = (typ == "b") * 512 + hg * 256
                        free(V.tensor_tensor(xn[0:r, t, c0:c0 + 256].rearrange("p (h w) -> p h w", h=4),
                                             pair(key, r)[:, 0:256].rearrange("p (h w) -> p h w", h=4),
                                             bc(rden[0:r, b, :], HD), ALU.mult), key)
                        wait_out(dve, key)

                def add_rows(key, d):
                    wait_full(dve, key)
                    v = pair(key).rearrange("p (t c) -> p t c", c=P)
                    V.tensor_tensor(xres[:, 0:2, d * P:(d + 1) * P], xres[:, 0:2, d * P:(d + 1) * P], v[:, 0:2, :], ALU.add)
                    free(V.tensor_tensor(xres[0:DEC, 2, d * P:(d + 1) * P], xres[0:DEC, 2, d * P:(d + 1) * P],
                                         v[0:DEC, 2, :], ALU.add), key)

                for d in range(KD):
                    add_rows(("ty", l, d), d)
                norm(l, 1)
                if l == 0:
                    dve.wait_ge(stored, 16 * 10)
                    for f in range(FT):
                        dve.wait_ge(silu_ready, f + 1)
                        free(V.tensor_tensor(aT[:, f, :], sg[:, f % 2, :], pair(("gu", f))[:, 512:512 + TOK], ALU.mult), ("gu", f))
                    for d in range(KD):
                        add_rows(("tz", d), d)

            wait_full(dve, ("router",))
            dve.wait_ge(stored, 16 * 20)
            lp = pair(("router",))
            iota8 = C("iota")[:, 0:NE]
            for t in range(3):
                r = ROWS[t]
                link(V.tensor_copy(lg[0:r, t, :], lp[0:r, NE * t:NE * t + NE]))
                link(V.max(mx8[0:r, t, :], lg[0:r, t, :]))
                link(V.max_index(idx8[0:r, t, :], mx8[0:r, t, :], lg[0:r, t, :]))
                link(V.tensor_copy(idf[0:r, t, :], idx8[0:r, t, :]))
                V.tensor_scalar(oh1[0:r, t, :], iota8[0:r], idf[0:r, t, 0:1], None, ALU.is_equal)
                link(V.tensor_scalar(oh2[0:r, t, :], iota8[0:r], idf[0:r, t, 1:2], None, ALU.is_equal))
                V.tensor_tensor(member[0:r, t, :], oh1[0:r, t, :], oh2[0:r, t, :], ALU.add)
                ins = V.tensor_tensor(dlt[0:r, t, 0:1], mx8[0:r, t, 1:2], mx8[0:r, t, 0:1], ALU.subtract)
            ins.then_inc(pair_diff, 1)
            dve.wait_ge(pair_diff, 1)
            free(V.tensor_copy(cnt[0:1, 8:9], lp[0:1, 0:1]), ("router",))
            dve.wait_ge(pair_exp, 1)
            for t in range(3):
                r = ROWS[t]
                link(V.tensor_scalar(dlt[0:r, t, 2:3], dlt[0:r, t, 1:2], 1.0, None, ALU.add))
                link(V.reciprocal(dlt[0:r, t, 2:3], dlt[0:r, t, 2:3]))
                link(V.tensor_tensor(dlt[0:r, t, 3:4], dlt[0:r, t, 1:2], dlt[0:r, t, 2:3], ALU.mult))
                link(V.tensor_scalar(gtmp[0:r, t, :], oh2[0:r, t, :], dlt[0:r, t, 3:4], None, ALU.mult))
                for q in range(ROUNDS):
                    ins = V.scalar_tensor_tensor(out=gate[0:r, t, NE * q:NE * q + NE], in0=oh1[0:r, t, :], scalar=dlt[0:r, t, 2:3],
                                                 in1=gtmp[0:r, t, :], op0=ALU.mult, op1=ALU.add)
                link(ins)
            wait_full(dve, ("pos",))
            pp = pair(("pos",))
            for t in range(3):
                r = ROWS[t]
                for q in range(ROUNDS):
                    ins = V.scalar_tensor_tensor(out=posn[0:r, t, NE * q:NE * q + NE], in0=pp[0:r, NE * t:NE * t + NE],
                                                 scalar=ABSENT - SLOTS * q, in1=member[0:r, t, :], op0=ALU.add, op1=ALU.mult)
                link(ins)
                link(V.tensor_scalar(possel[0:r, t, :], posn[0:r, t, :], -ABSENT, None, ALU.add))
            link(V.tensor_copy(cnt[0:1, 0:8], pp[0:1, NE * 3:NE * 4]))
            link(V.reduce_max(cnt[0:1, 8:9], cnt[0:1, 0:8], AX_X))
            V.tensor_scalar(cnt[0:1, 9:10], cnt[0:1, 8:9], SLOTS + 0.5, None, ALU.is_gt)
            link(V.tensor_scalar(cnt[0:1, 10:11], cnt[0:1, 8:9], 2 * SLOTS + 0.5, 1.0, ALU.is_gt, ALU.add))
            V.tensor_tensor(nround[:, :], cnt[0:1, 9:10], cnt[0:1, 10:11], ALU.add).then_inc(plan_ready, 1)
            dve.wait_ge(plan_ready, 1)

            rounds = dve.value_load(nround[0:1, 0:1], min_val=1, max_val=ROUNDS)
            with dve.Fori(0, rounds) as r_:
                with dve.Fori(0, NE) as e:
                    j = dve.snap(r_ * NE + e)
                    for t in range(3):
                        r = ROWS[t]
                        V.tensor_scalar(pick[0:r, t, :], C("iota", r), possel[0:r, t, bass.ds(j, 1)], None, ALU.is_equal)
                        ins = V.tensor_scalar(pickg[0:r, t, :], C("iota", r), possel[0:r, t, bass.ds(j, 1)],
                                              gate[0:r, t, bass.ds(j, 1)], ALU.is_equal, ALU.mult)
                    ins.then_inc(pick_ready, 1)
                    dve.wait_ge(gathered, j + 1)
                    c0 = KD * 3
                    V.tensor_tensor(xgT[:, :, :], ps[:, 0:2, :].rearrange("p a (k c) -> p (a k) c", c=P),
                                    bc(ln_cols[:, c0:c0 + KD], SLOTS), ALU.mult).then_inc(gathered_out, 1)
                    dve.wait_ge(pickT_full, j + 1)
                    V.tensor_copy(pgT[:, 0:2, :], ps[:, 4, 0:2 * P].rearrange("p (t c) -> p t c", t=2))
                    V.tensor_copy(pgT[:, 2, 0:DEC], ps[:, 4, 2 * P:2 * P + DEC]).then_inc(pickT_free, 1)
                    for c in range(CHUNKS):
                        q = c % 2
                        dve.wait_ge(silu_done, j * CHUNKS + (c + 1))
                        V.tensor_tensor(act_m[:, q, 0:WIDTH[c]], sgm[:, q, 0:WIDTH[c]], ps[:, 2 * (1 - q) + 1, 0:WIDTH[c]],
                                        ALU.mult).then_inc(gu_free[q], 1)
                    for t in range(3):
                        r = ROWS[t]
                        dve.wait_ge(sc_full, j * 3 + (t + 1))
                        b = 2 * (1 - t % 2)
                        V.tensor_tensor(xres[0:r, t, :], xres[0:r, t, :], ps[0:r, b:b + 2, :].rearrange("p a c -> p (a c)"),
                                        ALU.add).then_inc(sc_free, 1)
            link(V.memset(cnt[0:1, 11:12], 0.0))
            V.memset(cnt[0:1, 12:13], 0.0).then_inc(moe_done, 1)

        @block.tensor
        def _(pe):
            mm_ = nc.tensor.matmul
            tr = nc.tensor.transpose
            seen = set()

            def weights(key):
                if key not in seen:
                    seen.add(key)
                    pe.wait_ge(w_ready[slot_of[key]], ready_at[key])

            def used_up(ins, key):
                ins.then_inc(w_used[slot_of[key]], 1)

            pe.wait_ge(loaded_c, 16)
            pe.wait_ge(loaded_ln, 32)
            ident = C("ident")
            tr(ps[:, 0, 0:4 * KD], ln_rows[:, :], ident[0:4 * KD, 0:4 * KD]).then_inc(ln_done, 1)
            pe.wait_ge(ln_evac, 1)

            def turn(key, src, rows):
                wait_room(pe, key)
                v = pair(key)
                for k in range(KD):
                    ins = tr(v[:, k * P:k * P + rows], src[0:rows, k * P:(k + 1) * P], ident[0:rows, 0:rows])
                    if key == ("h", 1, 0) and k == 0:
                        used_up(ins, ("down", 1, 5))
                full(ins, key)

            def turn_back(key, d, src):
                wait_room(pe, key)
                wait_out(pe, src)
                v = pair(key)
                for t in range(3):
                    ins = tr(v[0:ROWS[t], t * P:(t + 1) * P], yT[:, d % 2, TOFF[t]:TOFF[t] + ROWS[t]], ident)
                full(ins, key)

            for l in range(DEPTH):
                for t in range(3):
                    pe.wait_ge(xn_ready, norm_no(l, 0, t))
                    turn(("h", l, t), xn[:, t, :], ROWS[t])
                for t in range(3):
                    r = ROWS[t]
                    wait_out(pe, ("h", l, t))
                    key = ("za", l, t)
                    wait_room(pe, key)
                    v = pair(key, r)
                    for c in range(2):
                        for k in range(KD):
                            wk = ("in", l, c, k // 4)
                            weights(wk)
                            ins = mm_(v[:, 512 * c:512 * c + 512], hT[:, k, TOFF[t]:TOFF[t] + r], slot(wk, 4, 512)[:, k % 4, :],
                                      start=(k == 0), stop=(k == KD - 1))
                            if t == 2 and k % 4 == 3 and not (c == 1 and k == KD - 1):
                                used_up(ins, wk)
                    full(ins, key)
                    key = ("zc", l, t)
                    wait_room(pe, key)
                    wk = ("in", l, 2, 0)
                    weights(wk)
                    for k in range(KD):
                        ins = mm_(pair(key, r)[:, 0:IN_W - S3], hT[:, k, TOFF[t]:TOFF[t] + r], slot(wk, 8, IN_W - S3)[:, k, :],
                                  start=(k == 0), stop=(k == KD - 1))
                    full(ins, key)
                key = ("tc", l)
                wait_room(pe, key)
                pe.wait_ge(loaded_cache, CACHES_IN)
                v = pair(key)
                tr(v[:, 0:P], kc[:, l, :], ident)
                ins = tr(v[:, P:2 * P], ckvc[:, l, :], ident)
                full(ins, key)
                for t in range(3):
                    r = ROWS[t]
                    key = ("tq", l, t)
                    pe.wait_ge(rows_ready, 3 * l + t + 1)
                    wait_room(pe, key)
                    v = pair(key)
                    for i in range(4):
                        ins = tr(v[:, i * P:i * P + r], qa[0:r, t % 2, i * P:(i + 1) * P], ident[0:r, 0:r])
                        if t == 0 and i < 2:
                            used_up(ins, (("in", l, 1, 1), ("in", l, 2, 0))[i])
                    tr(v[:, 4 * P:4 * P + r], ka[0:r, t, :], ident[0:r, 0:r])
                    for i in range(2):
                        tr(v[:, (5 + i) * P:(5 + i) * P + r], cqn[0:r, t % 2, i * P:(i + 1) * P], ident[0:r, 0:r])
                    full(tr(v[:, 7 * P:7 * P + r], ckv[0:r, t, :], ident[0:r, 0:r]), key)
                weights(("uq", l))
                weights(("ukv", l))
                wait_out(pe, ("tc", l))
                for i in range(len(ITEMS) + 1):
                    if i < len(ITEMS):
                        kind, t = ITEMS[i]
                        key = ("item", l, i)
                        if kind == "q" or t != 2:
                            wait_out(pe, ("tq", l, t if kind == "q" else min(t, 2)))
                        wait_room(pe, key)
                        if kind == "q":
                            r = ROWS[t]
                            for c0, w in ((0, 512), (512, 256)):
                                for k in range(2):
                                    ins = mm_(pair(key, r)[:, c0:c0 + w], cqT[:, k, TOFF[t]:TOFF[t] + r],
                                              slot(("uq", l), 2, 768)[:, k, c0:c0 + w], start=(k == 0), stop=(k == 1))
                        else:
                            r = KROWS[t]
                            for c0 in (0, 512):
                                ins = mm_(pair(key, r)[:, c0:c0 + 512], ckvT[:, KOFF[t]:KOFF[t] + r],
                                          slot(("ukv", l), 1, 1024)[:, 0, c0:c0 + 512], start=True, stop=True)
                        full(ins, key)
                    if i >= 1:
                        kind, t = ITEMS[i - 1]
                        r = ROWS[t] if kind == "q" else KROWS[t]
                        key = ("titem", l, i - 1)
                        pe.wait_ge(item_ready, len(ITEMS) * l + i)
                        wait_room(pe, key)
                        for h in range(HEADS):
                            ins = tr(pair(key, QK)[:, h * P:h * P + r], qkb[0:r, (i - 1) % 2, h * QK:(h + 1) * QK], ident[0:r, 0:r])
                            if i == len(ITEMS) and h < 2:
                                used_up(ins, (("uq", l), ("ukv", l))[h])
                        full(ins, key)
                for g in range(len(GROUPS) + 2):
                    if g < len(GROUPS):
                        typ, t, hg = GROUPS[g]
                        r = ROWS[t]
                        k0 = KOFF[KEYS_OF[t][0]]
                        nk = sum(KROWS[KEYS_OF[t][0]:KEYS_OF[t][1]])
                        key = ("s", l, g)
                        if g == 0:
                            wait_out(pe, ("tq", l, 2))
                        if g == 6:
                            for i in range(len(ITEMS)):
                                wait_out(pe, ("titem", l, i))
                        wait_room(pe, key)
                        v = pair(key, r)
                        for i in range(4):
                            if typ == "a":
                                q, kk = qTa[64 * hg:64 * hg + 64, i, TOFF[t]:TOFF[t] + r], kTa[64 * hg:64 * hg + 64, k0:k0 + nk]
                            else:
                                h = 4 * hg + i
                                q, kk = qTb[0:QK, h, TOFF[t]:TOFF[t] + r], kTb[0:QK, h, k0:k0 + nk]
                            ins = mm_(v[:, 256 * i:256 * i + nk], q, kk, start=True, stop=True)
                        full(ins, key)
                    if 1 <= g <= len(GROUPS):
                        typ, t, hg = GROUPS[g - 1]
                        r, b = ROWS[t], (g - 1) % 2
                        key = ("p", l, g - 1)
                        pe.wait_ge(exp_ready, len(GROUPS) * l + g)
                        wait_room(pe, key)
                        v = pair(key).rearrange("p (h k c) -> p h k c", h=4, k=2)
                        for i in range(4):
                            for k, kt in enumerate(range(*KEYS_OF[t])):
                                kr_ = KROWS[kt]
                                ins = tr(v[0:kr_, i, k, 0:r], sp_[0:r, b, i, P * k:P * k + kr_], ident[0:r, 0:r])
                        full(ins, key)
                    if g >= 2:
                        typ, t, hg = GROUPS[g - 2]
                        r, b = ROWS[t], (g - 2) % 2
                        key = ("o", l, g - 2)
                        wait_out(pe, ("p", l, g - 2))
                        wait_room(pe, key)
                        kts = list(range(*KEYS_OF[t]))
                        for i in range(4):
                            for k, kt in enumerate(kts):
                                kr_ = KROWS[kt]
                                if typ == "b":
                                    h = 4 * hg + i
                                    val = vb[0:kr_, kt, h * VD:(h + 1) * VD]
                                elif kt == 2:
                                    val = vc[:, l, 64 * hg:64 * hg + 64]
                                else:
                                    val = v_sb[0:kr_, min(kt, 2), 64 * hg:64 * hg + 64]
                                ins = mm_(pair(key, r)[:, 64 * i:64 * i + 64], pT[0:kr_, b, i, P * k:P * k + r], val,
                                          start=(k == 0), stop=(k == len(kts) - 1))
                        full(ins, key)
                for t in range(3):
                    wait_out(pe, ("o", l, len(GROUPS) - 1))
                    wait_out(pe, ("o", l, len(GROUPS) - 2))
                    turn(("to", l, t), xn[:, t, :], ROWS[t])
                for t in range(3):
                    wait_out(pe, ("to", l, t))

                def project_back(kind, back, n_k, inT, w_of, last_use):
                    for d in range(KD + 1):
                        if d < KD:
                            key = kind + (d,)
                            wait_room(pe, key)
                            for k in range(n_k):
                                wk, lhs = w_of(d, k)
                                weights(wk)
                                ins = mm_(pair(key)[:, 0:TOK], lhs, inT[:, k, :], start=(k == 0), stop=(k == n_k - 1))
                                if k < n_k - 1 and last_use(d, k):
                                    used_up(ins, wk)
                                if k == 0 and kind == ("dn",) and d in (0, 4):
                                    used_up(ins, ("up", CHUNKS - 1, 1) if d == 0 else ("down", 0, 5))
                            full(ins, key)
                        if d >= 1:
                            turn_back(back + (d - 1,), d - 1, kind + (d - 1,))

                project_back(("wo", l), ("ty", l), KD, hT,
                             lambda d, k: (("wo", l, d // 4, k // 4), slot(("wo", l, d // 4, k // 4), 4, 512)[:, k % 4, (d % 4) * P:(d % 4 + 1) * P]),
                             lambda d, k: d % 4 == 3 and k % 4 == 3)
                for t in range(3):
                    pe.wait_ge(xn_ready, norm_no(l, 1, t))
                    if t < 2:
                        key = ("hf", l, t)
                        wait_room(pe, key)
                        v = pair(key)
                        for k in range(KD):
                            ins = tr(v[:, k * P:k * P + ROWS[t]], xn[0:ROWS[t], t, k * P:(k + 1) * P], ident[0:ROWS[t], 0:ROWS[t]])
                            if k == 0:
                                used_up(ins, ("wo", l, t, 1))
                        full(ins, key)
                    else:
                        turn(("hf", l, t), xn[:, t, :], ROWS[t])
                for t in range(3):
                    wait_out(pe, ("hf", l, t))
                if l == 0:
                    for f in range(FT):
                        c, fc = f // 4, f % 4
                        key = ("gu", f)
                        wait_room(pe, key)
                        for m, kind in enumerate(("gate", "up")):
                            for k in range(KD):
                                wk = (kind, c, k // 4)
                                weights(wk)
                                ins = mm_(pair(key)[:, 512 * m:512 * m + TOK], slot(wk, 4, WIDTH[c])[:, k % 4, fc * P:(fc + 1) * P],
                                          hT[:, k, :], start=(k == 0), stop=(k == KD - 1))
                                last = (fc == WIDTH[c] // P - 1) and k % 4 == 3
                                if last and not (m == 1 and k == KD - 1):
                                    used_up(ins, wk)
                                if fc == 0 and c > 0 and m == 0 and k == 0:
                                    used_up(ins, ("up", c - 1, 1))
                        full(ins, key)
                    wait_out(pe, ("gu", FT - 1))
                    wait_out(pe, ("gu", FT - 2))
                    first = [True]

                    def w_down(d, k):
                        wk = ("down", d // 4, k // 4)
                        n = min(4, FT - 4 * (k // 4))
                        return wk, slot(wk, n, 512)[:, k % 4, (d % 4) * P:(d % 4 + 1) * P]

                    project_back(("dn",), ("tz",), FT, aT, w_down, lambda d, k: d % 4 == 3 and k % 4 == 3)

            key = ("router",)
            wait_room(pe, key)
            for t in range(3):
                r = ROWS[t]
                for k in range(KD):
                    ins = mm_(pair(key, r)[:, NE * t:NE * t + NE], hT[:, k, TOFF[t]:TOFF[t] + r], wr[:, k, :],
                              start=(k == 0), stop=(k == KD - 1))
            full(ins, key)
            key = ("pos",)
            wait_room(pe, key)
            pe.wait_ge(pair_diff, 1)
            for t in range(3):
                r = ROWS[t]
                for u in range(t + 1):
                    lhs = C("upper", r)[:, 0:r] if u == t else C("ones")[:, 0:r]
                    mm_(pair(key, r)[:, NE * t:NE * t + NE], lhs, member[0:ROWS[u], u, :], start=(u == 0), stop=(u == t))
            for u in range(3):
                ins = mm_(pair(key, 1)[:, NE * 3:NE * 4], C("ones", ROWS[u])[:, 0:1], member[0:ROWS[u], u, :],
                          start=(u == 0), stop=(u == 2))
            full(ins, key)

            pe.wait_ge(plan_ready, 1)
            rounds = pe.value_load(nround[0:1, 0:1], min_val=1, max_val=ROUNDS)
            with pe.Fori(0, rounds) as r_:
                with pe.Fori(0, NE) as e:
                    j = r_ * NE + e

                    def mslot(u, n, w):
                        return ring[:, u % RING, 0:n * w].rearrange("p (n w) -> p n w", n=n)

                    def wait_w(u):
                        pe.wait_ge(w_ready[u % RING], j * (16 * per_expert) + 16 * (base_fills[u % RING] + u // RING + 1))

                    pe.wait_ge(pick_ready, j + 1)
                    for k in range(KD):
                        for t in range(3):
                            ins = mm_(ps[:, k // 4, (k % 4) * P:(k % 4 + 1) * P], xn[0:ROWS[t], t, k * P:(k + 1) * P],
                                      pick[0:ROWS[t], t, :], start=(t == 0), stop=(t == 2))
                    ins.then_inc(gathered, 1)
                    for t in range(3):
                        ins = tr(ps[:, 4, t * P:t * P + ROWS[t]], pickg[0:ROWS[t], t, :], ident[0:ROWS[t], 0:ROWS[t]])
                    ins.then_inc(pickT_full, 1)
                    pe.wait_ge(gathered_out, j + 1)

                    def gate_up(c):
                        q = c % 2
                        if c >= 2:
                            pe.wait_ge(gu_free[q], j * 3 + c // 2)
                        for m in range(2):
                            for k in range(KD):
                                u = unit[("gate", "up")[m], c, k // 4]
                                if k % 4 == 0:
                                    wait_w(u)
                                ins = mm_(ps[:, 2 * (1 - q) + m, 0:WIDTH[c]], xgT[:, k, :], mslot(u, 4, WIDTH[c])[:, k % 4, :],
                                          start=(k == 0), stop=(k == KD - 1))
                                if k % 4 == 3 and not (m == 1 and k == KD - 1):
                                    ins.then_inc(w_used[u % RING], 1)
                                if c in (1, 2) and m == 0 and k == 0:
                                    ins.then_inc(w_used[unit["up", c - 1, 1] % RING], 1)
                        ins.then_inc(gu_full[q], 1)

                    def turn_chunk(c):
                        b, w = c % 2, WIDTH[c] // P
                        pe.wait_ge(gu_free[b], j * 3 + (c // 2 + 1))
                        if c == 1:
                            pe.wait_ge(pickT_free, j + 1)
                        if c >= 2:
                            pe.wait_ge(aT_free, j * CHUNKS + (c - 1))
                        for k in range(w):
                            ins = tr(ps[:, 5 if b == 0 else 4, k * P:(k + 1) * P], act_m[:, b, k * P:(k + 1) * P], ident)
                        ins.then_inc(aT_full, 1)

                    def down(c):
                        b, n = c % 2, WIDTH[c] // P // 2
                        pe.wait_ge(aT_free, j * CHUNKS + (c + 1))
                        for k in range(2 * n):
                            u = unit["down", c, k // n]
                            if k % n == 0:
                                wait_w(u)
                            for h in range(2):
                                ins = mm_(ps[:, 6 + h, :], aTm[:, b, k, :], mslot(u, n, D)[:, k % n, 512 * h:512 * h + 512],
                                          start=(c == 0 and k == 0), stop=(c == CHUNKS - 1 and k == 2 * n - 1))
                                if c + 2 < CHUNKS and k == 0 and h == 0:
                                    ins.then_inc(w_used[unit["up", c + 2, 1] % RING], 1)
                                if k % n == n - 1 and h == 1:
                                    if c == CHUNKS - 1 and k == 2 * n - 1:
                                        ins.then_inc(y_full, 1)
                                    else:
                                        ins.then_inc(w_used[u % RING], 1)

                    gate_up(0)
                    gate_up(1)
                    turn_chunk(0)
                    for c in range(2, CHUNKS):
                        gate_up(c)
                        down(c - 2)
                        turn_chunk(c - 1)
                    down(CHUNKS - 2)
                    turn_chunk(CHUNKS - 1)
                    down(CHUNKS - 1)
                    pe.wait_ge(y_free, j + 1)
                    for t in range(3):
                        r = ROWS[t]
                        b = 2 * (1 - t % 2)
                        if t == 0:
                            pe.wait_ge(gu_free[0], j * 3 + 3)
                        elif t == 1:
                            pe.wait_ge(gu_free[1], j * 3 + 3)
                        else:
                            pe.wait_ge(sc_free, j * 3 + 1)
                        for h in range(2):
                            ins = mm_(ps[0:r, b + h, :], pgT[:, t, 0:r], ysb[:, 512 * h:512 * h + 512], start=True, stop=True)
                            if t == 0 and h == 0:
                                ins.then_inc(w_used[unit["down", CHUNKS - 1, 1] % RING], 1)
                        ins.then_inc(sc_full, 1)
                    pe.wait_ge(sc_free, j * 3 + 3)



_INS = ["x_prompt", "x_sample", "cache_swa_k", "cache_swa_v", "cache_mla_ckv", "cache_mla_krope", "ln_attn", "w_in",
        "a_q_norm", "a_k_norm", "a_sinks", "b_cq_norm", "b_w_uq", "b_ckv_norm", "b_w_ukv", "b_qn_norm", "b_qr_norm",
        "b_kn_norm", "b_kr_norm", "w_o", "ln_ffn", "ffn_w_gate", "ffn_w_up", "ffn_w_down", "moe_router", "moe_w_gate",
        "moe_w_up", "moe_w_down"]
_OUTS = [("y_p", (1, SEQ, D)), ("y_s", (1, DEC, D)), ("k_p", (DEPTH, 1, WINDOW, KVH, HD)), ("v_p", (DEPTH, 1, WINDOW, KVH, HD)),
         ("ckv_p", (DEPTH, 1, SEQ, KL)), ("kr_p", (DEPTH, 1, SEQ, ROPE)), ("k_s", (DEPTH, 1, DEC, KVH, HD)),
         ("v_s", (DEPTH, 1, DEC, KVH, HD)), ("ckv_s", (DEPTH, 1, DEC, KL)), ("kr_s", (DEPTH, 1, DEC, ROPE))]


def shape_constants():
    import numpy as np

    out = np.zeros((P, CONST_W), np.float32)

    def put(name, v):
        at, w = CONST[name]
        out[:, at:at + w] = v

    row = np.arange(P)
    put("ident", np.eye(P))
    put("upper", row[:, None] < row[None, :])
    put("ones", 1.0)
    put("iota", row[None, :])
    for w, c_name, s_name in ((HD, "c64", "s64"), (ROPE, "c32", "s32")):
        half = w // 2
        inv = np.float32(10000.0) ** (-(np.arange(half, dtype=np.float32) / np.float32(half)))
        for tile in range(2):
            ang = (row + P * tile).astype(np.float32)[:, None] * inv[None, :]
            c, s = np.cos(ang), np.sin(ang)
            at = CONST[c_name][0] + tile * w
            out[:, at:at + w] = np.concatenate([c, c], 1)
            at = CONST[s_name][0] + tile * w
            out[:, at:at + w] = np.concatenate([-s, s], 1)
    q, k = row[:, None] // CHUNK, np.arange(2 * P)[None, :] // CHUNK
    put("mask0", np.where(k[:, :P] <= q, 0.0, -1e30))
    q = q + P // CHUNK
    put("mask1a", np.where((k <= q) & (k >= q - WINDOW // CHUNK), 0.0, -1e30))
    put("mask1b", np.where(k <= q, 0.0, -1e30))
    put("inv_a", np.array([1 / HD] * 10 + [1 / QL, 1 / KL, 1 / ROPE], np.float32)[None, :])
    put("inv_b", np.array([1 / NOPE] * 8 + [1 / ROPE] * 8, np.float32)[None, :])
    put("eps", EPS)
    return out


def kernel(**inputs):
    import numpy as _np
    import concourse.bacc as _bacc
    from concourse.bass_utils import run_bass_kernel_spmd as _run

    nc = _bacc.Bacc("TRN2", target_bir_lowering=False, num_devices=1)
    arrays, a, out = {}, {}, {}
    for name in _INS:
        v = _np.ascontiguousarray(inputs[name])
        arrays[f"in_{name}"] = v
        a[name] = nc.dram_tensor(f"in_{name}", v.shape, mybir.dt.from_np(v.dtype), kind="ExternalInput").ap()
    arrays["shape_consts"] = shape_constants()
    consts = nc.dram_tensor("shape_consts", (P, CONST_W), F32, kind="ExternalInput").ap()
    for name, shape in _OUTS:
        out[name] = nc.dram_tensor(f"out_{name}", shape, F32, kind="ExternalOutput").ap()
    build(nc, a, out, consts)
    r = _run(nc, [arrays], core_ids=[0])
    return tuple(r.results[0][f"out_{name}"] for name, _ in _OUTS)
```

```python
from contextlib import ExitStack

import concourse.bass as bass
from concourse import mybir

F32 = mybir.dt.float32
F32R = mybir.dt.float32r
I32 = mybir.dt.int32
U32 = mybir.dt.uint32
ALU = mybir.AluOpType
ACT = mybir.ActivationFunctionType
AX_X = mybir.AxisListType.X

P = 128
D = 1024
KD = D // P
SEQ, DEC = 256, 32
TOK = SEQ + DEC
ROWS = [P, P, DEC]
TOFF = [0, P, 2 * P]
CHUNK, WINDOW = 64, 128
HEADS, KVH, HD = 8, 2, 64
GRP = HEADS // KVH
NOPE, ROPE, VD, QK = 64, 32, 64, 96
QL, KL = 256, 128
S0, S1, S2 = HEADS * HD, HEADS * HD + KVH * HD, HEADS * HD + 2 * KVH * HD
S3, S4 = S2 + QL, S2 + QL + KL
IN_W = S4 + ROPE
DFF = 2816
FT = DFF // P
NE = 8
DEPTH = 2
EPS = 1e-6
A_SCALE, B_SCALE = HD ** -0.5, QK ** -0.5
KEYS = 4
KOFF = [0, 128, 256, 384]
NKEY = 416
KROWS = [P, P, P, DEC]
KT_OF_TILE = [0, 1, 3]
KEYS_OF = [(0, 1), (0, 2), (2, 4)]
SLOTS = P
ROUNDS = (TOK + SLOTS - 1) // SLOTS
NJ = NE * ROUNDS
CW = 512
CHUNKS = (DFF + CW - 1) // CW
WIDTH = [min(CW, DFF - CW * c) for c in range(CHUNKS)]
DW = 2 * P
DCH = DFF // DW
RING = 6
DENSE_PAIRS, MOE_PAIRS = 3, 4
SLOT_W = 2048
ABSENT = 1000.0

CONST = {}
_at = 0
for _name, _w in (("ident", P), ("upper", P), ("ones", P), ("iota", P), ("c64", 2 * HD), ("s64", 2 * HD),
                  ("c32", 2 * ROPE), ("s32", 2 * ROPE), ("mask0", P), ("mask1a", 2 * P), ("mask1b", 2 * P),
                  ("inv_a", 13), ("inv_b", 16), ("eps", 1)):
    CONST[_name] = (_at, _w)
    _at += _w
CONST_W = _at

GAIN = {}
_at = 0
for _name, _w in (("a_q_norm", HD), ("a_k_norm", HD), ("b_cq_norm", QL), ("b_ckv_norm", KL), ("b_qn_norm", NOPE),
                  ("b_qr_norm", ROPE), ("b_kn_norm", NOPE), ("b_kr_norm", ROPE), ("a_sinks", HEADS)):
    GAIN[_name] = (_at, _w)
    _at += _w
GAIN_W = _at

ITEMS = [("q", 0), ("k", 0), ("q", 1), ("k", 1), ("k", 2), ("q", 2), ("k", 3)]
GROUPS = [(typ, t, hg) for typ in "ab" for t in range(3) for hg in range(2)]


DENSE = [(m, i) for i in range(DCH) for m in ("gate", "up")] + [("down", c, g) for c in range(2) for g in range(6)]


def weight_plan():
    plan = []
    for layer in range(DEPTH):
        plan += [("in", layer, c, h) for c in range(2) for h in range(2)] + [("in", layer, 2, 0)]
        plan += [("uq", layer), ("ukv", layer)]
        plan += [("wo", layer, c, h) for c in range(2) for h in range(2)]
        plan += [None] * (-len(plan) % RING)
        if layer == 0:
            plan += DENSE
            plan += [None] * (-len(plan) % RING)
    return plan


def expert_plan():
    order = []
    for c in range(CHUNKS + 2):
        if c < CHUNKS:
            order += [(m, c, h) for m in ("gate", "up") for h in range(2)]
        if c >= 2:
            order += [("down", c - 2, h) for h in range(2)]
    return order


def moe_events():
    at = {key: u for u, key in enumerate(expert_plan())}
    ev = {}

    def put(u, what, c=0):
        ev.setdefault(u, []).append((what, c))

    put(at["up", 0, 1] + MOE_PAIRS, "act", 0)
    put(at["up", 0, 1] + MOE_PAIRS + 1, "scatter")
    for c in range(1, CHUNKS):
        put(at["up", c, 1] + MOE_PAIRS, "act", c)
        if c == 1:
            put(at["up", 1, 1] + MOE_PAIRS, "slots")
        put((at["up", 1, 1] if c == 1 else at["down", c - 2, 1]) + MOE_PAIRS, "turned", c - 1)
    put(at["up", 2, 1] + MOE_PAIRS + 2, "picks")
    put(at["down", CHUNKS - 3, 1] + MOE_PAIRS + 1, "tokens")
    put(at["down", CHUNKS - 2, 1] + MOE_PAIRS, "turned", CHUNKS - 1)
    put(at["down", CHUNKS - 1, 1] + MOE_PAIRS, "output")
    return ev


def psum_plan():
    jobs = []
    for l in range(DEPTH):
        jobs += [("h", l, t) for t in range(3)]
        for t in range(3):
            jobs += [("za", l, t), ("zc", l, t)]
        jobs += [("tc", l)] + [("tq", l, t) for t in range(3)]
        for i in range(len(ITEMS) + 1):
            if i < len(ITEMS):
                jobs.append(("item", l, i))
            if i >= 1:
                jobs.append(("titem", l, i - 1))
        for g in range(len(GROUPS) + 2):
            if g < len(GROUPS):
                jobs.append(("s", l, g))
            if 1 <= g <= len(GROUPS):
                jobs.append(("p", l, g - 1))
            if g >= 2:
                jobs.append(("o", l, g - 2))
        jobs += [("to", l, t) for t in range(3)]
        for d in range(KD + 1):
            if d < KD:
                jobs.append(("wo", l, d))
            if d >= 1:
                jobs.append(("ty", l, d - 1))
        jobs += [("hf", l, t) for t in range(3)]
        if l == 0:
            jobs += [(m, i) for i in range(DCH) for m in ("gate", "up")]
            for c in range(2):
                jobs += [("dn", c, h) for h in range(2)]
                jobs += [("tz", d) for d in range(4 * c, 4 * c + 4)]
        else:
            jobs += [("router",), ("pos",)]
    return jobs


def build(nc, a, out, consts):
    plan = weight_plan()
    slot_of, ready_at = {}, {}
    fills = [0] * RING
    for n, key in enumerate(plan):
        if key is not None:
            slot_of[key] = n % RING
            fills[n % RING] += 1
            ready_at[key] = 16 * fills[n % RING]
    base_fills = list(fills)
    assert len(plan) % RING == 0
    before = {}
    for n, key in enumerate(plan):
        prev = [k for k in plan[n % RING:n:RING] if k is not None]
        if key is not None and prev:
            before[key] = prev[-1]
    last_in_slot = [[k for k in plan[s_::RING] if k is not None][-1] for s_ in range(RING)]
    used_at, tally = {}, [0] * RING
    for n, key in enumerate(plan):
        if key is not None and key not in DENSE:
            tally[n % RING] += 1
            used_at[key] = tally[n % RING]
    EXPERT = expert_plan()
    unit = {key: u for u, key in enumerate(EXPERT)}
    MOE_EVENTS = moe_events()
    per_expert = len(EXPERT) // RING
    assert len(EXPERT) % RING == 0
    jobs = {key: n for n, key in enumerate(psum_plan())}

    with ExitStack() as ctx:
        def sb(name, shape, dt=F32):
            return ctx.enter_context(nc.sbuf_tensor(name, shape, dt))

        def sem(name):
            return ctx.enter_context(nc.semaphore(name))

        ring = sb("ring", [P, RING, SLOT_W])
        cst = sb("cst", [P, CONST_W])
        gains = sb("gains", [P, DEPTH, GAIN_W])
        ln_rows = sb("ln_rows", [4 * KD, P])
        ln_cols = sb("ln_cols", [P, 4 * KD])
        xres = sb("xres", [P, 3, D])
        ssx = sb("ssx", [P, 3])
        rtx = sb("rtx", [P, 3])
        rsx = sb("rsx", [P, 3])
        kc, vc, ckvc, krc = (sb("cache_" + n, [P, DEPTH, w]) for n, w in (("k", KVH * HD), ("v", KVH * HD), ("ckv", KL), ("kr", ROPE)))
        wr = sb("wr", [P, KD, NE])
        yT = sb("yT", [P, 2, 2, TOK])
        rot = {}
        for name, w in (("a_q_norm", HD), ("a_k_norm", HD), ("b_qr_norm", ROPE), ("b_kr_norm", ROPE)):
            rot[name] = (sb("rc_" + name, [P, 2, w]), sb("rs_" + name, [P, 2, w]), w)
        idx8 = sb("idx8", [P, 3, NE], U32)
        nround = sb("nround", [1, 1], I32)

        slab_at = (nc.sbuf_base + 63) // 64 * 64
        slab_w = (nc.sbuf_usable_end - slab_at) // 4 - 32
        sb("slab", [P, slab_w])

        def at(name, offset, shape, dt=F32):
            n = 1
            for s in shape[1:]:
                n *= s
            assert offset + n <= slab_w, (name, offset + n, slab_w)
            return nc.alloc_sbuf_tensor_at(name, shape, dt, offset=slab_at + 4 * offset)

        XN, HT = 0, 3 * D
        PHASE = HT + KD * TOK
        xn = at("xn", XN, [P, 3, D])
        hT = at("hT", HT, [P, KD, TOK])
        w_hi = [at(f"w_hi{i}", PHASE + 2 * SLOT_W * i, [P, SLOT_W], F32R) for i in range(MOE_PAIRS)]
        w_lo = [at(f"w_lo{i}", PHASE + 2 * SLOT_W * i + SLOT_W, [P, SLOT_W], F32R) for i in range(MOE_PAIRS)]

        class Carve:

            def __init__(self, start):
                self.at = start

            def __call__(self, name, *shape, dt=F32):
                n = 1
                for s in shape:
                    n *= s
                start, self.at = self.at, self.at + (n + 7) // 8 * 8
                return at(name, start, [P, *shape], dt)

        carve = Carve(PHASE)
        sq = carve("sq", IN_W)
        sqb = carve("sqb", HEADS * QK)
        qa = carve("qa", 2, S0)
        cqn = carve("cqn", 2, QL)
        tmp1 = carve("tmp1", S1)
        tmp2 = carve("tmp2", S1)
        over = Carve(PHASE)
        sp_ = over("sp_", 2, 4, 2 * P)
        pT = over("pT", 2, 4, 2 * P)
        assert over.at <= carve.at
        v_sb = carve("v_sb", 3, KVH * HD)
        ka = carve("ka", 3, KVH * HD)
        ckv = carve("ckv", 3, KL)
        kr = carve("kr", 3, ROPE)
        tmp0 = carve("tmp0", S1)
        rt0 = carve("rt0", ROPE * HEADS)
        rt1 = carve("rt1", ROPE * HEADS)
        rt2 = carve("rt2", ROPE * HEADS)
        st = carve("st", 16)
        sr = carve("sr", 16)
        rs = carve("rs", 16)
        qTa = carve("qTa", GRP, TOK)
        kTa = carve("kTa", NKEY)
        cqT = carve("cqT", 2, TOK)
        ckvT = carve("ckvT", NKEY)
        qkb = carve("qkb", 2, HEADS * QK)
        vb = carve("vb", KEYS, HEADS * VD)
        qTb = carve("qTb", HEADS, TOK)
        kTb = carve("kTb", HEADS, NKEY)
        mx, mm, nb, dsk, es, rsum, den, rden = (carve(n, 2, 4) for n in ("mx", "mm", "nb", "dsk", "es", "rsum", "den", "rden"))

        carve = Carve(PHASE + 2 * SLOT_W * DENSE_PAIRS)
        hT_hi = at("hT_hi", XN, [P, KD, TOK], F32R)
        hT_lo = at("hT_lo", HT, [P, KD, TOK], F32R)
        sg = yT
        aa = carve("aa", 2, 2, TOK)
        aT_hi = carve("aT_hi", FT, TOK, dt=F32R)
        aT_lo = carve("aT_lo", FT, TOK, dt=F32R)

        xn_lo = at("xn_lo", XN, [P, 3, D], F32R)
        over = Carve(HT)
        xg_hi = over("xg_hi", KD, SLOTS, dt=F32R)
        xg_lo = over("xg_lo", KD, SLOTS, dt=F32R)
        assert over.at <= PHASE
        carve = Carve(PHASE + 2 * SLOT_W * MOE_PAIRS)
        xn_hi = carve("xn_hi", 3, D, dt=F32R)
        lg, mx8, idf, oh1, oh2, member, gtmp = (carve(n, 3, NE) for n in ("lg", "mx8", "idf", "oh1", "oh2", "member", "gtmp"))
        dlt = carve("dlt", 3, 4)
        gate = carve("gate", 3, NJ + 1)
        posn = carve("posn", 3, NJ)
        possel = carve("possel", 3, NJ + 1)
        cnt = carve("cnt", 16)
        pick = carve("pick", 3, SLOTS, dt=F32R)
        gcol = carve("gcol", 4)
        gslot = carve("gslot", 1)
        pickT = carve("pickT", TOK, dt=F32R)
        xg = yT[:, :, :, :].rearrange("p a b c -> p (a b c)")[:, 0:KD * SLOTS].rearrange("p (k c) -> p k c", k=KD)
        sgm = gains[:, :, :].rearrange("p l w -> p (l w)")[:, 0:2 * CW].rearrange("p (a b) -> p a b", a=2)
        act_m = carve("act_m", 2, CW)
        am_hi = carve("am_hi", 2, CW // P, SLOTS, dt=F32R)
        am_lo = carve("am_lo", 2, CW // P, SLOTS, dt=F32R)
        y_hi = carve("y_hi", D, dt=F32R)
        y_lo = carve("y_lo", D, dt=F32R)
        ps = ctx.enter_context(nc.psum_tensor("ps", [P, 8, 512], F32))

        loaded_x = sem("loaded_x")
        loaded_c = sem("loaded_c")
        loaded_ln = sem("loaded_ln")
        loaded_g = sem("loaded_g")
        loaded_cache = sem("loaded_cache")
        w_ready = [sem(f"w_ready{i}") for i in range(RING)]
        w_used = [sem(f"w_used{i}") for i in range(RING)]
        bank_full = [sem(f"bank_full{i}") for i in range(4)]
        bank_free = [sem(f"bank_free{i}") for i in range(4)]
        ln_done = sem("ln_done")
        ln_evac = sem("ln_evac")
        rot_ready = sem("rot_ready")
        sumsq_x = sem("sumsq_x")
        root_x = sem("root_x")
        xn_ready = sem("xn_ready")
        dve_step = sem("dve_step")
        squares_z = sem("squares_z")
        mean_z = sem("mean_z")
        root_z = sem("root_z")
        rows_ready = sem("rows_ready")
        squares_i = sem("squares_i")
        mean_i = sem("mean_i")
        root_i = sem("root_i")
        item_ready = sem("item_ready")
        negmax_ready = sem("negmax_ready")
        exp_ready = sem("exp_ready")
        pair_diff = sem("pair_diff")
        pair_exp = sem("pair_exp")
        plan_ready = sem("plan_ready")
        stored = sem("stored")
        hi_ready = sem("hi_ready")
        lo_ready = sem("lo_ready")
        pair_used = sem("pair_used")
        tok_hi = sem("tok_hi")
        tok_ready = sem("tok_ready")
        dense_hi = sem("dense_hi")
        dense_act = sem("dense_act")
        pick_ready = sem("pick_ready")
        gathered = sem("gathered")
        xg_rows = sem("xg_rows")
        xg_high = sem("xg_high")
        xg_ready = sem("xg_ready")
        gu_full = [sem("gu_full0"), sem("gu_full1")]
        silu_done = sem("silu_done")
        gu_free = [sem("gu_free0"), sem("gu_free1")]
        pickT_full = sem("pickT_full")
        pickT_free = sem("pickT_free")
        aT_full = sem("aT_full")
        aT_high = sem("aT_high")
        aT_free = sem("aT_free")
        y_full = sem("y_full")
        y_high = sem("y_high")
        y_free = sem("y_free")
        sc_full = sem("sc_full")
        sc_free = sem("sc_free")
        last_full = sem("last_full")
        moe_done = sem("moe_done")

        def C(name, rows=P):
            at, w = CONST[name]
            return cst[0:rows, at:at + w]

        def G(name, l, rows=P):
            at, w = GAIN[name]
            return gains[0:rows, l, at:at + w]

        def pair(key, rows=P):
            p = jobs[key] % 4
            return ps[0:rows, 2 * p:2 * p + 2, :].rearrange("p a b -> p (a b)")

        def slot(key, n, w):
            s = slot_of[key]
            return ring[:, s, 0:n * w].rearrange("p (n w) -> p n w", n=n)

        def wait_full(eng, key):
            eng.wait_ge(bank_full[jobs[key] % 4], jobs[key] // 4 + 1)

        def wait_out(eng, key):
            eng.wait_ge(bank_free[jobs[key] % 4], jobs[key] // 4 + 1)

        def wait_room(eng, key):
            if jobs[key] >= 4:
                eng.wait_ge(bank_free[jobs[key] % 4], jobs[key] // 4)

        def full(ins, key):
            ins.then_inc(bank_full[jobs[key] % 4], 1)

        def free(ins, key):
            ins.then_inc(bank_free[jobs[key] % 4], 1)

        def norm_no(l, w, t):
            return 3 * (2 * l + w) + t + 1

        def bc(v, n):
            return v.unsqueeze(2).to_broadcast([v.shape[0], v.shape[1], n])

        def bh(v, n):
            return v.unsqueeze(1).to_broadcast([v.shape[0], n, v.shape[1]])

        ND = len(DENSE)
        unit_job = {}
        down_used = {}
        for n, key in enumerate(DENSE):
            if key[0] != "down":
                unit_job[n] = key
            elif key[2] == 5:
                unit_job[n] = ("dn", key[1], 1)
            else:
                down_used[n] = 5 * key[1] + key[2] + 1
        SC_BANKS = (0, 4, 2)
        DOWN_USED = 10

        def wait_pair(eng, n):
            m = n - DENSE_PAIRS
            if m >= 0:
                if m in unit_job:
                    wait_full(eng, unit_job[m])
                else:
                    eng.wait_ge(pair_used, down_used[m])

        def dense_size(key):
            return SLOT_W if key[0] != "down" or key[2] < 5 else SLOT_W // 2

        def moe_size(u):
            kind, c, h = EXPERT[u % len(EXPERT)]
            return 4 * WIDTH[c] if kind != "down" else WIDTH[c] // P // 2 * D

        GAINS_IN = 16 * len(GAIN) * DEPTH
        CACHES_IN = 16 * (1 + 4 * DEPTH)

        block = ctx.enter_context(nc.Block())

        @block.sync
        def _(sp):
            for t in range(2):
                sp.dma_start(xres[:, t, :], a["x_prompt"][0, t * P:(t + 1) * P, :]).then_inc(loaded_x, 16)
            sp.dma_start(xres[0:DEC, 2, :], a["x_sample"][0]).then_inc(loaded_x, 16)
            sp.dma_start(cst[:, :], consts).then_inc(loaded_c, 16)

            def source(key):
                kind = key[0]
                if kind == "in":
                    _, l, c, h = key
                    w = a["w_in"][l].rearrange("(k p) n -> p k n", p=P)
                    return (w[:, 4 * h:4 * h + 4, 512 * c:512 * c + 512], 4, 512) if c < 2 else (w[:, :, 1024:IN_W], 8, IN_W - 1024)
                if kind == "uq":
                    return a["b_w_uq"][key[1]].rearrange("(k p) n -> p k n", p=P), 2, HEADS * QK
                if kind == "ukv":
                    return a["b_w_ukv"][key[1]].rearrange("(k p) n -> p k n", p=P), 1, HEADS * (NOPE + VD)
                if kind == "wo":
                    _, l, c, h = key
                    return a["w_o"][l].rearrange("(k p) n -> p k n", p=P)[:, 4 * h:4 * h + 4, 512 * c:512 * c + 512], 4, 512
                if kind in ("gate", "up"):
                    w = a["ffn_w_" + kind][0].rearrange("(k p) n -> p k n", p=P)
                    return w[:, :, DW * key[1]:DW * key[1] + DW], KD, DW
                _, c, g = key
                n = min(4, FT - 4 * g)
                return a["ffn_w_down"][0].rearrange("(k p) n -> p k n", p=P)[:, 4 * g:4 * g + n, 512 * c:512 * c + 512], n, 512

            def slot_room(key):
                if key in DENSE:
                    sp.wait_ge(lo_ready, DENSE.index(key) + 1)
                else:
                    sp.wait_ge(w_used[slot_of[key]], used_at[key])

            for key in plan:
                if key is None:
                    continue
                if key in before:
                    slot_room(before[key])
                src, n, w = source(key)
                sp.dma_start(slot(key, n, w), src).then_inc(w_ready[slot_of[key]], 16)

            def load_unit(u, e):
                kind, c, h = EXPERT[u]
                s = u % RING
                if kind != "down":
                    n, wd = 4, WIDTH[c]
                    src = a["moe_w_" + kind][0, bass.ds(e, 1)].rearrange("o (k p) n -> p (o k) n", p=P)[:, 4 * h:4 * h + 4, CW * c:CW * c + wd]
                else:
                    n, wd = WIDTH[c] // P // 2, D
                    k0 = 4 * c + n * h
                    src = a["moe_w_down"][0].rearrange("e (k p) n -> p (e k) n", p=P)[:, bass.ds(e * FT + k0, n), :]
                sp.dma_start(ring[:, s, 0:n * wd].rearrange("p (n w) -> p n w", n=n), src).then_inc(w_ready[s], 16)

            for u in range(RING):
                slot_room(last_in_slot[u])
                load_unit(u, 0)

            def load_expert(j, e):
                after = sp.snap((e + 1) % NE)
                for u in range(RING, len(EXPERT) + RING):
                    sp.wait_ge(lo_ready, j * len(EXPERT) + (ND + u - RING + 1))
                    load_unit(u % len(EXPERT), e if u < len(EXPERT) else after)

            with sp.Fori(0, NE) as e:
                load_expert(e, e)
            sp.wait_ge(plan_ready, 1)
            rounds = sp.value_load(nround[0:1, 0:1], min_val=1, max_val=ROUNDS)
            with sp.If(rounds > 1):
                with sp.Fori(1, rounds) as r:
                    with sp.Fori(0, NE) as e:
                        load_expert(r * NE + e, e)

        @block.gpsimd
        def _(pool):
            pool.dma_start(wr[:, :, :], a["moe_router"][0].rearrange("(k p) e -> p k e", p=P)).then_inc(loaded_cache, 16)
            for l in range(DEPTH):
                pool.dma_start(kc[:, l, :], a["cache_swa_k"][l, 0].rearrange("s h d -> s (h d)")).then_inc(loaded_cache, 16)
                pool.dma_start(vc[:, l, :], a["cache_swa_v"][l, 0].rearrange("s h d -> s (h d)")).then_inc(loaded_cache, 16)
                pool.dma_start(ckvc[:, l, :], a["cache_mla_ckv"][l, 0]).then_inc(loaded_cache, 16)
                pool.dma_start(krc[:, l, :], a["cache_mla_krope"][l, 0]).then_inc(loaded_cache, 16)
            pool.wait_ge(loaded_g, GAINS_IN)
            pool.wait_ge(loaded_c, 16)
            for l in range(DEPTH):
                if l == 1:
                    wait_out(pool, ("to", 0, 2))
                for name, (rc, rsn, w) in rot.items():
                    cc = C("c64" if w == HD else "c32").rearrange("p (c w) -> p c w", c=2)
                    ss = C("s64" if w == HD else "s32").rearrange("p (c w) -> p c w", c=2)
                    g = G(name, l)
                    hw = w // 2
                    pool.tensor_tensor(rc[:, :, :], cc, bh(g, 2), ALU.mult)
                    pool.tensor_tensor(rsn[:, :, 0:hw], ss[:, :, 0:hw], bh(g[:, hw:w], 2), ALU.mult)
                    pool.tensor_tensor(rsn[:, :, hw:w], ss[:, :, hw:w], bh(g[:, 0:hw], 2), ALU.mult).then_inc(rot_ready, 1)
                pool.wait_ge(rows_ready, 3 * l + 3)
                for t in range(3):
                    rows = ROWS[t]
                    if t < 2:
                        o_c, o_r = out["ckv_p"][l, 0, t * P:(t + 1) * P, :], out["kr_p"][l, 0, t * P:(t + 1) * P, :]
                    else:
                        o_c, o_r = out["ckv_s"][l, 0], out["kr_s"][l, 0]
                    pool.dma_start(o_c, ckv[0:rows, t, :]).then_inc(stored, 16)
                    pool.dma_start(o_r, kr[0:rows, t, :]).then_inc(stored, 16)
                for t, o_k, o_v in ((1, out["k_p"], out["v_p"]), (2, out["k_s"], out["v_s"])):
                    rows = ROWS[t]
                    pool.dma_start(o_k[l, 0].rearrange("s h d -> s (h d)"), ka[0:rows, t, :]).then_inc(stored, 16)
                    pool.dma_start(o_v[l, 0].rearrange("s h d -> s (h d)"), v_sb[0:rows, t, :]).then_inc(stored, 16)

            pool.wait_ge(plan_ready, 1)
            rounds = pool.value_load(nround[0:1, 0:1], min_val=1, max_val=ROUNDS)
            surplus = [pool.snap(rounds * (NE * per_expert * 16) + 16 * (base_fills[s] + 1)) for s in range(MOE_PAIRS, RING)]
            pool.wait_ge(moe_done, 3)
            for t in range(2):
                pool.dma_start(out["y_p"][0, t * P:(t + 1) * P, :], xres[:, t, :]).then_inc(stored, 16)
            pool.dma_start(out["y_s"][0], xres[0:DEC, 2, :]).then_inc(stored, 16)
            pool.wait_ge(stored, 16 * (DEPTH * 10 + 3))
            for s, fills_ in zip(range(MOE_PAIRS, RING), surplus):
                pool.wait_ge(w_ready[s], fills_)

        @block.scalar
        def _(act):
            A = nc.scalar.activation
            act.dma_start(ln_rows[0:2 * KD, :], a["ln_attn"].rearrange("l (k p) -> (l k) p", p=P)).then_inc(loaded_ln, 16)
            act.dma_start(ln_rows[2 * KD:4 * KD, :], a["ln_ffn"].rearrange("l (k p) -> (l k) p", p=P)).then_inc(loaded_ln, 16)
            for l in range(DEPTH):
                for name, (at, w) in GAIN.items():
                    act.dma_start(gains[:, l, at:at + w], a[name][l:l + 1, :].to_broadcast([P, w])).then_inc(loaded_g, 16)

            def split_hi(src, n, hi, size):
                A(hi[:, 0:size], src[:, 0:size], ACT.Copy).then_inc(hi_ready, 1)

            def dense_hi_part(n):
                key = DENSE[n]
                act.wait_ge(w_ready[slot_of[key]], ready_at[key])
                wait_pair(act, n)
                split_hi(ring[:, slot_of[key], :], n, w_hi[n % DENSE_PAIRS], dense_size(key))

            def moe_hi_part(j, u, first=False):
                s = u % RING
                if first:
                    act.wait_ge(w_ready[s], 16 * (base_fills[s] + u // RING + 1))
                else:
                    act.wait_ge(w_ready[s], j * (16 * per_expert) + 16 * (base_fills[s] + u // RING + 1))
                    if u - MOE_PAIRS < len(EXPERT) - 1:
                        act.wait_ge(pair_used, j * (len(EXPERT) - 1) + (DOWN_USED + u - MOE_PAIRS + 1))
                    else:
                        act.wait_ge(y_full, j + 1)
                split_hi(ring[:, s, :], u, w_hi[u % MOE_PAIRS], moe_size(u))

            def norm(l, w):
                for t in range(3):
                    r = ROWS[t]
                    if w == 0 and l == 0:
                        act.wait_ge(loaded_x, 16 * 3)
                        act.wait_ge(loaded_c, 16)
                    elif w == 1:
                        wait_out(act, ("ty", l, KD - 1))
                    else:
                        wait_out(act, ("tz", KD - 1))
                    A(xn[0:r, t, :], xres[0:r, t, :], ACT.Square, accum_out=ssx[0:r, t:t + 1]).then_inc(sumsq_x, 1)
                for t in range(3):
                    r = ROWS[t]
                    act.wait_ge(sumsq_x, norm_no(l, w, t))
                    A(rtx[0:r, t:t + 1], ssx[0:r, t:t + 1], ACT.Sqrt, bias=C("eps", r), scale=1.0 / D).then_inc(root_x, 1)

            for l in range(DEPTH):
                norm(l, 0)
                for t in range(3):
                    r = ROWS[t]
                    wait_full(act, ("za", l, t))
                    za = pair(("za", l, t), r)
                    n = 3 * l + t
                    if n:
                        act.wait_ge(mean_z, n)
                    if l == 1 and t == 0:
                        act.wait_ge(stored, 16 * 10)
                    A(sq[0:r, 0:512], za[:, 0:512], ACT.Square)
                    A(sq[0:r, 512:S1], za[:, 512:S1], ACT.Square)
                    A(v_sb[0:r, t, :], za[:, S1:S2], ACT.Copy)
                    A(sq[0:r, S2:S3], za[:, S2:S3], ACT.Square)
                    wait_full(act, ("zc", l, t))
                    A(sq[0:r, S3:IN_W], pair(("zc", l, t), r)[:, 0:IN_W - S3], ACT.Square).then_inc(squares_z, 1)
                    act.wait_ge(mean_z, n + 1)
                    A(sr[0:r, 0:13], st[0:r, 0:13], ACT.Sqrt, bias=C("eps", r)).then_inc(root_z, 1)
                wait_full(act, ("tc", l))
                pc = pair(("tc", l))
                A(kTa[:, KOFF[2]:KOFF[2] + P], pc[:, 0:P], ACT.Copy)
                free(A(ckvT[:, KOFF[2]:KOFF[2] + P], pc[:, P:2 * P], ACT.Copy), ("tc", l))
                for t in range(3):
                    r, k0 = ROWS[t], KOFF[KT_OF_TILE[t]]
                    wait_full(act, ("tq", l, t))
                    v = pair(("tq", l, t)).rearrange("p (i c) -> p i c", c=P)
                    A(qTa[:, :, TOFF[t]:TOFF[t] + r], v[:, 0:4, 0:r], ACT.Copy)
                    A(kTa[:, k0:k0 + r], v[:, 4, 0:r], ACT.Copy)
                    A(cqT[:, :, TOFF[t]:TOFF[t] + r], v[:, 5:7, 0:r], ACT.Copy)
                    free(A(ckvT[:, k0:k0 + r], v[:, 7, 0:r], ACT.Copy), ("tq", l, t))
                for i in range(len(ITEMS) + 1):
                    if i < len(ITEMS):
                        kind, t = ITEMS[i]
                        r = ROWS[t] if kind == "q" else KROWS[t]
                        n = len(ITEMS) * l + i
                        wait_full(act, ("item", l, i))
                        v = pair(("item", l, i), r)
                        if n:
                            act.wait_ge(mean_i, n)
                        if kind == "q":
                            A(sqb[0:r, 0:512], v[:, 0:512], ACT.Square)
                            A(sqb[0:r, 512:768], v[:, 512:768], ACT.Square).then_inc(squares_i, 1)
                        else:
                            kv = v.rearrange("p (h c) -> p h c", h=HEADS)
                            A(vb[0:r, t, :].rearrange("p (h c) -> p h c", h=HEADS), kv[:, :, NOPE:NOPE + VD], ACT.Copy)
                            A(sqb[0:r, 0:512].rearrange("p (h c) -> p h c", h=HEADS), kv[:, :, 0:NOPE], ACT.Square)\
                                .then_inc(squares_i, 1)
                        act.wait_ge(mean_i, n + 1)
                        w = 16 if kind == "q" else 8
                        A(sr[0:r, 0:w], st[0:r, 0:w], ACT.Sqrt, bias=C("eps", r),
                          scale=1.0 if kind == "q" else 1.0 / NOPE).then_inc(root_i, 1)
                    if i >= 1:
                        kind, t = ITEMS[i - 1]
                        r = ROWS[t] if kind == "q" else KROWS[t]
                        wait_full(act, ("titem", l, i - 1))
                        v = pair(("titem", l, i - 1), QK).rearrange("p (h c) -> p h c", h=HEADS)[:, :, 0:r]
                        dst = qTb[0:QK, :, TOFF[t]:TOFF[t] + r] if kind == "q" else kTb[0:QK, :, KOFF[t]:KOFF[t] + r]
                        free(A(dst, v, ACT.Copy), ("titem", l, i - 1))
                for g in range(len(GROUPS) + 1):
                    if g < len(GROUPS):
                        typ, t, hg = GROUPS[g]
                        r = ROWS[t]
                        b = g % 2
                        nk = sum(KROWS[KEYS_OF[t][0]:KEYS_OF[t][1]])
                        act.wait_ge(negmax_ready, len(GROUPS) * l + g + 1)
                        if typ == "a":
                            A(es[0:r, b, :], dsk[0:r, b, :], ACT.Exp)
                        for i in range(4):
                            ins = A(sp_[0:r, b, i, 0:nk], sp_[0:r, b, i, 0:nk], ACT.Exp, bias=nb[0:r, b, i:i + 1],
                                    scale=A_SCALE if typ == "a" else B_SCALE, accum_out=rsum[0:r, b, i:i + 1])
                        ins.then_inc(exp_ready, 1)
                    if g >= 1:
                        typ, t, hg = GROUPS[g - 1]
                        r, b = ROWS[t], (g - 1) % 2
                        key = ("p", l, g - 1)
                        wait_full(act, key)
                        v = pair(key).rearrange("p (h k c) -> p h k c", h=4, k=2)
                        dst = pT[:, b].rearrange("p h (k c) -> p h k c", k=2)
                        if t == 0:
                            free(A(dst[:, :, 0, 0:r], v[:, :, 0, 0:r], ACT.Copy), key)
                        elif t == 1:
                            free(A(dst[:, :, :, 0:r], v[:, :, :, 0:r], ACT.Copy), key)
                        else:
                            A(dst[:, :, 0, 0:r], v[:, :, 0, 0:r], ACT.Copy)
                            free(A(dst[0:DEC, :, 1, 0:r], v[0:DEC, :, 1, 0:r], ACT.Copy), key)
                for t in range(3):
                    r = ROWS[t]
                    wait_full(act, ("to", l, t))
                    v = pair(("to", l, t)).rearrange("p (k c) -> p k c", k=KD)
                    free(A(hT[:, :, TOFF[t]:TOFF[t] + r], v[:, :, 0:r], ACT.Copy), ("to", l, t))
                for d in range(KD):
                    wait_full(act, ("wo", l, d))
                    if d >= 2:
                        wait_full(act, ("ty", l, d - 2))
                    free(A(yT[:, 0, d % 2, :], pair(("wo", l, d))[:, 0:TOK], ACT.Copy), ("wo", l, d))
                    if d == 0:
                        act.wait_ge(stored, 16 * 10 * (l + 1))
                    if d >= 5 and l == 0:
                        dense_hi_part(d - 5)
                    elif d >= 5:
                        moe_hi_part(0, d - 5, first=True)
                norm(l, 1)
                if l == 1:
                    for u in range(3, MOE_PAIRS):
                        moe_hi_part(0, u, first=True)
                if l == 0:
                    wait_full(act, ("hf", 0, 2))
                    for t in range(3):
                        wait_out(act, ("hf", 0, t))
                        A(hT_hi[:, :, TOFF[t]:TOFF[t] + ROWS[t]], hT[:, :, TOFF[t]:TOFF[t] + ROWS[t]], ACT.Copy).then_inc(tok_hi, 1)

                    def activations(i):
                        b = i % 2
                        wait_full(act, ("gate", i))
                        if i >= 2:
                            wait_out(act, ("up", i - 2))
                        g = pair(("gate", i)).rearrange("p (f c) -> p f c", f=2)[:, :, 0:TOK]
                        free(A(sg[:, b, :, :], g, ACT.Silu), ("gate", i))

                    def act_high(i):
                        wait_out(act, ("up", i))
                        A(aT_hi[:, 2 * i:2 * i + 2, :], aa[:, i % 2, :, :], ACT.Copy).then_inc(dense_hi, 1)

                    def down_out(c):
                        for h in range(2):
                            wait_full(act, ("dn", c, h))
                            wait_full(act, ("tz", 2 * h + 1) if c else ("ty", 0, KD - 1))
                            v = pair(("dn", c, h)).rearrange("p (f c) -> p f c", f=2)[:, :, 0:TOK]
                            free(A(yT[:, h, :, :], v, ACT.Copy), ("dn", c, h))

                    for n in range(DENSE_PAIRS, ND):
                        if n % 2 == 1 and 0 <= n // 2 - 2 < DCH:
                            act_high(n // 2 - 2)
                        if n % 2 == 1 and n // 2 - 1 < DCH:
                            activations(n // 2 - 1)
                        if n == DENSE.index(("down", 0, 5)) + DENSE_PAIRS:
                            down_out(0)
                        dense_hi_part(n)
                    down_out(1)

            for t in range(3):
                act.wait_ge(xn_ready, norm_no(1, 1, t))
                wait_full(act, ("hf", 1, t))
                A(xn_hi[0:ROWS[t], t, :], xn[0:ROWS[t], t, :], ACT.Copy).then_inc(tok_hi, 1)

            act.wait_ge(pair_diff, 1)
            for t in range(3):
                ins = A(dlt[0:ROWS[t], t, 1:2], dlt[0:ROWS[t], t, 0:1], ACT.Exp)
            ins.then_inc(pair_exp, 1)
            act.wait_ge(plan_ready, 1)
            rounds = act.value_load(nround[0:1, 0:1], min_val=1, max_val=ROUNDS)

            def tokens_high(count):
                act.wait_ge(xg_rows, count)
                A(xg_hi[:, :, :], xg[:, :, :], ACT.Copy).then_inc(xg_high, 1)

            tokens_high(1)
            with act.Fori(0, rounds) as r_:
                with act.Fori(0, NE) as e:
                    j = act.snap(r_ * NE + e)

                    def silu(c):
                        q = c % 2
                        act.wait_ge(gu_full[q], j * 3 + (c // 2 + 1))
                        A(sgm[:, q, 0:WIDTH[c]], ps[:, 2 * (1 - q), 0:WIDTH[c]], ACT.Silu).then_inc(silu_done, 1)

                    def chunk_high(c):
                        b, w = c % 2, WIDTH[c] // P
                        act.wait_ge(aT_full, j * CHUNKS + (c + 1))
                        A(am_hi[:, b, 0:w, :], ps[:, 5 if b == 0 else 4, 0:w * P].rearrange("p (k c) -> p k c", k=w),
                          ACT.Copy).then_inc(aT_high, 1)

                    def output_high():
                        act.wait_ge(pickT_free, j + 1)
                        act.wait_ge(y_full, j + 1)
                        A(y_hi[:, :], ps[:, 6:8, :].rearrange("p a c -> p (a c)"), ACT.Copy, scale=gslot[:, 0:1]).then_inc(y_high, 1)

                    for u in range(MOE_PAIRS, len(EXPERT) + MOE_PAIRS):
                        for what, c in MOE_EVENTS.get(u, ()):
                            if what == "act":
                                silu(c)
                            elif what == "turned":
                                chunk_high(c)
                            elif what == "tokens":
                                tokens_high(j + 2)
                            elif what == "output":
                                output_high()
                        moe_hi_part(j, u)

        @block.vector
        def _(dve):
            V = nc.vector
            steps = [0]

            def link(ins):
                steps[0] += 1
                ins.then_inc(dve_step, 1)
                dve.wait_ge(dve_step, steps[0])

            dve.wait_ge(ln_done, 1)
            V.tensor_copy(ln_cols[:, :], ps[:, 0, 0:4 * KD]).then_inc(ln_evac, 1)
            dve.wait_ge(ln_evac, 1)

            def split_lo(src, n_done, hi, lo, size):
                dve.wait_ge(hi_ready, n_done)
                V.tensor_tensor(lo[:, 0:size], src[:, 0:size], hi[:, 0:size].bitcast(F32), ALU.subtract).then_inc(lo_ready, 1)

            def dense_lo_part(n):
                key = DENSE[n]
                split_lo(ring[:, slot_of[key], :], n + 1, w_hi[n % DENSE_PAIRS], w_lo[n % DENSE_PAIRS], dense_size(key))

            def moe_lo_part(j, u, first=False):
                q = u % MOE_PAIRS
                done = ND + u + 1 if first else j * len(EXPERT) + (ND + u + 1)
                split_lo(ring[:, u % RING, :], done, w_hi[q], w_lo[q], moe_size(u))

            def norm(l, w):
                for t in range(3):
                    r = ROWS[t]
                    dve.wait_ge(root_x, norm_no(l, w, t))
                    link(V.reciprocal(rsx[0:r, t:t + 1], rtx[0:r, t:t + 1]))
                    V.tensor_scalar(xn[0:r, t, :], xres[0:r, t, :], rsx[0:r, t:t + 1], None, ALU.mult).then_inc(xn_ready, 1)
                for t in range(3):
                    r = ROWS[t]
                    key = ("hf" if w else "h", l, t)
                    wait_full(dve, key)
                    c0 = KD * (2 * w + l)
                    v = pair(key).rearrange("p (k c) -> p k c", k=KD)[:, :, 0:r]
                    free(V.tensor_tensor(hT[:, :, TOFF[t]:TOFF[t] + r], v, bc(ln_cols[:, c0:c0 + KD], r), ALU.mult), key)

            def rotate(dst, src, name, l, t, heads, t1, t2, perm=False):
                rc, rsn, w = rot[name]
                r, cls, hw = ROWS[t], min(t, 1), w // 2
                x = src.rearrange("p (h w) -> p h w", h=heads) if len(src.shape) == 2 else src
                u = t1[0:r, 0:heads * w].rearrange("p (h w) -> p h w", h=heads)
                v = t2[0:r, 0:heads * w].rearrange("p (h w) -> p h w", h=heads)
                V.tensor_tensor(u, x, bh(rc[0:r, cls, :], heads), ALU.mult)
                V.tensor_tensor(v[:, :, 0:hw], x[:, :, hw:w], bh(rsn[0:r, cls, 0:hw], heads), ALU.mult)
                link(V.tensor_tensor(v[:, :, hw:w], x[:, :, 0:hw], bh(rsn[0:r, cls, hw:w], heads), ALU.mult))
                if perm:
                    u = u.rearrange("p (g i) w -> p g i w", g=KVH)
                    v = v.rearrange("p (g i) w -> p g i w", g=KVH)
                    dst = dst.rearrange("p (i g w) -> p g i w", g=KVH, i=GRP)
                    for g in range(KVH):
                        ins = V.tensor_tensor(dst[:, g], u[:, g], v[:, g], ALU.add)
                    return ins
                return V.tensor_tensor(dst, u, v, ALU.add)

            for l in range(DEPTH):
                norm(l, 0)
                dve.wait_ge(rot_ready, 4 * (l + 1))
                for t in range(3):
                    r = ROWS[t]
                    dve.wait_ge(squares_z, 3 * l + t + 1)
                    V.reduce_sum(st[0:r, 0:10], sq[0:r, 0:S1].rearrange("p (h w) -> p h w", w=HD), AX_X)
                    V.reduce_sum(st[0:r, 10:11], sq[0:r, S2:S3], AX_X)
                    V.reduce_sum(st[0:r, 11:12], sq[0:r, S3:S4], AX_X)
                    link(V.reduce_sum(st[0:r, 12:13], sq[0:r, S4:IN_W], AX_X))
                    V.tensor_tensor(st[0:r, 0:13], st[0:r, 0:13], C("inv_a", r), ALU.mult).then_inc(mean_z, 1)
                    dve.wait_ge(root_z, 3 * l + t + 1)
                    link(V.reciprocal(rs[0:r, 0:13], sr[0:r, 0:13]))
                    za, zc = pair(("za", l, t), r), pair(("zc", l, t), r)
                    if t == 2:
                        wait_full(dve, ("tq", l, 0))
                    if t == 0 and l == 1:
                        dve.wait_ge(stored, 16 * 10)
                    V.tensor_tensor(tmp0[0:r, :].rearrange("p (h w) -> p h w", w=HD), za[:, 0:S1].rearrange("p (h w) -> p h w", w=HD),
                                    bc(rs[0:r, 0:10], HD), ALU.mult)
                    free(V.scalar_tensor_tensor(out=cqn[0:r, t % 2, :], in0=za[:, S2:S3], scalar=rs[0:r, 10:11],
                                                in1=G("b_cq_norm", l, r), op0=ALU.mult, op1=ALU.mult), ("za", l, t))
                    V.scalar_tensor_tensor(out=ckv[0:r, t, :], in0=zc[:, 0:KL], scalar=rs[0:r, 11:12],
                                           in1=G("b_ckv_norm", l, r), op0=ALU.mult, op1=ALU.mult)
                    free(V.tensor_scalar(rt0[0:r, 0:ROPE], zc[:, KL:KL + ROPE], rs[0:r, 12:13], None, ALU.mult), ("zc", l, t))
                    wait_out(dve, ("zc", l, t))
                    rotate(qa[0:r, t % 2, :], tmp0[0:r, 0:S0], "a_q_norm", l, t, HEADS, tmp1, tmp2, perm=True)
                    rotate(ka[0:r, t, :].rearrange("p (h w) -> p h w", h=KVH), tmp0[0:r, S0:S1], "a_k_norm", l, t, KVH,
                           tmp1[:, S0:S1], tmp2[:, S0:S1])
                    rotate(kr[0:r, t, :].rearrange("p (h w) -> p h w", h=1), rt0[0:r, 0:ROPE], "b_kr_norm", l, t, 1,
                           rt1, rt2).then_inc(rows_ready, 1)
                dve.wait_ge(rows_ready, 3 * l + 3)

                for i, (kind, t) in enumerate(ITEMS):
                    r = ROWS[t] if kind == "q" else KROWS[t]
                    n = len(ITEMS) * l + i
                    v = pair(("item", l, i), r)
                    dve.wait_ge(squares_i, n + 1)
                    if kind == "q":
                        s3 = sqb[0:r, :].rearrange("p (h w) -> p h w", h=HEADS)
                        V.reduce_sum(st[0:r, 0:8], s3[:, :, 0:NOPE], AX_X)
                        link(V.reduce_sum(st[0:r, 8:16], s3[:, :, NOPE:QK], AX_X))
                        V.tensor_tensor(st[0:r, :], st[0:r, :], C("inv_b", r), ALU.mult).then_inc(mean_i, 1)
                    else:
                        V.reduce_sum(st[0:r, 0:8], sqb[0:r, 0:512].rearrange("p (h w) -> p h w", h=HEADS), AX_X).then_inc(mean_i, 1)
                    dve.wait_ge(root_i, n + 1)
                    w = 16 if kind == "q" else 8
                    link(V.reciprocal(rs[0:r, 0:w], sr[0:r, 0:w]))
                    if i >= 2:
                        wait_full(dve, ("titem", l, i - 2))
                    dst = qkb[0:r, i % 2, :].rearrange("p (h w) -> p h w", h=HEADS)
                    nope = tmp0[0:r, 0:512].rearrange("p (h w) -> p h w", h=HEADS)
                    if kind == "q":
                        x = v[:, 0:768].rearrange("p (h w) -> p h w", h=HEADS)
                        xr = rt0[0:r, :].rearrange("p (h w) -> p h w", h=HEADS)
                        V.tensor_tensor(nope, x[:, :, 0:NOPE], bc(rs[0:r, 0:8], NOPE), ALU.mult)
                        free(V.tensor_tensor(xr, x[:, :, NOPE:QK], bc(rs[0:r, 8:16], ROPE), ALU.mult), ("item", l, i))
                        wait_out(dve, ("item", l, i))
                        V.tensor_tensor(dst[:, :, 0:NOPE], nope, bh(G("b_qn_norm", l, r), HEADS), ALU.mult)
                        rotate(dst[:, :, NOPE:QK], rt0[0:r, :], "b_qr_norm", l, t, HEADS, rt1, rt2).then_inc(item_ready, 1)
                    else:
                        x = v.rearrange("p (h w) -> p h w", h=HEADS)
                        free(V.tensor_tensor(nope, x[:, :, 0:NOPE], bc(rs[0:r, 0:8], NOPE), ALU.mult), ("item", l, i))
                        wait_out(dve, ("item", l, i))
                        V.tensor_tensor(dst[:, :, 0:NOPE], nope, bh(G("b_kn_norm", l, r), HEADS), ALU.mult)
                        if t == 2:
                            dve.wait_ge(loaded_cache, CACHES_IN)
                        own = krc[:, l, :] if t == 2 else kr[0:r, min(t, 2), :]
                        V.tensor_copy(dst[:, :, NOPE:QK], bh(own, HEADS)).then_inc(item_ready, 1)

                for g in range(len(GROUPS) + 2):
                    if g < len(GROUPS):
                        typ, t, hg = GROUPS[g]
                        r, b = ROWS[t], g % 2
                        nk = sum(KROWS[KEYS_OF[t][0]:KEYS_OF[t][1]])
                        key = ("s", l, g)
                        wait_full(dve, key)
                        if g >= 2:
                            wait_full(dve, ("p", l, g - 2))
                        src = pair(key, r).rearrange("p (h c) -> p h c", h=4)[:, :, 0:nk]
                        dst = sp_[0:r, b, :, 0:nk]
                        if t == 2:
                            free(V.tensor_copy(dst, src), key)
                        else:
                            m = C("mask0" if t == 0 else "mask1" + typ, r)
                            free(V.tensor_tensor(dst, src, bh(m, 4), ALU.add), key)
                        wait_out(dve, key)
                        link(V.reduce_max(mx[0:r, b, :], dst, AX_X))
                        if typ == "a":
                            sink = G("a_sinks", l, r)[:, 4 * hg:4 * hg + 4]
                            link(V.scalar_tensor_tensor(out=mm[0:r, b, :], in0=mx[0:r, b, :], scalar=A_SCALE, in1=sink,
                                                        op0=ALU.mult, op1=ALU.max))
                            V.tensor_scalar(nb[0:r, b, :], mm[0:r, b, :], -1.0, None, ALU.mult)
                            V.tensor_tensor(dsk[0:r, b, :], sink, mm[0:r, b, :], ALU.subtract).then_inc(negmax_ready, 1)
                        else:
                            V.tensor_scalar(nb[0:r, b, :], mx[0:r, b, :], -B_SCALE, None, ALU.mult).then_inc(negmax_ready, 1)
                    if 1 <= g <= len(GROUPS):
                        typ, t, hg = GROUPS[g - 1]
                        r, b = ROWS[t], (g - 1) % 2
                        dve.wait_ge(exp_ready, len(GROUPS) * l + g)
                        if typ == "a":
                            link(V.tensor_tensor(den[0:r, b, :], rsum[0:r, b, :], es[0:r, b, :], ALU.add))
                            link(V.reciprocal(rden[0:r, b, :], den[0:r, b, :]))
                        else:
                            link(V.reciprocal(rden[0:r, b, :], rsum[0:r, b, :]))
                    if g >= 2:
                        typ, t, hg = GROUPS[g - 2]
                        r, b = ROWS[t], (g - 2) % 2
                        key = ("o", l, g - 2)
                        wait_full(dve, key)
                        c0 = (typ == "b") * 512 + hg * 256
                        free(V.tensor_tensor(xn[0:r, t, c0:c0 + 256].rearrange("p (h w) -> p h w", h=4),
                                             pair(key, r)[:, 0:256].rearrange("p (h w) -> p h w", h=4),
                                             bc(rden[0:r, b, :], HD), ALU.mult), key)
                        wait_out(dve, key)

                def add_rows(key, d):
                    wait_full(dve, key)
                    v = pair(key).rearrange("p (t c) -> p t c", c=P)
                    V.tensor_tensor(xres[:, 0:2, d * P:(d + 1) * P], xres[:, 0:2, d * P:(d + 1) * P], v[:, 0:2, :], ALU.add)
                    free(V.tensor_tensor(xres[0:DEC, 2, d * P:(d + 1) * P], xres[0:DEC, 2, d * P:(d + 1) * P],
                                         v[0:DEC, 2, :], ALU.add), key)

                for d in range(KD):
                    add_rows(("ty", l, d), d)
                    if d >= 5 and l == 0:
                        dense_lo_part(d - 5)
                    elif d >= 5:
                        moe_lo_part(0, d - 5, first=True)
                norm(l, 1)
                if l == 1:
                    for u in range(3, MOE_PAIRS):
                        moe_lo_part(0, u, first=True)
                if l == 0:
                    for t in range(3):
                        c0, c1 = TOFF[t], TOFF[t] + ROWS[t]
                        dve.wait_ge(tok_hi, t + 1)
                        V.tensor_tensor(hT_lo[:, :, c0:c1], hT[:, :, c0:c1], hT_hi[:, :, c0:c1].bitcast(F32), ALU.subtract)\
                            .then_inc(tok_ready, 1)

                    def activations(i):
                        b = i % 2
                        if i >= 2:
                            dve.wait_ge(dense_act, i - 1)
                        wait_out(dve, ("gate", i))
                        wait_full(dve, ("up", i))
                        u = pair(("up", i)).rearrange("p (f c) -> p f c", f=2)[:, :, 0:TOK]
                        free(V.tensor_tensor(aa[:, b, :, :], sg[:, b, :, :], u, ALU.mult), ("up", i))

                    def act_low(i):
                        dve.wait_ge(dense_hi, i + 1)
                        V.tensor_tensor(aT_lo[:, 2 * i:2 * i + 2, :], aa[:, i % 2, :, :], aT_hi[:, 2 * i:2 * i + 2, :].bitcast(F32),
                                        ALU.subtract).then_inc(dense_act, 1)

                    for n in range(DENSE_PAIRS, ND):
                        if n % 2 == 0 and n // 2 - 2 < DCH:
                            activations(n // 2 - 2)
                        if n % 2 == 0 and 0 <= n // 2 - 3 < DCH:
                            act_low(n // 2 - 3)
                        if n == DENSE.index(("down", 0, 5)) + DENSE_PAIRS:
                            for d in range(4):
                                add_rows(("tz", d), d)
                        dense_lo_part(n)
                    for d in range(4, KD):
                        add_rows(("tz", d), d)

            wait_full(dve, ("router",))
            dve.wait_ge(stored, 16 * 20)
            for t in range(3):
                r = ROWS[t]
                dve.wait_ge(tok_hi, 3 + t + 1)
                V.tensor_tensor(xn_lo[0:r, t, :], xn[0:r, t, :], xn_hi[0:r, t, :].bitcast(F32), ALU.subtract).then_inc(tok_ready, 1)
            V.memset(y_hi[:, :].bitcast(F32), 0.0)
            V.memset(y_lo[:, :].bitcast(F32), 0.0)
            V.memset(pickT[:, :].bitcast(F32), 0.0).then_inc(y_free, 1)
            V.memset(possel[:, :, NJ:NJ + 1], -ABSENT)
            link(V.memset(gate[:, :, NJ:NJ + 1], 0.0))
            lp = pair(("router",))
            iota8 = C("iota")[:, 0:NE]
            for t in range(3):
                r = ROWS[t]
                link(V.tensor_copy(lg[0:r, t, :], lp[0:r, NE * t:NE * t + NE]))
                link(V.max(mx8[0:r, t, :], lg[0:r, t, :]))
                link(V.max_index(idx8[0:r, t, :], mx8[0:r, t, :], lg[0:r, t, :]))
                link(V.tensor_copy(idf[0:r, t, :], idx8[0:r, t, :]))
                V.tensor_scalar(oh1[0:r, t, :], iota8[0:r], idf[0:r, t, 0:1], None, ALU.is_equal)
                link(V.tensor_scalar(oh2[0:r, t, :], iota8[0:r], idf[0:r, t, 1:2], None, ALU.is_equal))
                V.tensor_tensor(member[0:r, t, :], oh1[0:r, t, :], oh2[0:r, t, :], ALU.add)
                ins = V.tensor_tensor(dlt[0:r, t, 0:1], mx8[0:r, t, 1:2], mx8[0:r, t, 0:1], ALU.subtract)
            ins.then_inc(pair_diff, 1)
            dve.wait_ge(pair_diff, 1)
            free(V.tensor_copy(cnt[0:1, 8:9], lp[0:1, 0:1]), ("router",))
            dve.wait_ge(pair_exp, 1)
            for t in range(3):
                r = ROWS[t]
                link(V.tensor_scalar(dlt[0:r, t, 2:3], dlt[0:r, t, 1:2], 1.0, None, ALU.add))
                link(V.reciprocal(dlt[0:r, t, 2:3], dlt[0:r, t, 2:3]))
                link(V.tensor_tensor(dlt[0:r, t, 3:4], dlt[0:r, t, 1:2], dlt[0:r, t, 2:3], ALU.mult))
                link(V.tensor_scalar(gtmp[0:r, t, :], oh2[0:r, t, :], dlt[0:r, t, 3:4], None, ALU.mult))
                for q in range(ROUNDS):
                    ins = V.scalar_tensor_tensor(out=gate[0:r, t, NE * q:NE * q + NE], in0=oh1[0:r, t, :], scalar=dlt[0:r, t, 2:3],
                                                 in1=gtmp[0:r, t, :], op0=ALU.mult, op1=ALU.add)
                link(ins)
            wait_full(dve, ("pos",))
            pp = pair(("pos",))
            for t in range(3):
                r = ROWS[t]
                for q in range(ROUNDS):
                    ins = V.scalar_tensor_tensor(out=posn[0:r, t, NE * q:NE * q + NE], in0=pp[0:r, NE * t:NE * t + NE],
                                                 scalar=ABSENT - SLOTS * q, in1=member[0:r, t, :], op0=ALU.add, op1=ALU.mult)
                link(ins)
                link(V.tensor_scalar(possel[0:r, t, 0:NJ], posn[0:r, t, :], -ABSENT, None, ALU.add))
            link(V.tensor_copy(cnt[0:1, 0:8], pp[0:1, NE * 3:NE * 4]))
            link(V.reduce_max(cnt[0:1, 8:9], cnt[0:1, 0:8], AX_X))
            V.tensor_scalar(cnt[0:1, 9:10], cnt[0:1, 8:9], SLOTS + 0.5, None, ALU.is_gt)
            link(V.tensor_scalar(cnt[0:1, 10:11], cnt[0:1, 8:9], 2 * SLOTS + 0.5, 1.0, ALU.is_gt, ALU.add))
            V.tensor_tensor(nround[:, :], cnt[0:1, 9:10], cnt[0:1, 10:11], ALU.add).then_inc(plan_ready, 1)
            dve.wait_ge(plan_ready, 1)

            rounds = dve.value_load(nround[0:1, 0:1], min_val=1, max_val=ROUNDS)

            def picks(col):
                for t in range(3):
                    r = ROWS[t]
                    V.tensor_copy(gcol[0:r, t:t + 1], gate[0:r, t, col])
                for t in range(3):
                    r = ROWS[t]
                    ins = V.tensor_scalar(pick[0:r, t, :], C("iota", r), possel[0:r, t, col], None, ALU.is_equal)
                ins.then_inc(pick_ready, 1)

            def tokens(count):
                dve.wait_ge(gathered, count)
                c0 = KD * 3
                V.tensor_tensor(xg[:, :, :], ps[:, 0:2, :].rearrange("p a (k c) -> p (a k) c", c=P),
                                bc(ln_cols[:, c0:c0 + KD], SLOTS), ALU.mult).then_inc(xg_rows, 1)
                dve.wait_ge(xg_high, count)
                V.tensor_tensor(xg_lo[:, :, :], xg[:, :, :], xg_hi[:, :, :].bitcast(F32), ALU.subtract).then_inc(xg_ready, 1)

            def add_tile(t, banks):
                r = ROWS[t]
                return V.tensor_tensor(xres[0:r, t, :], xres[0:r, t, :], ps[0:r, banks:banks + 2, :].rearrange("p a c -> p (a c)"), ALU.add)

            picks(slice(0, 1))
            tokens(1)
            with dve.Fori(0, rounds) as r_:
                with dve.Fori(0, NE) as e:
                    j = dve.snap(r_ * NE + e)

                    def activations(c):
                        q = c % 2
                        dve.wait_ge(silu_done, j * CHUNKS + (c + 1))
                        V.tensor_tensor(act_m[:, q, 0:WIDTH[c]], sgm[:, q, 0:WIDTH[c]], ps[:, 2 * (1 - q) + 1, 0:WIDTH[c]],
                                        ALU.mult).then_inc(gu_free[q], 1)

                    def chunk_low(c):
                        b, w = c % 2, WIDTH[c] // P
                        dve.wait_ge(aT_high, j * CHUNKS + (c + 1))
                        V.tensor_tensor(am_lo[:, b, 0:w, :], ps[:, 5 if b == 0 else 4, 0:w * P].rearrange("p (k c) -> p k c", k=w),
                                        am_hi[:, b, 0:w, :].bitcast(F32), ALU.subtract).then_inc(aT_free, 1)

                    def scatter():
                        for t in range(3):
                            dve.wait_ge(sc_full, j * 3 + (t + 1))
                            add_tile(t, SC_BANKS[t]).then_inc(sc_free, 1)

                    def slots():
                        dve.wait_ge(pickT_full, j + 1)
                        V.tensor_copy(gslot[:, :], ps[:, 4, TOK:TOK + 1])
                        V.tensor_copy(pickT[:, :], ps[:, 4, 0:TOK]).then_inc(pickT_free, 1)

                    def output_low():
                        dve.wait_ge(y_high, j + 1)
                        V.scalar_tensor_tensor(out=y_lo[:, :], in0=ps[:, 6:8, :].rearrange("p a c -> p (a c)"), scalar=gslot[:, 0:1],
                                               in1=y_hi[:, :].bitcast(F32), op0=ALU.mult, op1=ALU.subtract).then_inc(y_free, 1)

                    for u in range(MOE_PAIRS, len(EXPERT) + MOE_PAIRS):
                        for what, c in MOE_EVENTS.get(u, ()):
                            if what == "act":
                                activations(c)
                            elif what == "turned":
                                chunk_low(c)
                            elif what == "scatter":
                                scatter()
                            elif what == "slots":
                                slots()
                            elif what == "picks":
                                picks(bass.ds(j + 1, 1))
                            elif what == "tokens":
                                tokens(j + 2)
                            elif what == "output":
                                output_low()
                        moe_lo_part(j, u)
            for t in range(3):
                dve.wait_ge(last_full, t + 1)
                add_tile(t, SC_BANKS[t]).then_inc(moe_done, 1)

        @block.tensor
        def _(pe):
            mm_ = nc.tensor.matmul
            tr = nc.tensor.transpose
            seen = set()

            def weights(key):
                if key not in seen:
                    seen.add(key)
                    pe.wait_ge(w_ready[slot_of[key]], ready_at[key])

            def used_up(ins, key):
                ins.then_inc(w_used[slot_of[key]], 1)

            pe.wait_ge(loaded_c, 16)
            pe.wait_ge(loaded_ln, 32)
            ident = C("ident")
            tr(ps[:, 0, 0:4 * KD], ln_rows[:, :], ident[0:4 * KD, 0:4 * KD]).then_inc(ln_done, 1)
            pe.wait_ge(ln_evac, 1)

            def turn(key, src, rows):
                wait_room(pe, key)
                v = pair(key)
                for k in range(KD):
                    ins = tr(v[:, k * P:k * P + rows], src[0:rows, k * P:(k + 1) * P], ident[0:rows, 0:rows])
                full(ins, key)

            def turn_back(key, src_T, src, last_of=None):
                wait_room(pe, key)
                wait_out(pe, src)
                v = pair(key)
                for t in range(3):
                    ins = tr(v[0:ROWS[t], t * P:(t + 1) * P], src_T[:, TOFF[t]:TOFF[t] + ROWS[t]], ident)
                    if t == 0 and last_of:
                        used_up(ins, last_of)
                full(ins, key)

            for l in range(DEPTH):
                for t in range(3):
                    pe.wait_ge(xn_ready, norm_no(l, 0, t))
                    turn(("h", l, t), xn[:, t, :], ROWS[t])
                for t in range(3):
                    r = ROWS[t]
                    wait_out(pe, ("h", l, t))
                    key = ("za", l, t)
                    wait_room(pe, key)
                    v = pair(key, r)
                    for c in range(2):
                        for k in range(KD):
                            wk = ("in", l, c, k // 4)
                            weights(wk)
                            ins = mm_(v[:, 512 * c:512 * c + 512], hT[:, k, TOFF[t]:TOFF[t] + r], slot(wk, 4, 512)[:, k % 4, :],
                                      start=(k == 0), stop=(k == KD - 1))
                            if t == 2 and k % 4 == 3 and not (c == 1 and k == KD - 1):
                                used_up(ins, wk)
                    full(ins, key)
                    key = ("zc", l, t)
                    wait_room(pe, key)
                    wk = ("in", l, 2, 0)
                    weights(wk)
                    for k in range(KD):
                        ins = mm_(pair(key, r)[:, 0:IN_W - S3], hT[:, k, TOFF[t]:TOFF[t] + r], slot(wk, 8, IN_W - S3)[:, k, :],
                                  start=(k == 0), stop=(k == KD - 1))
                    full(ins, key)
                key = ("tc", l)
                wait_room(pe, key)
                pe.wait_ge(loaded_cache, CACHES_IN)
                v = pair(key)
                tr(v[:, 0:P], kc[:, l, :], ident)
                ins = tr(v[:, P:2 * P], ckvc[:, l, :], ident)
                full(ins, key)
                for t in range(3):
                    r = ROWS[t]
                    key = ("tq", l, t)
                    pe.wait_ge(rows_ready, 3 * l + t + 1)
                    wait_room(pe, key)
                    v = pair(key)
                    for i in range(4):
                        ins = tr(v[:, i * P:i * P + r], qa[0:r, t % 2, i * P:(i + 1) * P], ident[0:r, 0:r])
                        if t == 0 and i < 2:
                            used_up(ins, (("in", l, 1, 1), ("in", l, 2, 0))[i])
                    tr(v[:, 4 * P:4 * P + r], ka[0:r, t, :], ident[0:r, 0:r])
                    for i in range(2):
                        tr(v[:, (5 + i) * P:(5 + i) * P + r], cqn[0:r, t % 2, i * P:(i + 1) * P], ident[0:r, 0:r])
                    full(tr(v[:, 7 * P:7 * P + r], ckv[0:r, t, :], ident[0:r, 0:r]), key)
                weights(("uq", l))
                weights(("ukv", l))
                wait_out(pe, ("tc", l))
                for i in range(len(ITEMS) + 1):
                    if i < len(ITEMS):
                        kind, t = ITEMS[i]
                        key = ("item", l, i)
                        if kind == "q" or t != 2:
                            wait_out(pe, ("tq", l, t if kind == "q" else min(t, 2)))
                        wait_room(pe, key)
                        if kind == "q":
                            r = ROWS[t]
                            for c0, w in ((0, 512), (512, 256)):
                                for k in range(2):
                                    ins = mm_(pair(key, r)[:, c0:c0 + w], cqT[:, k, TOFF[t]:TOFF[t] + r],
                                              slot(("uq", l), 2, 768)[:, k, c0:c0 + w], start=(k == 0), stop=(k == 1))
                        else:
                            r = KROWS[t]
                            for c0 in (0, 512):
                                ins = mm_(pair(key, r)[:, c0:c0 + 512], ckvT[:, KOFF[t]:KOFF[t] + r],
                                          slot(("ukv", l), 1, 1024)[:, 0, c0:c0 + 512], start=True, stop=True)
                        full(ins, key)
                    if i >= 1:
                        kind, t = ITEMS[i - 1]
                        r = ROWS[t] if kind == "q" else KROWS[t]
                        key = ("titem", l, i - 1)
                        pe.wait_ge(item_ready, len(ITEMS) * l + i)
                        wait_room(pe, key)
                        for h in range(HEADS):
                            ins = tr(pair(key, QK)[:, h * P:h * P + r], qkb[0:r, (i - 1) % 2, h * QK:(h + 1) * QK], ident[0:r, 0:r])
                            if i == len(ITEMS) and h < 2:
                                used_up(ins, (("uq", l), ("ukv", l))[h])
                        full(ins, key)
                for g in range(len(GROUPS) + 2):
                    if g < len(GROUPS):
                        typ, t, hg = GROUPS[g]
                        r = ROWS[t]
                        k0 = KOFF[KEYS_OF[t][0]]
                        nk = sum(KROWS[KEYS_OF[t][0]:KEYS_OF[t][1]])
                        key = ("s", l, g)
                        if g == 0:
                            wait_out(pe, ("tq", l, 2))
                        if g == 6:
                            for i in range(len(ITEMS)):
                                wait_out(pe, ("titem", l, i))
                        wait_room(pe, key)
                        v = pair(key, r)
                        for i in range(4):
                            if typ == "a":
                                q, kk = qTa[64 * hg:64 * hg + 64, i, TOFF[t]:TOFF[t] + r], kTa[64 * hg:64 * hg + 64, k0:k0 + nk]
                            else:
                                h = 4 * hg + i
                                q, kk = qTb[0:QK, h, TOFF[t]:TOFF[t] + r], kTb[0:QK, h, k0:k0 + nk]
                            ins = mm_(v[:, 256 * i:256 * i + nk], q, kk, start=True, stop=True)
                        full(ins, key)
                    if 1 <= g <= len(GROUPS):
                        typ, t, hg = GROUPS[g - 1]
                        r, b = ROWS[t], (g - 1) % 2
                        key = ("p", l, g - 1)
                        pe.wait_ge(exp_ready, len(GROUPS) * l + g)
                        wait_room(pe, key)
                        v = pair(key).rearrange("p (h k c) -> p h k c", h=4, k=2)
                        for i in range(4):
                            for k, kt in enumerate(range(*KEYS_OF[t])):
                                kr_ = KROWS[kt]
                                ins = tr(v[0:kr_, i, k, 0:r], sp_[0:r, b, i, P * k:P * k + kr_], ident[0:r, 0:r])
                        full(ins, key)
                    if g >= 2:
                        typ, t, hg = GROUPS[g - 2]
                        r, b = ROWS[t], (g - 2) % 2
                        key = ("o", l, g - 2)
                        wait_out(pe, ("p", l, g - 2))
                        wait_room(pe, key)
                        kts = list(range(*KEYS_OF[t]))
                        for i in range(4):
                            for k, kt in enumerate(kts):
                                kr_ = KROWS[kt]
                                if typ == "b":
                                    h = 4 * hg + i
                                    val = vb[0:kr_, kt, h * VD:(h + 1) * VD]
                                elif kt == 2:
                                    val = vc[:, l, 64 * hg:64 * hg + 64]
                                else:
                                    val = v_sb[0:kr_, min(kt, 2), 64 * hg:64 * hg + 64]
                                ins = mm_(pair(key, r)[:, 64 * i:64 * i + 64], pT[0:kr_, b, i, P * k:P * k + r], val,
                                          start=(k == 0), stop=(k == len(kts) - 1))
                        full(ins, key)
                for t in range(3):
                    wait_out(pe, ("o", l, len(GROUPS) - 1))
                    wait_out(pe, ("o", l, len(GROUPS) - 2))
                    turn(("to", l, t), xn[:, t, :], ROWS[t])
                for t in range(3):
                    wait_out(pe, ("to", l, t))

                for d in range(KD + 1):
                    if d < KD:
                        key = ("wo", l, d)
                        wait_room(pe, key)
                        for k in range(KD):
                            wk = ("wo", l, d // 4, k // 4)
                            weights(wk)
                            ins = mm_(pair(key)[:, 0:TOK], slot(wk, 4, 512)[:, k % 4, (d % 4) * P:(d % 4 + 1) * P], hT[:, k, :],
                                      start=(k == 0), stop=(k == KD - 1))
                            if d % 4 == 3 and k == 3:
                                used_up(ins, wk)
                        full(ins, key)
                    if d >= 1:
                        turn_back(("ty", l, d - 1), yT[:, 0, (d - 1) % 2, :], ("wo", l, d - 1),
                                  last_of=("wo", l, d // 4 - 1, 1) if d % 4 == 0 else None)
                for t in range(3):
                    pe.wait_ge(xn_ready, norm_no(l, 1, t))
                    turn(("hf", l, t), xn[:, t, :], ROWS[t])
                for t in range(3):
                    wait_out(pe, ("hf", l, t))
                if l == 0:
                    pe.wait_ge(tok_ready, 3)
                    for n, (kind, i, *rest) in enumerate(DENSE):
                        hi, lo = w_hi[n % DENSE_PAIRS], w_lo[n % DENSE_PAIRS]
                        if kind != "down":
                            hi, lo = (w[:, :].rearrange("p (k c) -> p k c", k=KD) for w in (hi, lo))
                            key = (kind, i)
                            wait_room(pe, key)
                            pe.wait_ge(lo_ready, n + 1)
                            for f in range(2):
                                for k in range(KD):
                                    for m, (w, x) in enumerate(((hi, hT_hi), (hi, hT_lo), (lo, hT_hi))):
                                        ins = mm_(pair(key)[:, 512 * f:512 * f + TOK], w[:, k, f * P:(f + 1) * P], x[:, k, :],
                                                  start=(k == 0 and m == 0), stop=(k == KD - 1 and m == 2))
                            full(ins, key)
                            continue
                        g = rest[0]
                        hi, lo = (w[:, :].rearrange("p (k c) -> p k c", k=4) for w in (hi, lo))
                        if g == 0:
                            for h in range(2):
                                wait_room(pe, ("dn", i, h))
                        pe.wait_ge(dense_act, min(DCH, 2 * g + 2))
                        pe.wait_ge(lo_ready, n + 1)
                        last = min(4, FT - 4 * g) - 1
                        for k in range(last + 1):
                            for d in range(4):
                                for m, (w, x) in enumerate(((hi, aT_hi), (hi, aT_lo), (lo, aT_hi))):
                                    kk = 4 * g + k
                                    ins = mm_(pair(("dn", i, d // 2))[:, 512 * (d % 2):512 * (d % 2) + TOK], w[:, k, d * P:(d + 1) * P],
                                              x[:, kk, :], start=(kk == 0 and m == 0), stop=(kk == FT - 1 and m == 2))
                                if kk == FT - 1 and d % 2 == 1:
                                    full(ins, ("dn", i, d // 2))
                        if g < 5:
                            ins.then_inc(pair_used, 1)
                        else:
                            for d in range(4 * i, 4 * i + 4):
                                turn_back(("tz", d), yT[:, d // 2 % 2, d % 2, :], ("dn", i, d // 2 % 2))

            key = ("router",)
            wait_room(pe, key)
            for t in range(3):
                r = ROWS[t]
                for k in range(KD):
                    ins = mm_(pair(key, r)[:, NE * t:NE * t + NE], hT[:, k, TOFF[t]:TOFF[t] + r], wr[:, k, :],
                              start=(k == 0), stop=(k == KD - 1))
            full(ins, key)
            key = ("pos",)
            wait_room(pe, key)
            pe.wait_ge(pair_diff, 1)
            for t in range(3):
                r = ROWS[t]
                for u in range(t + 1):
                    lhs = C("upper", r)[:, 0:r] if u == t else C("ones")[:, 0:r]
                    mm_(pair(key, r)[:, NE * t:NE * t + NE], lhs, member[0:ROWS[u], u, :], start=(u == 0), stop=(u == t))
            for u in range(3):
                ins = mm_(pair(key, 1)[:, NE * 3:NE * 4], C("ones", ROWS[u])[:, 0:1], member[0:ROWS[u], u, :],
                          start=(u == 0), stop=(u == 2))
            full(ins, key)

            pe.wait_ge(plan_ready, 1)
            rounds = pe.value_load(nround[0:1, 0:1], min_val=1, max_val=ROUNDS)
            PARTS = ((0, 0), (0, 1), (1, 0))

            def gather(count):
                pe.wait_ge(pick_ready, count)
                for k in range(KD):
                    for t in range(3):
                        for m, x in enumerate((xn_hi, xn_lo)):
                            ins = mm_(ps[:, k // 4, (k % 4) * P:(k % 4 + 1) * P], x[0:ROWS[t], t, k * P:(k + 1) * P],
                                      pick[0:ROWS[t], t, :], start=(t == 0 and m == 0), stop=(t == 2 and m == 1))
                ins.then_inc(gathered, 1)

            def scatter(done, before_last=None, first_inc=None):
                for t in range(3):
                    if t == 2 and before_last:
                        before_last()
                    for h in range(2):
                        for m, y in enumerate((y_hi, y_lo)):
                            ins = mm_(ps[0:ROWS[t], SC_BANKS[t] + h, :], pickT[:, TOFF[t]:TOFF[t] + ROWS[t]],
                                      y[:, 512 * h:512 * h + 512], start=(m == 0), stop=(m == 1))
                            if first_inc is not None and t == 0 and h == 0 and m == 0:
                                ins.then_inc(first_inc, 1)
                    ins.then_inc(done, 1)

            pe.wait_ge(tok_ready, 6)
            gather(1)
            with pe.Fori(0, rounds) as r_:
                with pe.Fori(0, NE) as e:
                    j = pe.snap(r_ * NE + e)

                    def wait_unit(u):
                        pe.wait_ge(lo_ready, j * len(EXPERT) + (ND + u + 1))

                    def gate_up(c):
                        q = c % 2
                        if c >= 2:
                            pe.wait_ge(gu_free[q], j * 3 + c // 2)
                        for m in range(2):
                            for k in range(KD):
                                u = unit[("gate", "up")[m], c, k // 4]
                                if k % 4 == 0:
                                    wait_unit(u)
                                w = [x[u % MOE_PAIRS][:, 0:4 * WIDTH[c]].rearrange("p (k c) -> p k c", k=4) for x in (w_hi, w_lo)]
                                for n, (wp, xp) in enumerate(PARTS):
                                    ins = mm_(ps[:, 2 * (1 - q) + m, 0:WIDTH[c]], (xg_hi, xg_lo)[xp][:, k, :], w[wp][:, k % 4, :],
                                              start=(k == 0 and n == 0), stop=(k == KD - 1 and n == 2))
                                if k % 4 == 3 and not (m == 1 and k == KD - 1):
                                    ins.then_inc(pair_used, 1)
                        ins.then_inc(gu_full[q], 1)

                    def turn_chunk(c):
                        b, w = c % 2, WIDTH[c] // P
                        pe.wait_ge(gu_free[b], j * 3 + (c // 2 + 1))
                        if c == 1:
                            pe.wait_ge(pickT_free, j + 1)
                        if c >= 2:
                            pe.wait_ge(aT_free, j * CHUNKS + (c - 1))
                        for k in range(w):
                            ins = tr(ps[:, 5 if b == 0 else 4, k * P:(k + 1) * P], act_m[:, b, k * P:(k + 1) * P], ident)
                        ins.then_inc(aT_full, 1)

                    def down(c):
                        b, n = c % 2, WIDTH[c] // P // 2
                        pe.wait_ge(aT_free, j * CHUNKS + (c + 1))
                        for k in range(2 * n):
                            u = unit["down", c, k // n]
                            if k % n == 0:
                                wait_unit(u)
                            w = [x[u % MOE_PAIRS][:, 0:n * D].rearrange("p (k c) -> p k c", k=n) for x in (w_hi, w_lo)]
                            first, last = (c == 0 and k == 0), (c == CHUNKS - 1 and k == 2 * n - 1)
                            for h in range(2):
                                for i, (wp, xp) in enumerate(PARTS):
                                    ins = mm_(ps[:, 6 + h, :], (am_hi, am_lo)[xp][:, b, k, :], w[wp][:, k % n, 512 * h:512 * h + 512],
                                              start=(first and i == 0), stop=(last and i == 2))
                                    if c + 2 < CHUNKS and k == 0 and h == 0 and i == 0:
                                        ins.then_inc(pair_used, 1)
                            if k % n == n - 1:
                                ins.then_inc(y_full if last else pair_used, 1)

                    pe.wait_ge(xg_ready, j + 1)
                    gate_up(0)
                    pe.wait_ge(y_free, j + 1)
                    scatter(sc_full, lambda: pe.wait_ge(gu_free[0], j * 3 + 1), pair_used)
                    pe.wait_ge(sc_free, j * 3 + 1)
                    gate_up(1)
                    pe.wait_ge(sc_free, j * 3 + 2)
                    for t in range(3):
                        ins = tr(ps[:, 4, TOFF[t]:TOFF[t] + ROWS[t]], pick[0:ROWS[t], t, :].bitcast(F32), ident[0:ROWS[t], 0:ROWS[t]])
                        if t == 0:
                            ins.then_inc(pair_used, 1)
                    for t in range(3):
                        ins = mm_(ps[:, 4, TOK:TOK + 1], pick[0:ROWS[t], t, :].bitcast(F32), gcol[0:ROWS[t], t:t + 1],
                                  start=(t == 0), stop=(t == 2))
                    ins.then_inc(pickT_full, 1)
                    turn_chunk(0)
                    pe.wait_ge(sc_free, j * 3 + 3)
                    for c in range(2, CHUNKS):
                        gate_up(c)
                        down(c - 2)
                        turn_chunk(c - 1)
                    pe.wait_ge(gu_free[1], j * 3 + 3)
                    gather(j + 2)
                    down(CHUNKS - 2)
                    turn_chunk(CHUNKS - 1)
                    down(CHUNKS - 1)
            pe.wait_ge(y_free, rounds * NE + 1)
            pe.wait_ge(xg_ready, rounds * NE + 1)
            scatter(last_full)


_INS = ["x_prompt", "x_sample", "cache_swa_k", "cache_swa_v", "cache_mla_ckv", "cache_mla_krope", "ln_attn", "w_in",
        "a_q_norm", "a_k_norm", "a_sinks", "b_cq_norm", "b_w_uq", "b_ckv_norm", "b_w_ukv", "b_qn_norm", "b_qr_norm",
        "b_kn_norm", "b_kr_norm", "w_o", "ln_ffn", "ffn_w_gate", "ffn_w_up", "ffn_w_down", "moe_router", "moe_w_gate",
        "moe_w_up", "moe_w_down"]
_OUTS = [("y_p", (1, SEQ, D)), ("y_s", (1, DEC, D)), ("k_p", (DEPTH, 1, WINDOW, KVH, HD)), ("v_p", (DEPTH, 1, WINDOW, KVH, HD)),
         ("ckv_p", (DEPTH, 1, SEQ, KL)), ("kr_p", (DEPTH, 1, SEQ, ROPE)), ("k_s", (DEPTH, 1, DEC, KVH, HD)),
         ("v_s", (DEPTH, 1, DEC, KVH, HD)), ("ckv_s", (DEPTH, 1, DEC, KL)), ("kr_s", (DEPTH, 1, DEC, ROPE))]


def shape_constants():
    import numpy as np

    out = np.zeros((P, CONST_W), np.float32)

    def put(name, v):
        at, w = CONST[name]
        out[:, at:at + w] = v

    row = np.arange(P)
    put("ident", np.eye(P))
    put("upper", row[:, None] < row[None, :])
    put("ones", 1.0)
    put("iota", row[None, :])
    for w, c_name, s_name in ((HD, "c64", "s64"), (ROPE, "c32", "s32")):
        half = w // 2
        inv = np.float32(10000.0) ** (-(np.arange(half, dtype=np.float32) / np.float32(half)))
        for tile in range(2):
            ang = (row + P * tile).astype(np.float32)[:, None] * inv[None, :]
            c, s = np.cos(ang), np.sin(ang)
            at = CONST[c_name][0] + tile * w
            out[:, at:at + w] = np.concatenate([c, c], 1)
            at = CONST[s_name][0] + tile * w
            out[:, at:at + w] = np.concatenate([-s, s], 1)
    q, k = row[:, None] // CHUNK, np.arange(2 * P)[None, :] // CHUNK
    put("mask0", np.where(k[:, :P] <= q, 0.0, -1e30))
    q = q + P // CHUNK
    put("mask1a", np.where((k <= q) & (k >= q - WINDOW // CHUNK), 0.0, -1e30))
    put("mask1b", np.where(k <= q, 0.0, -1e30))
    put("inv_a", np.array([1 / HD] * 10 + [1 / QL, 1 / KL, 1 / ROPE], np.float32)[None, :])
    put("inv_b", np.array([1 / NOPE] * 8 + [1 / ROPE] * 8, np.float32)[None, :])
    put("eps", EPS)
    return out


def kernel(**inputs):
    import numpy as _np
    import concourse.bacc as _bacc
    from concourse.bass_utils import run_bass_kernel_spmd as _run

    nc = _bacc.Bacc("TRN2", target_bir_lowering=False, num_devices=1)
    arrays, a, out = {}, {}, {}
    for name in _INS:
        v = _np.ascontiguousarray(inputs[name])
        arrays[f"in_{name}"] = v
        a[name] = nc.dram_tensor(f"in_{name}", v.shape, mybir.dt.from_np(v.dtype), kind="ExternalInput").ap()
    arrays["shape_consts"] = shape_constants()
    consts = nc.dram_tensor("shape_consts", (P, CONST_W), F32, kind="ExternalInput").ap()
    for name, shape in _OUTS:
        out[name] = nc.dram_tensor(f"out_{name}", shape, F32, kind="ExternalOutput").ap()
    build(nc, a, out, consts)
    r = _run(nc, [arrays], core_ids=[0])
    return tuple(r.results[0][f"out_{name}"] for name, _ in _OUTS)
```

```python
from contextlib import ExitStack

import concourse.bass as bass
from concourse import mybir

F32 = mybir.dt.float32
F32R = mybir.dt.float32r
I32 = mybir.dt.int32
U32 = mybir.dt.uint32
ALU = mybir.AluOpType
ACT = mybir.ActivationFunctionType
AX_X = mybir.AxisListType.X

P = 128
D = 1024
KD = D // P
SEQ, DEC = 256, 32
TOK = SEQ + DEC
ROWS = [P, P, DEC]
TOFF = [0, P, 2 * P]
CHUNK, WINDOW = 64, 128
HEADS, KVH, HD = 8, 2, 64
GRP = HEADS // KVH
NOPE, ROPE, VD, QK = 64, 32, 64, 96
QL, KL = 256, 128
S0, S1, S2 = HEADS * HD, HEADS * HD + KVH * HD, HEADS * HD + 2 * KVH * HD
S3, S4 = S2 + QL, S2 + QL + KL
IN_W = S4 + ROPE
DFF = 2816
FT = DFF // P
NE = 8
DEPTH = 2
EPS = 1e-6
A_SCALE, B_SCALE = HD ** -0.5, QK ** -0.5
KEYS = 4
KOFF = [0, 128, 256, 384]
NKEY = 416
KROWS = [P, P, P, DEC]
KT_OF_TILE = [0, 1, 3]
KEYS_OF = [(0, 1), (0, 2), (2, 4)]
SLOTS = P
ROUNDS = (TOK + SLOTS - 1) // SLOTS
NJ = NE * ROUNDS
CW = 512
CHUNKS = (DFF + CW - 1) // CW
WIDTH = [min(CW, DFF - CW * c) for c in range(CHUNKS)]
DW = 2 * P
DCH = DFF // DW
RING = 6
DENSE_PAIRS, MOE_PAIRS = 3, 4
SLOT_W = 2048
ABSENT = 1000.0

CONST = {}
_at = 0
for _name, _w in (("ident", P), ("upper", P), ("ones", P), ("iota", P), ("c64", 2 * HD), ("s64", 2 * HD),
                  ("c32", 2 * ROPE), ("s32", 2 * ROPE), ("mask0", P), ("mask1a", 2 * P), ("mask1b", 2 * P),
                  ("inv_a", 13), ("inv_b", 16), ("eps", 1)):
    CONST[_name] = (_at, _w)
    _at += _w
CONST_W = _at

GAIN = {}
_at = 0
for _name, _w in (("a_q_norm", HD), ("a_k_norm", HD), ("b_cq_norm", QL), ("b_ckv_norm", KL), ("b_qn_norm", NOPE),
                  ("b_qr_norm", ROPE), ("b_kn_norm", NOPE), ("b_kr_norm", ROPE), ("a_sinks", HEADS)):
    GAIN[_name] = (_at, _w)
    _at += _w
GAIN_W = _at

ITEMS = [("k", 2), ("k", 0), ("q", 0), ("k", 1), ("q", 1), ("q", 2), ("k", 3)]
GROUPS = [(typ, t, hg) for typ in "ab" for t in range(3) for hg in range(2)]
FRONT = [("za", 0), ("tc",), ("zc", 0), ("item", 0),
         ("za", 1), ("zc", 1), ("tq", 0), ("titem", 0), ("item", 1), ("item", 2),
         ("za", 2), ("titem", 1), ("zc", 2), ("titem", 2), ("tq", 1), ("item", 3), ("item", 4),
         ("tq", 2), ("titem", 3), ("item", 5), ("item", 6), ("titem", 4), ("titem", 5), ("titem", 6)]
STEPS = len(GROUPS) + 2
NEEDS = {g: [i for i, (kind, t) in enumerate(ITEMS) if (t == tile if kind == "q" else KEYS_OF[tile][0] <= t < KEYS_OF[tile][1])]
         for g, (typ, tile, _) in enumerate(GROUPS) if typ == "b"}
TO_STEP = [STEPS - 4, STEPS - 2, STEPS - 1]


DENSE = [(m, i) for i in range(DCH) for m in ("gate", "up")] + [("down", c, g) for c in range(2) for g in range(6)]


def weight_plan():
    plan = []
    for layer in range(DEPTH):
        plan += [("in", layer, c, h) for c in range(2) for h in range(2)] + [("in", layer, 2, 0)]
        plan += [("uq", layer)]
        plan += [None] * (-(len(plan) + 4) % RING)
        plan += [("wo", layer, c, h) for c in range(2) for h in range(2)]
        if layer == 0:
            plan += DENSE
            plan += [None] * (-len(plan) % RING)
    return plan


def expert_plan():
    order = []
    for c in range(CHUNKS + 2):
        if c < CHUNKS:
            order += [(m, c, h) for m in ("gate", "up") for h in range(2)]
        if c >= 2:
            order += [("down", c - 2, h) for h in range(2)]
    return order


def moe_events():
    at = {key: u for u, key in enumerate(expert_plan())}
    ev = {}

    def put(u, what, c=0):
        ev.setdefault(u, []).append((what, c))

    put(at["up", 0, 1] + MOE_PAIRS, "act", 0)
    put(at["gate", 0, 1] + MOE_PAIRS, "scatter", 0)
    put(at["gate", 0, 1] + MOE_PAIRS, "scatter", 1)
    put(at["up", 0, 1] + MOE_PAIRS + 1, "scatter", 2)
    for c in range(1, CHUNKS):
        put(at["up", c, 1] + MOE_PAIRS, "act", c)
        if c == 1:
            put(at["up", 1, 1] + MOE_PAIRS, "slots")
        put((at["up", 1, 1] if c == 1 else at["down", c - 2, 1]) + MOE_PAIRS, "turned", c - 1)
    put(at["up", 2, 1] + MOE_PAIRS + 2, "picks")
    put(at["down", CHUNKS - 3, 1] + MOE_PAIRS + 1, "tokens")
    put(at["down", CHUNKS - 3, 1] + MOE_PAIRS + 1, "turned", CHUNKS - 1)
    put(at["down", CHUNKS - 1, 1] + MOE_PAIRS, "output")
    return ev


def psum_plan():
    jobs = []
    for l in range(DEPTH):
        jobs += [("h", l, t) for t in range(3)]
        jobs += [(kind, l, *n) for kind, *n in FRONT]
        for g in range(STEPS):
            if g < len(GROUPS):
                jobs.append(("s", l, g))
            if 1 <= g <= len(GROUPS):
                jobs.append(("p", l, g - 1))
            if g >= 2:
                jobs.append(("o", l, g - 2))
            if g in TO_STEP:
                jobs.append(("to", l, TO_STEP.index(g)))
        for d in range(KD + 1):
            if d < KD:
                jobs.append(("wo", l, d))
            if d >= 1:
                jobs.append(("ty", l, d - 1))
        jobs += [("hf", l, t) for t in range(3)]
        if l == 0:
            jobs += [(m, i) for i in range(DCH) for m in ("gate", "up")]
            for c in range(2):
                jobs += [("dn", c, h) for h in range(2)]
                jobs += [("tz", d) for d in range(4 * c, 4 * c + 4)]
        else:
            jobs += [("router",), ("pos",)]
    return jobs


def build(nc, a, out, consts):
    plan = weight_plan()
    slot_of, ready_at = {}, {}
    fills = [0] * RING
    for n, key in enumerate(plan):
        if key is not None:
            slot_of[key] = n % RING
            fills[n % RING] += 1
            ready_at[key] = 16 * fills[n % RING]
    base_fills = list(fills)
    assert len(plan) % RING == 0
    before = {}
    for n, key in enumerate(plan):
        prev = [k for k in plan[n % RING:n:RING] if k is not None]
        if key is not None and prev:
            before[key] = prev[-1]
    last_in_slot = [[k for k in plan[s_::RING] if k is not None][-1] for s_ in range(RING)]
    used_at, tally = {}, [0] * RING
    for n, key in enumerate(plan):
        if key is not None and key not in DENSE:
            tally[n % RING] += 1
            used_at[key] = tally[n % RING]
    EXPERT = expert_plan()
    unit = {key: u for u, key in enumerate(EXPERT)}
    MOE_EVENTS = moe_events()
    per_expert = len(EXPERT) // RING
    assert len(EXPERT) % RING == 0
    jobs = {key: n for n, key in enumerate(psum_plan())}

    with ExitStack() as ctx:
        def sb(name, shape, dt=F32):
            return ctx.enter_context(nc.sbuf_tensor(name, shape, dt))

        def sem(name):
            return ctx.enter_context(nc.semaphore(name))

        ring = sb("ring", [P, RING, SLOT_W])
        cst = sb("cst", [P, CONST_W])
        gains = sb("gains", [P, DEPTH, GAIN_W])
        ln_rows = sb("ln_rows", [4 * KD, P])
        ln_cols = sb("ln_cols", [P, 4 * KD])
        xres = sb("xres", [P, 3, D])
        ssx = sb("ssx", [P, 3])
        warm = sb("warm", [P, 1])
        rtx = sb("rtx", [P, 3])
        rsx = sb("rsx", [P, 3])
        kc, vc, ckvc, krc = (sb("cache_" + n, [P, DEPTH, w]) for n, w in (("k", KVH * HD), ("v", KVH * HD), ("ckv", KL), ("kr", ROPE)))
        wr = sb("wr", [P, KD, NE])
        yT = sb("yT", [P, 2, 2, TOK])
        rot = {}
        for name, w in (("a_q_norm", HD), ("a_k_norm", HD), ("b_qr_norm", ROPE), ("b_kr_norm", ROPE)):
            rot[name] = (sb("rc_" + name, [P, 2, w]), sb("rs_" + name, [P, 2, w]), w)
        idx8 = sb("idx8", [P, 3, NE], U32)
        nround = sb("nround", [1, 1], I32)

        slab_at = (nc.sbuf_base + 63) // 64 * 64
        slab_w = (nc.sbuf_usable_end - slab_at) // 4 - 32
        sb("slab", [P, slab_w])

        def at(name, offset, shape, dt=F32):
            n = 1
            for s in shape[1:]:
                n *= s
            assert offset + n <= slab_w, (name, offset + n, slab_w)
            return nc.alloc_sbuf_tensor_at(name, shape, dt, offset=slab_at + 4 * offset)

        XN, HT = 0, 3 * D
        PHASE = HT + KD * TOK
        xn = at("xn", XN, [P, 3, D])
        hT = at("hT", HT, [P, KD, TOK])
        w_hi = [at(f"w_hi{i}", PHASE + 2 * SLOT_W * i, [P, SLOT_W], F32R) for i in range(MOE_PAIRS)]
        w_lo = [at(f"w_lo{i}", PHASE + 2 * SLOT_W * i + SLOT_W, [P, SLOT_W], F32R) for i in range(MOE_PAIRS)]

        class Carve:

            def __init__(self, start):
                self.at = start

            def __call__(self, name, *shape, dt=F32):
                n = 1
                for s in shape:
                    n *= s
                start, self.at = self.at, self.at + (n + 7) // 8 * 8
                return at(name, start, [P, *shape], dt)

        carve = Carve(PHASE)
        sq = carve("sq", IN_W)
        sqb = carve("sqb", HEADS * QK)
        qa = carve("qa", 2, S0)
        cqn = carve("cqn", 2, QL)
        tmp1 = carve("tmp1", S1)
        tmp2 = carve("tmp2", S1)
        sp_ = carve("sp_", 2, 4, 2 * P)
        pT = carve("pT", 2, 4, 2 * P)
        v_sb = carve("v_sb", 3, KVH * HD)
        ka = carve("ka", 3, KVH * HD)
        ckv = carve("ckv", 3, KL)
        kr = carve("kr", 3, ROPE)
        tmp0 = carve("tmp0", S1)
        rt0 = carve("rt0", ROPE * HEADS)
        rt1 = carve("rt1", ROPE * HEADS)
        rt2 = carve("rt2", ROPE * HEADS)
        st = carve("st", 16)
        sr = carve("sr", 16)
        rs = carve("rs", 16)
        qTa = carve("qTa", GRP, TOK)
        kTa = carve("kTa", NKEY)
        cqT = carve("cqT", 2, TOK)
        ckvT = carve("ckvT", NKEY)
        qkb = carve("qkb", 2, HEADS * QK)
        vb = carve("vb", KEYS, HEADS * VD)
        qTb = carve("qTb", HEADS, TOK)
        kTb = carve("kTb", HEADS, NKEY)
        mx, mm, nb, dsk, es, rsum, den, rden = (carve(n, 2, 4) for n in ("mx", "mm", "nb", "dsk", "es", "rsum", "den", "rden"))

        carve = Carve(PHASE + 2 * SLOT_W * DENSE_PAIRS)
        w_ukv = yT[:, :, :, :].rearrange("p a b c -> p (a b c)")[:, 0:HEADS * (NOPE + VD)]
        hT_hi = at("hT_hi", XN, [P, KD, TOK], F32R)
        hT_lo = at("hT_lo", HT, [P, KD, TOK], F32R)
        sg = yT
        aa = carve("aa", 2, 2, TOK)
        aT_hi = carve("aT_hi", FT, TOK, dt=F32R)
        aT_lo = carve("aT_lo", FT, TOK, dt=F32R)

        xn_lo = at("xn_lo", XN, [P, 3, D], F32R)
        over = Carve(HT)
        xg_hi = over("xg_hi", KD, SLOTS, dt=F32R)
        xg_lo = over("xg_lo", KD, SLOTS, dt=F32R)
        assert over.at <= PHASE
        carve = Carve(PHASE + 2 * SLOT_W * MOE_PAIRS)
        xn_hi = carve("xn_hi", 3, D, dt=F32R)
        lg, mx8, idf, oh1, oh2, member, goh, gtmp = (carve(n, 3, NE) for n in ("lg", "mx8", "idf", "oh1", "oh2", "member", "goh", "gtmp"))
        dlt = carve("dlt", 3, 4)
        gate = carve("gate", 3, NJ + 1)
        posn = carve("posn", 3, NJ)
        possel = carve("possel", 3, NJ + 1)
        cnt = carve("cnt", 16)
        pick = carve("pick", 3, SLOTS, dt=F32R)
        gcol = carve("gcol", 4)
        gslot = carve("gslot", 1)
        pickT = carve("pickT", TOK, dt=F32R)
        xg = yT[:, :, :, :].rearrange("p a b c -> p (a b c)")[:, 0:KD * SLOTS].rearrange("p (k c) -> p k c", k=KD)
        sgm = gains[:, :, :].rearrange("p l w -> p (l w)")[:, 0:2 * CW].rearrange("p (a b) -> p a b", a=2)
        act_m = carve("act_m", 2, CW)
        am_hi = carve("am_hi", 2, CW // P, SLOTS, dt=F32R)
        am_lo = carve("am_lo", 2, CW // P, SLOTS, dt=F32R)
        y_hi = carve("y_hi", D, dt=F32R)
        y_lo = carve("y_lo", D, dt=F32R)
        ps = ctx.enter_context(nc.psum_tensor("ps", [P, 8, 512], F32))

        warm_set = sem("warm_set")
        loaded_x = sem("loaded_x")
        loaded_c = sem("loaded_c")
        loaded_ln = sem("loaded_ln")
        loaded_g = [sem(f"loaded_g{l}") for l in range(DEPTH)]
        loaded_cache = sem("loaded_cache")
        ukv_ready = sem("ukv_ready")
        w_ready = [sem(f"w_ready{i}") for i in range(RING)]
        w_used = [sem(f"w_used{i}") for i in range(RING)]
        bank_full = [sem(f"bank_full{i}") for i in range(4)]
        bank_free = [sem(f"bank_free{i}") for i in range(4)]
        ln_done = sem("ln_done")
        ln_evac = sem("ln_evac")
        rot_ready = sem("rot_ready")
        sumsq_x = sem("sumsq_x")
        root_x = sem("root_x")
        xn_ready = sem("xn_ready")
        dve_step = sem("dve_step")
        squares_z = sem("squares_z")
        mean_z = sem("mean_z")
        root_z = sem("root_z")
        rows_ready = sem("rows_ready")
        squares_i = sem("squares_i")
        mean_i = sem("mean_i")
        root_i = sem("root_i")
        item_ready = sem("item_ready")
        negmax_ready = sem("negmax_ready")
        exp_ready = sem("exp_ready")
        pair_diff = sem("pair_diff")
        pair_exp = sem("pair_exp")
        plan_ready = sem("plan_ready")
        stored = sem("stored")
        hi_ready = sem("hi_ready")
        lo_ready = sem("lo_ready")
        pair_used = sem("pair_used")
        tok_hi = sem("tok_hi")
        tok_ready = sem("tok_ready")
        dense_hi = sem("dense_hi")
        dense_act = sem("dense_act")
        pick_ready = sem("pick_ready")
        gathered = sem("gathered")
        xg_rows = sem("xg_rows")
        xg_high = sem("xg_high")
        xg_ready = sem("xg_ready")
        gu_full = [sem("gu_full0"), sem("gu_full1")]
        silu_done = sem("silu_done")
        gu_free = [sem("gu_free0"), sem("gu_free1")]
        pickT_full = sem("pickT_full")
        pickT_free = sem("pickT_free")
        aT_full = sem("aT_full")
        aT_high = sem("aT_high")
        aT_free = sem("aT_free")
        y_full = sem("y_full")
        y_high = sem("y_high")
        y_free = sem("y_free")
        sc_full = sem("sc_full")
        sc_free = sem("sc_free")
        last_full = sem("last_full")
        moe_done = sem("moe_done")

        def C(name, rows=P):
            at, w = CONST[name]
            return cst[0:rows, at:at + w]

        def G(name, l, rows=P):
            at, w = GAIN[name]
            return gains[0:rows, l, at:at + w]

        def pair(key, rows=P):
            p = jobs[key] % 4
            return ps[0:rows, 2 * p:2 * p + 2, :].rearrange("p a b -> p (a b)")

        def slot(key, n, w):
            s = slot_of[key]
            return ring[:, s, 0:n * w].rearrange("p (n w) -> p n w", n=n)

        def wait_full(eng, key):
            eng.wait_ge(bank_full[jobs[key] % 4], jobs[key] // 4 + 1)

        def wait_out(eng, key):
            eng.wait_ge(bank_free[jobs[key] % 4], jobs[key] // 4 + 1)

        def wait_room(eng, key):
            if jobs[key] >= 4:
                eng.wait_ge(bank_free[jobs[key] % 4], jobs[key] // 4)

        def full(ins, key):
            ins.then_inc(bank_full[jobs[key] % 4], 1)

        def free(ins, key):
            ins.then_inc(bank_free[jobs[key] % 4], 1)

        def norm_no(l, w, t):
            return 3 * (2 * l + w) + t + 1

        def bc(v, n):
            return v.unsqueeze(2).to_broadcast([v.shape[0], v.shape[1], n])

        def bh(v, n):
            return v.unsqueeze(1).to_broadcast([v.shape[0], n, v.shape[1]])

        ND = len(DENSE)
        unit_job = {}
        down_used = {}
        for n, key in enumerate(DENSE):
            if key[0] != "down":
                unit_job[n] = key
            elif key[2] == 5:
                unit_job[n] = ("dn", key[1], 1)
            else:
                down_used[n] = 5 * key[1] + key[2] + 1
        SC_BANKS = (0, 4, 4)
        SPLIT_AT = (2, 3, 5)
        DOWN_USED = 10

        def wait_pair(eng, n):
            m = n - DENSE_PAIRS
            if m >= 0:
                if m in unit_job:
                    wait_full(eng, unit_job[m])
                else:
                    eng.wait_ge(pair_used, down_used[m])

        def dense_size(key):
            return SLOT_W if key[0] != "down" or key[2] < 5 else SLOT_W // 2

        def moe_size(u):
            kind, c, h = EXPERT[u % len(EXPERT)]
            return 4 * WIDTH[c] if kind != "down" else WIDTH[c] // P // 2 * D

        GAINS_IN = 16 * len(GAIN)
        CACHES_IN = 16 * (1 + 4 * DEPTH)

        block = ctx.enter_context(nc.Block())

        @block.sync
        def _(sp):
            for t in range(2):
                sp.dma_start(xres[:, t, :], a["x_prompt"][0, t * P:(t + 1) * P, :]).then_inc(loaded_x, 16)
            sp.dma_start(xres[0:DEC, 2, :], a["x_sample"][0]).then_inc(loaded_x, 16)
            sp.dma_start(cst[:, :], consts).then_inc(loaded_c, 16)

            def source(key):
                kind = key[0]
                if kind == "in":
                    _, l, c, h = key
                    w = a["w_in"][l].rearrange("(k p) n -> p k n", p=P)
                    return (w[:, 4 * h:4 * h + 4, 512 * c:512 * c + 512], 4, 512) if c < 2 else (w[:, :, 1024:IN_W], 8, IN_W - 1024)
                if kind == "uq":
                    return a["b_w_uq"][key[1]].rearrange("(k p) n -> p k n", p=P), 2, HEADS * QK
                if kind == "wo":
                    _, l, c, h = key
                    return a["w_o"][l].rearrange("(k p) n -> p k n", p=P)[:, 4 * h:4 * h + 4, 512 * c:512 * c + 512], 4, 512
                if kind in ("gate", "up"):
                    w = a["ffn_w_" + kind][0].rearrange("(k p) n -> p k n", p=P)
                    return w[:, :, DW * key[1]:DW * key[1] + DW], KD, DW
                _, c, g = key
                n = min(4, FT - 4 * g)
                return a["ffn_w_down"][0].rearrange("(k p) n -> p k n", p=P)[:, 4 * g:4 * g + n, 512 * c:512 * c + 512], n, 512

            def slot_room(key):
                if key in DENSE:
                    sp.wait_ge(lo_ready, DENSE.index(key) + 1)
                else:
                    sp.wait_ge(w_used[slot_of[key]], used_at[key])

            def load_gains(l):
                for name, (at, w) in GAIN.items():
                    sp.dma_start(gains[:, l, at:at + w], a[name][l:l + 1, :].to_broadcast([P, w])).then_inc(loaded_g[l], 16)

            for key in plan:
                if key is None:
                    continue
                if key == ("uq", 0):
                    load_gains(0)
                elif key == ("wo", 0, 0, 0):
                    load_gains(1)
                if key in before:
                    slot_room(before[key])
                src, n, w = source(key)
                sp.dma_start(slot(key, n, w), src).then_inc(w_ready[slot_of[key]], 16)
                if key[0] == "uq":
                    if key[1]:
                        wait_full(sp, ("tz", KD - 1))
                    sp.dma_start(w_ukv, a["b_w_ukv"][key[1]]).then_inc(ukv_ready, 16)

            def load_unit(u, e):
                kind, c, h = EXPERT[u]
                s = u % RING
                if kind != "down":
                    n, wd = 4, WIDTH[c]
                    src = a["moe_w_" + kind][0, bass.ds(e, 1)].rearrange("o (k p) n -> p (o k) n", p=P)[:, 4 * h:4 * h + 4, CW * c:CW * c + wd]
                else:
                    n, wd = WIDTH[c] // P // 2, D
                    k0 = 4 * c + n * h
                    src = a["moe_w_down"][0].rearrange("e (k p) n -> p (e k) n", p=P)[:, bass.ds(e * FT + k0, n), :]
                sp.dma_start(ring[:, s, 0:n * wd].rearrange("p (n w) -> p n w", n=n), src).then_inc(w_ready[s], 16)

            for u in range(RING):
                slot_room(last_in_slot[u])
                load_unit(u, 0)

            def load_expert(j, e):
                after = sp.snap((e + 1) % NE)
                for u in range(RING, len(EXPERT) + RING):
                    sp.wait_ge(lo_ready, j * len(EXPERT) + (ND + u - RING + 1))
                    load_unit(u % len(EXPERT), e if u < len(EXPERT) else after)

            with sp.Fori(0, NE) as e:
                load_expert(e, e)
            sp.wait_ge(plan_ready, 1)
            rounds = sp.value_load(nround[0:1, 0:1], min_val=1, max_val=ROUNDS)
            with sp.If(rounds > 1):
                with sp.Fori(1, rounds) as r:
                    with sp.Fori(0, NE) as e:
                        load_expert(r * NE + e, e)

        @block.gpsimd
        def _(pool):
            pool.dma_start(wr[:, :, :], a["moe_router"][0].rearrange("(k p) e -> p k e", p=P)).then_inc(loaded_cache, 16)
            for l in range(DEPTH):
                pool.dma_start(kc[:, l, :], a["cache_swa_k"][l, 0].rearrange("s h d -> s (h d)")).then_inc(loaded_cache, 16)
                pool.dma_start(vc[:, l, :], a["cache_swa_v"][l, 0].rearrange("s h d -> s (h d)")).then_inc(loaded_cache, 16)
                pool.dma_start(ckvc[:, l, :], a["cache_mla_ckv"][l, 0]).then_inc(loaded_cache, 16)
                pool.dma_start(krc[:, l, :], a["cache_mla_krope"][l, 0]).then_inc(loaded_cache, 16)
            pool.wait_ge(loaded_c, 16)
            for l in range(DEPTH):
                pool.wait_ge(loaded_g[l], GAINS_IN)
                if l == 1:
                    wait_out(pool, ("to", 0, 2))
                for name, (rc, rsn, w) in rot.items():
                    cc = C("c64" if w == HD else "c32").rearrange("p (c w) -> p c w", c=2)
                    ss = C("s64" if w == HD else "s32").rearrange("p (c w) -> p c w", c=2)
                    g = G(name, l)
                    hw = w // 2
                    pool.tensor_tensor(rc[:, :, :], cc, bh(g, 2), ALU.mult)
                    pool.tensor_tensor(rsn[:, :, 0:hw], ss[:, :, 0:hw], bh(g[:, hw:w], 2), ALU.mult)
                    pool.tensor_tensor(rsn[:, :, hw:w], ss[:, :, hw:w], bh(g[:, 0:hw], 2), ALU.mult).then_inc(rot_ready, 1)
                pool.wait_ge(rows_ready, 3 * l + 3)
                for t in range(3):
                    rows = ROWS[t]
                    if t < 2:
                        o_c, o_r = out["ckv_p"][l, 0, t * P:(t + 1) * P, :], out["kr_p"][l, 0, t * P:(t + 1) * P, :]
                    else:
                        o_c, o_r = out["ckv_s"][l, 0], out["kr_s"][l, 0]
                    pool.dma_start(o_c, ckv[0:rows, t, :]).then_inc(stored, 16)
                    pool.dma_start(o_r, kr[0:rows, t, :]).then_inc(stored, 16)
                for t, o_k, o_v in ((1, out["k_p"], out["v_p"]), (2, out["k_s"], out["v_s"])):
                    rows = ROWS[t]
                    pool.dma_start(o_k[l, 0].rearrange("s h d -> s (h d)"), ka[0:rows, t, :]).then_inc(stored, 16)
                    pool.dma_start(o_v[l, 0].rearrange("s h d -> s (h d)"), v_sb[0:rows, t, :]).then_inc(stored, 16)

            pool.wait_ge(plan_ready, 1)
            rounds = pool.value_load(nround[0:1, 0:1], min_val=1, max_val=ROUNDS)
            surplus = [pool.snap(rounds * (NE * per_expert * 16) + 16 * (base_fills[s] + 1)) for s in range(MOE_PAIRS, RING)]
            pool.wait_ge(moe_done, 3)
            for t in range(2):
                pool.dma_start(out["y_p"][0, t * P:(t + 1) * P, :], xres[:, t, :]).then_inc(stored, 16)
            pool.dma_start(out["y_s"][0], xres[0:DEC, 2, :]).then_inc(stored, 16)
            pool.wait_ge(stored, 16 * (DEPTH * 10 + 3))
            for s, fills_ in zip(range(MOE_PAIRS, RING), surplus):
                pool.wait_ge(w_ready[s], fills_)

        @block.scalar
        def _(act):
            A = nc.scalar.activation
            act.dma_start(ln_rows[0:2 * KD, :], a["ln_attn"].rearrange("l (k p) -> (l k) p", p=P)).then_inc(loaded_ln, 16)
            act.dma_start(ln_rows[2 * KD:4 * KD, :], a["ln_ffn"].rearrange("l (k p) -> (l k) p", p=P)).then_inc(loaded_ln, 16)

            act.wait_ge(warm_set, 1)

            def split_hi(src, n, hi, size):
                A(hi[:, 0:size], src[:, 0:size], ACT.Copy).then_inc(hi_ready, 1)

            def dense_hi_part(n):
                key = DENSE[n]
                act.wait_ge(w_ready[slot_of[key]], ready_at[key])
                wait_pair(act, n)
                split_hi(ring[:, slot_of[key], :], n, w_hi[n % DENSE_PAIRS], dense_size(key))

            def moe_hi_part(j, u, first=False):
                s = u % RING
                if first:
                    act.wait_ge(w_ready[s], 16 * (base_fills[s] + u // RING + 1))
                else:
                    act.wait_ge(w_ready[s], j * (16 * per_expert) + 16 * (base_fills[s] + u // RING + 1))
                    if u - MOE_PAIRS < len(EXPERT) - 1:
                        act.wait_ge(pair_used, j * (len(EXPERT) - 1) + (DOWN_USED + u - MOE_PAIRS + 1))
                    else:
                        act.wait_ge(y_full, j + 1)
                split_hi(ring[:, s, :], u, w_hi[u % MOE_PAIRS], moe_size(u))

            def norm(l, w):
                A(warm[:, 0:1], warm[:, 0:1], ACT.Sqrt)
                for t in range(3):
                    r = ROWS[t]
                    if w == 0 and l == 0:
                        act.wait_ge(loaded_x, 16 * 3)
                        act.wait_ge(loaded_c, 16)
                    elif w == 1:
                        wait_out(act, ("ty", l, KD - 1))
                    else:
                        wait_out(act, ("tz", KD - 1))
                    A(xn[0:r, t, :], xres[0:r, t, :], ACT.Square, accum_out=ssx[0:r, t:t + 1]).then_inc(sumsq_x, 1)
                    act.wait_ge(sumsq_x, norm_no(l, w, t))
                    A(rtx[0:r, t:t + 1], ssx[0:r, t:t + 1], ACT.Sqrt, bias=C("eps", r), scale=1.0 / D).then_inc(root_x, 1)

            for l in range(DEPTH):
                norm(l, 0)
                for what, *n_ in FRONT:
                    if what == "zc":
                        t, = n_
                        r = ROWS[t]
                        wait_full(act, ("za", l, t))
                        za = pair(("za", l, t), r)
                        n = 3 * l + t
                        if n:
                            act.wait_ge(mean_z, n)
                        if l == 1 and t == 0:
                            act.wait_ge(stored, 16 * 10)
                        A(sq[0:r, 0:512], za[:, 0:512], ACT.Square)
                        A(sq[0:r, 512:S1], za[:, 512:S1], ACT.Square)
                        A(v_sb[0:r, t, :], za[:, S1:S2], ACT.Copy)
                        A(sq[0:r, S2:S3], za[:, S2:S3], ACT.Square)
                        wait_full(act, ("zc", l, t))
                        A(sq[0:r, S3:IN_W], pair(("zc", l, t), r)[:, 0:IN_W - S3], ACT.Square).then_inc(squares_z, 1)
                        act.wait_ge(mean_z, n + 1)
                        A(sr[0:r, 0:13], st[0:r, 0:13], ACT.Sqrt, bias=C("eps", r)).then_inc(root_z, 1)
                    elif what == "tc":
                        wait_full(act, ("tc", l))
                        pc = pair(("tc", l))
                        A(kTa[:, KOFF[2]:KOFF[2] + P], pc[:, 0:P], ACT.Copy)
                        free(A(ckvT[:, KOFF[2]:KOFF[2] + P], pc[:, P:2 * P], ACT.Copy), ("tc", l))
                    elif what == "tq":
                        t, = n_
                        r, k0 = ROWS[t], KOFF[KT_OF_TILE[t]]
                        wait_full(act, ("tq", l, t))
                        v = pair(("tq", l, t)).rearrange("p (i c) -> p i c", c=P)
                        A(qTa[:, :, TOFF[t]:TOFF[t] + r], v[:, 0:4, 0:r], ACT.Copy)
                        A(kTa[:, k0:k0 + r], v[:, 4, 0:r], ACT.Copy)
                        A(cqT[:, :, TOFF[t]:TOFF[t] + r], v[:, 5:7, 0:r], ACT.Copy)
                        free(A(ckvT[:, k0:k0 + r], v[:, 7, 0:r], ACT.Copy), ("tq", l, t))
                    elif what == "item":
                        i, = n_
                        kind, t = ITEMS[i]
                        r = ROWS[t] if kind == "q" else KROWS[t]
                        n = len(ITEMS) * l + i
                        wait_full(act, ("item", l, i))
                        v = pair(("item", l, i), r)
                        if n:
                            act.wait_ge(mean_i, n)
                        if kind == "q":
                            A(sqb[0:r, 0:512], v[:, 0:512], ACT.Square)
                            A(sqb[0:r, 512:768], v[:, 512:768], ACT.Square).then_inc(squares_i, 1)
                        else:
                            kv = v.rearrange("p (h c) -> p h c", h=HEADS)
                            A(vb[0:r, t, :].rearrange("p (h c) -> p h c", h=HEADS), kv[:, :, NOPE:NOPE + VD], ACT.Copy)
                            A(sqb[0:r, 0:512].rearrange("p (h c) -> p h c", h=HEADS), kv[:, :, 0:NOPE], ACT.Square)\
                                .then_inc(squares_i, 1)
                        act.wait_ge(mean_i, n + 1)
                        w = 16 if kind == "q" else 8
                        A(sr[0:r, 0:w], st[0:r, 0:w], ACT.Sqrt, bias=C("eps", r),
                          scale=1.0 if kind == "q" else 1.0 / NOPE).then_inc(root_i, 1)
                    elif what == "titem":
                        i, = n_
                        kind, t = ITEMS[i]
                        r = ROWS[t] if kind == "q" else KROWS[t]
                        wait_full(act, ("titem", l, i))
                        v = pair(("titem", l, i), QK).rearrange("p (h c) -> p h c", h=HEADS)[:, :, 0:r]
                        dst = qTb[0:QK, :, TOFF[t]:TOFF[t] + r] if kind == "q" else kTb[0:QK, :, KOFF[t]:KOFF[t] + r]
                        free(A(dst, v, ACT.Copy), ("titem", l, i))
                for g in range(STEPS):
                    if g < len(GROUPS):
                        typ, t, hg = GROUPS[g]
                        r = ROWS[t]
                        b = g % 2
                        nk = sum(KROWS[KEYS_OF[t][0]:KEYS_OF[t][1]])
                        act.wait_ge(negmax_ready, len(GROUPS) * l + g + 1)
                        if typ == "a":
                            A(es[0:r, b, :], dsk[0:r, b, :], ACT.Exp)
                        for h in range(4):
                            ins = A(sp_[0:r, b, h, 0:nk], sp_[0:r, b, h, 0:nk], ACT.Exp, bias=nb[0:r, b, h:h + 1],
                                    scale=A_SCALE if typ == "a" else B_SCALE, accum_out=rsum[0:r, b, h:h + 1])
                        ins.then_inc(exp_ready, 1)
                    if 1 <= g <= len(GROUPS):
                        typ, t, hg = GROUPS[g - 1]
                        r, b = ROWS[t], (g - 1) % 2
                        key = ("p", l, g - 1)
                        wait_full(act, key)
                        v = pair(key).rearrange("p (h k c) -> p h k c", h=4, k=2)
                        dst = pT[:, b].rearrange("p h (k c) -> p h k c", k=2)
                        if t == 0:
                            free(A(dst[:, :, 0, 0:r], v[:, :, 0, 0:r], ACT.Copy), key)
                        elif t == 1:
                            free(A(dst[:, :, :, 0:r], v[:, :, :, 0:r], ACT.Copy), key)
                        else:
                            A(dst[:, :, 0, 0:r], v[:, :, 0, 0:r], ACT.Copy)
                            free(A(dst[0:DEC, :, 1, 0:r], v[0:DEC, :, 1, 0:r], ACT.Copy), key)
                    if g in TO_STEP:
                        t = TO_STEP.index(g)
                        r = ROWS[t]
                        wait_full(act, ("to", l, t))
                        v = pair(("to", l, t)).rearrange("p (k c) -> p k c", k=KD)
                        free(A(hT[:, :, TOFF[t]:TOFF[t] + r], v[:, :, 0:r], ACT.Copy), ("to", l, t))
                for d in range(KD):
                    wait_full(act, ("wo", l, d))
                    if d >= 2:
                        wait_full(act, ("ty", l, d - 2))
                    free(A(yT[:, 0, d % 2, :], pair(("wo", l, d))[:, 0:TOK], ACT.Copy), ("wo", l, d))
                    if d == 0:
                        act.wait_ge(stored, 16 * 10 * (l + 1))
                    if d in SPLIT_AT and l == 0:
                        dense_hi_part(SPLIT_AT.index(d))
                    elif d in SPLIT_AT:
                        moe_hi_part(0, SPLIT_AT.index(d), first=True)
                norm(l, 1)
                if l == 1:
                    for u in range(3, MOE_PAIRS):
                        moe_hi_part(0, u, first=True)
                if l == 0:
                    wait_full(act, ("hf", 0, 2))
                    for t in range(3):
                        wait_out(act, ("hf", 0, t))
                        A(hT_hi[:, :, TOFF[t]:TOFF[t] + ROWS[t]], hT[:, :, TOFF[t]:TOFF[t] + ROWS[t]], ACT.Copy).then_inc(tok_hi, 1)

                    def activations(i):
                        b = i % 2
                        wait_full(act, ("gate", i))
                        if i >= 2:
                            wait_out(act, ("up", i - 2))
                        g = pair(("gate", i)).rearrange("p (f c) -> p f c", f=2)[:, :, 0:TOK]
                        free(A(sg[:, b, :, :], g, ACT.Silu), ("gate", i))

                    def act_high(i):
                        wait_out(act, ("up", i))
                        A(aT_hi[:, 2 * i:2 * i + 2, :], aa[:, i % 2, :, :], ACT.Copy).then_inc(dense_hi, 1)

                    def down_out(c):
                        for h in range(2):
                            wait_full(act, ("dn", c, h))
                            wait_full(act, ("tz", 2 * h + 1) if c else ("ty", 0, KD - 1))
                            v = pair(("dn", c, h)).rearrange("p (f c) -> p f c", f=2)[:, :, 0:TOK]
                            free(A(yT[:, h, :, :], v, ACT.Copy), ("dn", c, h))

                    for n in range(DENSE_PAIRS, ND):
                        if n % 2 == 1 and 0 <= n // 2 - 2 < DCH:
                            act_high(n // 2 - 2)
                        if n % 2 == 1 and n // 2 - 1 < DCH:
                            activations(n // 2 - 1)
                        if n == DENSE.index(("down", 0, 5)) + DENSE_PAIRS:
                            down_out(0)
                        dense_hi_part(n)
                    down_out(1)

            for t in range(3):
                act.wait_ge(xn_ready, norm_no(1, 1, t))
                wait_full(act, ("hf", 1, t))
                A(xn_hi[0:ROWS[t], t, :], xn[0:ROWS[t], t, :], ACT.Copy).then_inc(tok_hi, 1)

            act.wait_ge(pair_diff, 1)
            A(dlt[:, :, 1:2], dlt[:, :, 0:1], ACT.Exp).then_inc(pair_exp, 1)
            act.wait_ge(plan_ready, 1)
            rounds = act.value_load(nround[0:1, 0:1], min_val=1, max_val=ROUNDS)

            def tokens_high(count):
                act.wait_ge(xg_rows, count)
                A(xg_hi[:, :, :], xg[:, :, :], ACT.Copy).then_inc(xg_high, 1)

            tokens_high(1)
            with act.Fori(0, rounds) as r_:
                with act.Fori(0, NE) as e:
                    j = act.snap(r_ * NE + e)

                    A(warm[:, 0:1], warm[:, 0:1], ACT.Silu)

                    def silu(c):
                        q = c % 2
                        act.wait_ge(gu_full[q], j * 3 + (c // 2 + 1))
                        A(sgm[:, q, 0:WIDTH[c]], ps[:, 2 * (1 - q), 0:WIDTH[c]], ACT.Silu).then_inc(silu_done, 1)

                    def chunk_high(c):
                        b, w = c % 2, WIDTH[c] // P
                        act.wait_ge(aT_full, j * CHUNKS + (c + 1))
                        A(am_hi[:, b, 0:w, :], ps[:, 5 if b == 0 else 4, 0:w * P].rearrange("p (k c) -> p k c", k=w),
                          ACT.Copy).then_inc(aT_high, 1)

                    def output_high():
                        act.wait_ge(pickT_free, j + 1)
                        act.wait_ge(y_full, j + 1)
                        A(y_hi[:, :], ps[:, 6:8, :].rearrange("p a c -> p (a c)"), ACT.Copy, scale=gslot[:, 0:1]).then_inc(y_high, 1)

                    for u in range(MOE_PAIRS, len(EXPERT) + MOE_PAIRS):
                        for what, c in MOE_EVENTS.get(u, ()):
                            if what == "act":
                                silu(c)
                            elif what == "turned":
                                chunk_high(c)
                            elif what == "tokens":
                                tokens_high(j + 2)
                            elif what == "output":
                                output_high()
                        moe_hi_part(j, u)

        @block.vector
        def _(dve):
            V = nc.vector
            steps = [0]

            V.memset(warm[:, :], 0.0).then_inc(warm_set, 1)

            def link(ins):
                steps[0] += 1
                ins.then_inc(dve_step, 1)
                dve.wait_ge(dve_step, steps[0])

            dve.wait_ge(ln_done, 1)
            V.tensor_copy(ln_cols[:, :], ps[:, 0, 0:4 * KD]).then_inc(ln_evac, 1)
            dve.wait_ge(ln_evac, 1)

            def split_lo(src, n_done, hi, lo, size):
                dve.wait_ge(hi_ready, n_done)
                V.tensor_tensor(lo[:, 0:size], src[:, 0:size], hi[:, 0:size].bitcast(F32), ALU.subtract).then_inc(lo_ready, 1)

            def dense_lo_part(n):
                key = DENSE[n]
                split_lo(ring[:, slot_of[key], :], n + 1, w_hi[n % DENSE_PAIRS], w_lo[n % DENSE_PAIRS], dense_size(key))

            def moe_lo_part(j, u, first=False):
                q = u % MOE_PAIRS
                done = ND + u + 1 if first else j * len(EXPERT) + (ND + u + 1)
                split_lo(ring[:, u % RING, :], done, w_hi[q], w_lo[q], moe_size(u))

            def norm(l, w):
                for t in range(3):
                    r = ROWS[t]
                    dve.wait_ge(root_x, norm_no(l, w, t))
                    link(V.reciprocal(rsx[0:r, t:t + 1], rtx[0:r, t:t + 1]))
                    V.tensor_scalar(xn[0:r, t, :], xres[0:r, t, :], rsx[0:r, t:t + 1], None, ALU.mult).then_inc(xn_ready, 1)
                for t in range(3):
                    r = ROWS[t]
                    key = ("hf" if w else "h", l, t)
                    wait_full(dve, key)
                    c0 = KD * (2 * w + l)
                    v = pair(key).rearrange("p (k c) -> p k c", k=KD)[:, :, 0:r]
                    free(V.tensor_tensor(hT[:, :, TOFF[t]:TOFF[t] + r], v, bc(ln_cols[:, c0:c0 + KD], r), ALU.mult), key)

            def rotate(dst, src, name, l, t, heads, t1, t2, perm=False):
                rc, rsn, w = rot[name]
                r, cls, hw = ROWS[t], min(t, 1), w // 2
                x = src.rearrange("p (h w) -> p h w", h=heads) if len(src.shape) == 2 else src
                u = t1[0:r, 0:heads * w].rearrange("p (h w) -> p h w", h=heads)
                v = t2[0:r, 0:heads * w].rearrange("p (h w) -> p h w", h=heads)
                V.tensor_tensor(u, x, bh(rc[0:r, cls, :], heads), ALU.mult)
                V.tensor_tensor(v[:, :, 0:hw], x[:, :, hw:w], bh(rsn[0:r, cls, 0:hw], heads), ALU.mult)
                link(V.tensor_tensor(v[:, :, hw:w], x[:, :, 0:hw], bh(rsn[0:r, cls, hw:w], heads), ALU.mult))
                if perm:
                    u = u.rearrange("p (g i) w -> p g i w", g=KVH)
                    v = v.rearrange("p (g i) w -> p g i w", g=KVH)
                    dst = dst.rearrange("p (i g w) -> p g i w", g=KVH, i=GRP)
                    for g in range(KVH):
                        ins = V.tensor_tensor(dst[:, g], u[:, g], v[:, g], ALU.add)
                    return ins
                return V.tensor_tensor(dst, u, v, ALU.add)

            for l in range(DEPTH):
                norm(l, 0)
                dve.wait_ge(rot_ready, 4 * (l + 1))
                for what, *n_ in FRONT:
                    if what == "zc":
                        t, = n_
                        r = ROWS[t]
                        dve.wait_ge(squares_z, 3 * l + t + 1)
                        V.reduce_sum(st[0:r, 0:10], sq[0:r, 0:S1].rearrange("p (h w) -> p h w", w=HD), AX_X)
                        V.reduce_sum(st[0:r, 10:11], sq[0:r, S2:S3], AX_X)
                        V.reduce_sum(st[0:r, 11:12], sq[0:r, S3:S4], AX_X)
                        link(V.reduce_sum(st[0:r, 12:13], sq[0:r, S4:IN_W], AX_X))
                        V.tensor_tensor(st[0:r, 0:13], st[0:r, 0:13], C("inv_a", r), ALU.mult).then_inc(mean_z, 1)
                        dve.wait_ge(root_z, 3 * l + t + 1)
                        link(V.reciprocal(rs[0:r, 0:13], sr[0:r, 0:13]))
                        za, zc = pair(("za", l, t), r), pair(("zc", l, t), r)
                        if t == 2:
                            wait_full(dve, ("tq", l, 0))
                        if t == 0 and l == 1:
                            dve.wait_ge(stored, 16 * 10)
                        V.tensor_tensor(tmp0[0:r, :].rearrange("p (h w) -> p h w", w=HD), za[:, 0:S1].rearrange("p (h w) -> p h w", w=HD),
                                        bc(rs[0:r, 0:10], HD), ALU.mult)
                        free(V.scalar_tensor_tensor(out=cqn[0:r, t % 2, :], in0=za[:, S2:S3], scalar=rs[0:r, 10:11],
                                                    in1=G("b_cq_norm", l, r), op0=ALU.mult, op1=ALU.mult), ("za", l, t))
                        V.scalar_tensor_tensor(out=ckv[0:r, t, :], in0=zc[:, 0:KL], scalar=rs[0:r, 11:12],
                                               in1=G("b_ckv_norm", l, r), op0=ALU.mult, op1=ALU.mult)
                        free(V.tensor_scalar(rt0[0:r, 0:ROPE], zc[:, KL:KL + ROPE], rs[0:r, 12:13], None, ALU.mult), ("zc", l, t))
                        wait_out(dve, ("zc", l, t))
                        rotate(qa[0:r, t % 2, :], tmp0[0:r, 0:S0], "a_q_norm", l, t, HEADS, tmp1, tmp2, perm=True)
                        rotate(ka[0:r, t, :].rearrange("p (h w) -> p h w", h=KVH), tmp0[0:r, S0:S1], "a_k_norm", l, t, KVH,
                               tmp1[:, S0:S1], tmp2[:, S0:S1])
                        rotate(kr[0:r, t, :].rearrange("p (h w) -> p h w", h=1), rt0[0:r, 0:ROPE], "b_kr_norm", l, t, 1,
                               rt1, rt2).then_inc(rows_ready, 1)
                    elif what == "item":
                        i, = n_
                        kind, t = ITEMS[i]
                        r = ROWS[t] if kind == "q" else KROWS[t]
                        n = len(ITEMS) * l + i
                        v = pair(("item", l, i), r)
                        dve.wait_ge(squares_i, n + 1)
                        if kind == "q":
                            s3 = sqb[0:r, :].rearrange("p (h w) -> p h w", h=HEADS)
                            V.reduce_sum(st[0:r, 0:8], s3[:, :, 0:NOPE], AX_X)
                            link(V.reduce_sum(st[0:r, 8:16], s3[:, :, NOPE:QK], AX_X))
                            V.tensor_tensor(st[0:r, :], st[0:r, :], C("inv_b", r), ALU.mult).then_inc(mean_i, 1)
                        else:
                            V.reduce_sum(st[0:r, 0:8], sqb[0:r, 0:512].rearrange("p (h w) -> p h w", h=HEADS), AX_X).then_inc(mean_i, 1)
                        dve.wait_ge(root_i, n + 1)
                        w = 16 if kind == "q" else 8
                        link(V.reciprocal(rs[0:r, 0:w], sr[0:r, 0:w]))
                        if i >= 2:
                            wait_full(dve, ("titem", l, i - 2))
                        dst = qkb[0:r, i % 2, :].rearrange("p (h w) -> p h w", h=HEADS)
                        nope = tmp0[0:r, 0:512].rearrange("p (h w) -> p h w", h=HEADS)
                        if kind == "q":
                            x = v[:, 0:768].rearrange("p (h w) -> p h w", h=HEADS)
                            xr = rt0[0:r, :].rearrange("p (h w) -> p h w", h=HEADS)
                            V.tensor_tensor(nope, x[:, :, 0:NOPE], bc(rs[0:r, 0:8], NOPE), ALU.mult)
                            free(V.tensor_tensor(xr, x[:, :, NOPE:QK], bc(rs[0:r, 8:16], ROPE), ALU.mult), ("item", l, i))
                            wait_out(dve, ("item", l, i))
                            V.tensor_tensor(dst[:, :, 0:NOPE], nope, bh(G("b_qn_norm", l, r), HEADS), ALU.mult)
                            rotate(dst[:, :, NOPE:QK], rt0[0:r, :], "b_qr_norm", l, t, HEADS, rt1, rt2).then_inc(item_ready, 1)
                        else:
                            x = v.rearrange("p (h w) -> p h w", h=HEADS)
                            free(V.tensor_tensor(nope, x[:, :, 0:NOPE], bc(rs[0:r, 0:8], NOPE), ALU.mult), ("item", l, i))
                            wait_out(dve, ("item", l, i))
                            V.tensor_tensor(dst[:, :, 0:NOPE], nope, bh(G("b_kn_norm", l, r), HEADS), ALU.mult)
                            if t == 2:
                                dve.wait_ge(loaded_cache, CACHES_IN)
                            own = krc[:, l, :] if t == 2 else kr[0:r, min(t, 2), :]
                            V.tensor_copy(dst[:, :, NOPE:QK], bh(own, HEADS)).then_inc(item_ready, 1)
                for g in range(STEPS):
                    if g < len(GROUPS):
                        typ, t, hg = GROUPS[g]
                        r, b = ROWS[t], g % 2
                        nk = sum(KROWS[KEYS_OF[t][0]:KEYS_OF[t][1]])
                        key = ("s", l, g)
                        wait_full(dve, key)
                        if g >= 2:
                            wait_full(dve, ("p", l, g - 2))
                        src = pair(key, r).rearrange("p (h c) -> p h c", h=4)[:, :, 0:nk]
                        dst = sp_[0:r, b, :, 0:nk]
                        if t == 2:
                            free(V.tensor_copy(dst, src), key)
                        else:
                            m = C("mask0" if t == 0 else "mask1" + typ, r)
                            free(V.tensor_tensor(dst, src, bh(m, 4), ALU.add), key)
                        wait_out(dve, key)
                        link(V.reduce_max(mx[0:r, b, :], dst, AX_X))
                        if typ == "a":
                            sink = G("a_sinks", l, r)[:, 4 * hg:4 * hg + 4]
                            link(V.scalar_tensor_tensor(out=mm[0:r, b, :], in0=mx[0:r, b, :], scalar=A_SCALE, in1=sink,
                                                        op0=ALU.mult, op1=ALU.max))
                            V.tensor_scalar(nb[0:r, b, :], mm[0:r, b, :], -1.0, None, ALU.mult)
                            V.tensor_tensor(dsk[0:r, b, :], sink, mm[0:r, b, :], ALU.subtract).then_inc(negmax_ready, 1)
                        else:
                            V.tensor_scalar(nb[0:r, b, :], mx[0:r, b, :], -B_SCALE, None, ALU.mult).then_inc(negmax_ready, 1)
                    if 1 <= g <= len(GROUPS):
                        typ, t, hg = GROUPS[g - 1]
                        r, b = ROWS[t], (g - 1) % 2
                        dve.wait_ge(exp_ready, len(GROUPS) * l + g)
                        if typ == "a":
                            link(V.tensor_tensor(den[0:r, b, :], rsum[0:r, b, :], es[0:r, b, :], ALU.add))
                            link(V.reciprocal(rden[0:r, b, :], den[0:r, b, :]))
                        else:
                            link(V.reciprocal(rden[0:r, b, :], rsum[0:r, b, :]))
                    if g >= 2:
                        typ, t, hg = GROUPS[g - 2]
                        r, b = ROWS[t], (g - 2) % 2
                        key = ("o", l, g - 2)
                        wait_full(dve, key)
                        c0 = (typ == "b") * 512 + hg * 256
                        free(V.tensor_tensor(xn[0:r, t, c0:c0 + 256].rearrange("p (h w) -> p h w", h=4),
                                             pair(key, r)[:, 0:256].rearrange("p (h w) -> p h w", h=4),
                                             bc(rden[0:r, b, :], HD), ALU.mult), key)
                        wait_out(dve, key)

                def add_rows(key, d):
                    wait_full(dve, key)
                    v = pair(key).rearrange("p (t c) -> p t c", c=P)
                    V.tensor_tensor(xres[:, 0:2, d * P:(d + 1) * P], xres[:, 0:2, d * P:(d + 1) * P], v[:, 0:2, :], ALU.add)
                    free(V.tensor_tensor(xres[0:DEC, 2, d * P:(d + 1) * P], xres[0:DEC, 2, d * P:(d + 1) * P],
                                         v[0:DEC, 2, :], ALU.add), key)

                for d in range(KD):
                    add_rows(("ty", l, d), d)
                    if l == 1 and d == 4:
                        dve.wait_ge(stored, 16 * 20)
                        V.memset(y_hi[:, :].bitcast(F32), 0.0)
                        V.memset(y_lo[:, :].bitcast(F32), 0.0)
                        V.memset(pickT[:, :].bitcast(F32), 0.0).then_inc(y_free, 1)
                        V.memset(possel[:, :, NJ:NJ + 1], -ABSENT)
                        V.memset(lg[:, :, :], 0.0)
                        link(V.memset(gate[:, :, NJ:NJ + 1], 0.0))
                    if d in SPLIT_AT and l == 0:
                        dense_lo_part(SPLIT_AT.index(d))
                    elif d in SPLIT_AT:
                        moe_lo_part(0, SPLIT_AT.index(d), first=True)
                norm(l, 1)
                if l == 0:
                    for t in range(3):
                        c0, c1 = TOFF[t], TOFF[t] + ROWS[t]
                        dve.wait_ge(tok_hi, t + 1)
                        V.tensor_tensor(hT_lo[:, :, c0:c1], hT[:, :, c0:c1], hT_hi[:, :, c0:c1].bitcast(F32), ALU.subtract)\
                            .then_inc(tok_ready, 1)

                    def activations(i):
                        b = i % 2
                        if i >= 2:
                            dve.wait_ge(dense_act, i - 1)
                        wait_out(dve, ("gate", i))
                        wait_full(dve, ("up", i))
                        u = pair(("up", i)).rearrange("p (f c) -> p f c", f=2)[:, :, 0:TOK]
                        free(V.tensor_tensor(aa[:, b, :, :], sg[:, b, :, :], u, ALU.mult), ("up", i))

                    def act_low(i):
                        dve.wait_ge(dense_hi, i + 1)
                        V.tensor_tensor(aT_lo[:, 2 * i:2 * i + 2, :], aa[:, i % 2, :, :], aT_hi[:, 2 * i:2 * i + 2, :].bitcast(F32),
                                        ALU.subtract).then_inc(dense_act, 1)

                    for n in range(DENSE_PAIRS, ND):
                        if n % 2 == 0 and n // 2 - 2 < DCH:
                            activations(n // 2 - 2)
                        if n % 2 == 0 and 0 <= n // 2 - 3 < DCH:
                            act_low(n // 2 - 3)
                        if n == DENSE.index(("down", 0, 5)) + DENSE_PAIRS:
                            for d in range(4):
                                add_rows(("tz", d), d)
                        dense_lo_part(n)
                    for d in range(4, KD):
                        add_rows(("tz", d), d)

            for t in range(3):
                r = ROWS[t]
                dve.wait_ge(tok_hi, 3 + t + 1)
                V.tensor_tensor(xn_lo[0:r, t, :], xn[0:r, t, :], xn_hi[0:r, t, :].bitcast(F32), ALU.subtract).then_inc(tok_ready, 1)
            for u in range(3, MOE_PAIRS):
                moe_lo_part(0, u, first=True)
            wait_full(dve, ("router",))
            lp = pair(("router",))
            V.tensor_copy(lg[:, 0:2, :], lp[:, 0:2 * NE].rearrange("p (t e) -> p t e", e=NE))
            free(V.tensor_copy(lg[0:DEC, 2, :], lp[0:DEC, 2 * NE:3 * NE]), ("router",))
            wait_out(dve, ("router",))
            for t in range(3):
                ins = V.max(mx8[:, t, :], lg[:, t, :])
            link(ins)
            for t in range(3):
                ins = V.max_index(idx8[:, t, :], mx8[:, t, :], lg[:, t, :])
            link(ins)
            link(V.tensor_copy(idf[:, :, :], idx8[:, :, :]))
            iota8 = bh(C("iota")[:, 0:NE], 3)
            V.tensor_tensor(oh1[:, :, :], iota8, idf[:, :, 0:1].to_broadcast([P, 3, NE]), ALU.is_equal)
            link(V.tensor_tensor(oh2[:, :, :], iota8, idf[:, :, 1:2].to_broadcast([P, 3, NE]), ALU.is_equal))
            V.tensor_tensor(member[:, :, :], oh1[:, :, :], oh2[:, :, :], ALU.add)
            V.tensor_tensor(dlt[:, :, 0:1], mx8[:, :, 1:2], mx8[:, :, 0:1], ALU.subtract).then_inc(pair_diff, 1)
            dve.wait_ge(pair_exp, 1)
            link(V.tensor_scalar(dlt[:, :, 2:3], dlt[:, :, 1:2], 1.0, None, ALU.add))
            link(V.reciprocal(dlt[:, :, 2:3], dlt[:, :, 2:3]))
            V.tensor_tensor(goh[:, :, :], oh1[:, :, :], dlt[:, :, 2:3].to_broadcast([P, 3, NE]), ALU.mult)
            link(V.tensor_tensor(dlt[:, :, 3:4], dlt[:, :, 1:2], dlt[:, :, 2:3], ALU.mult))
            link(V.tensor_tensor(gtmp[:, :, :], oh2[:, :, :], dlt[:, :, 3:4].to_broadcast([P, 3, NE]), ALU.mult))
            for q in range(ROUNDS):
                V.tensor_tensor(gate[:, :, NE * q:NE * q + NE], goh[:, :, :], gtmp[:, :, :], ALU.add)
            wait_full(dve, ("pos",))
            pp = pair(("pos",))
            for q in range(ROUNDS):
                off = ABSENT - SLOTS * q
                V.scalar_tensor_tensor(out=posn[:, 0:2, NE * q:NE * q + NE], in0=pp[:, 0:2 * NE].rearrange("p (t e) -> p t e", e=NE),
                                       scalar=off, in1=member[:, 0:2, :], op0=ALU.add, op1=ALU.mult)
                ins = V.scalar_tensor_tensor(out=posn[0:DEC, 2, NE * q:NE * q + NE], in0=pp[0:DEC, 2 * NE:3 * NE],
                                             scalar=off, in1=member[0:DEC, 2, :], op0=ALU.add, op1=ALU.mult)
            link(ins)
            V.tensor_scalar(possel[:, 0:2, 0:NJ], posn[:, 0:2, :], -ABSENT, None, ALU.add)
            V.tensor_scalar(possel[0:DEC, 2, 0:NJ], posn[0:DEC, 2, :], -ABSENT, None, ALU.add)
            link(V.tensor_copy(cnt[0:1, 0:8], pp[0:1, NE * 3:NE * 4]))
            link(V.reduce_max(cnt[0:1, 8:9], cnt[0:1, 0:8], AX_X))
            V.tensor_scalar(cnt[0:1, 9:10], cnt[0:1, 8:9], SLOTS + 0.5, None, ALU.is_gt)
            link(V.tensor_scalar(cnt[0:1, 10:11], cnt[0:1, 8:9], 2 * SLOTS + 0.5, 1.0, ALU.is_gt, ALU.add))
            V.tensor_tensor(nround[:, :], cnt[0:1, 9:10], cnt[0:1, 10:11], ALU.add).then_inc(plan_ready, 1)
            dve.wait_ge(plan_ready, 1)

            rounds = dve.value_load(nround[0:1, 0:1], min_val=1, max_val=ROUNDS)

            def picks(col):
                for t in range(3):
                    r = ROWS[t]
                    V.tensor_copy(gcol[0:r, t:t + 1], gate[0:r, t, col])
                for t in range(3):
                    r = ROWS[t]
                    ins = V.tensor_scalar(pick[0:r, t, :], C("iota", r), possel[0:r, t, col], None, ALU.is_equal)
                ins.then_inc(pick_ready, 1)

            def tokens(count):
                dve.wait_ge(gathered, count)
                c0 = KD * 3
                V.tensor_tensor(xg[:, :, :], ps[:, 0:2, :].rearrange("p a (k c) -> p (a k) c", c=P),
                                bc(ln_cols[:, c0:c0 + KD], SLOTS), ALU.mult).then_inc(xg_rows, 1)
                dve.wait_ge(xg_high, count)
                V.tensor_tensor(xg_lo[:, :, :], xg[:, :, :], xg_hi[:, :, :].bitcast(F32), ALU.subtract).then_inc(xg_ready, 1)

            def add_tile(t, banks):
                r = ROWS[t]
                return V.tensor_tensor(xres[0:r, t, :], xres[0:r, t, :], ps[0:r, banks:banks + 2, :].rearrange("p a c -> p (a c)"), ALU.add)

            picks(slice(0, 1))
            tokens(1)
            with dve.Fori(0, rounds) as r_:
                with dve.Fori(0, NE) as e:
                    j = dve.snap(r_ * NE + e)

                    def activations(c):
                        q = c % 2
                        dve.wait_ge(silu_done, j * CHUNKS + (c + 1))
                        V.tensor_tensor(act_m[:, q, 0:WIDTH[c]], sgm[:, q, 0:WIDTH[c]], ps[:, 2 * (1 - q) + 1, 0:WIDTH[c]],
                                        ALU.mult).then_inc(gu_free[q], 1)

                    def chunk_low(c):
                        b, w = c % 2, WIDTH[c] // P
                        dve.wait_ge(aT_high, j * CHUNKS + (c + 1))
                        V.tensor_tensor(am_lo[:, b, 0:w, :], ps[:, 5 if b == 0 else 4, 0:w * P].rearrange("p (k c) -> p k c", k=w),
                                        am_hi[:, b, 0:w, :].bitcast(F32), ALU.subtract).then_inc(aT_free, 1)

                    def scatter(t):
                        dve.wait_ge(sc_full, j * 3 + (t + 1))
                        add_tile(t, SC_BANKS[t]).then_inc(sc_free, 1)

                    def slots():
                        dve.wait_ge(pickT_full, j + 1)
                        V.tensor_copy(gslot[:, :], ps[:, 4, TOK:TOK + 1])
                        V.tensor_copy(pickT[:, :], ps[:, 4, 0:TOK]).then_inc(pickT_free, 1)

                    def output_low():
                        dve.wait_ge(y_high, j + 1)
                        V.scalar_tensor_tensor(out=y_lo[:, :], in0=ps[:, 6:8, :].rearrange("p a c -> p (a c)"), scalar=gslot[:, 0:1],
                                               in1=y_hi[:, :].bitcast(F32), op0=ALU.mult, op1=ALU.subtract).then_inc(y_free, 1)

                    for u in range(MOE_PAIRS, len(EXPERT) + MOE_PAIRS):
                        for what, c in MOE_EVENTS.get(u, ()):
                            if what == "act":
                                activations(c)
                            elif what == "turned":
                                chunk_low(c)
                            elif what == "scatter":
                                scatter(c)
                            elif what == "slots":
                                slots()
                            elif what == "picks":
                                picks(bass.ds(j + 1, 1))
                            elif what == "tokens":
                                tokens(j + 2)
                            elif what == "output":
                                output_low()
                        moe_lo_part(j, u)
            for t in range(3):
                dve.wait_ge(last_full, t + 1)
                add_tile(t, SC_BANKS[t]).then_inc(moe_done, 1)

        @block.tensor
        def _(pe):
            mm_ = nc.tensor.matmul
            tr = nc.tensor.transpose
            seen = set()

            def weights(key):
                if key not in seen:
                    seen.add(key)
                    pe.wait_ge(w_ready[slot_of[key]], ready_at[key])

            def used_up(ins, key):
                ins.then_inc(w_used[slot_of[key]], 1)

            pe.wait_ge(loaded_c, 16)
            pe.wait_ge(loaded_ln, 32)
            ident = C("ident")
            tr(ps[:, 0, 0:4 * KD], ln_rows[:, :], ident[0:4 * KD, 0:4 * KD]).then_inc(ln_done, 1)
            pe.wait_ge(ln_evac, 1)

            def turn(key, src, rows):
                wait_room(pe, key)
                v = pair(key)
                for k in range(KD):
                    ins = tr(v[:, k * P:k * P + rows], src[0:rows, k * P:(k + 1) * P], ident[0:rows, 0:rows])
                full(ins, key)

            def turn_back(key, src_T, src, last_of=None):
                wait_room(pe, key)
                wait_out(pe, src)
                v = pair(key)
                for t in range(3):
                    ins = tr(v[0:ROWS[t], t * P:(t + 1) * P], src_T[:, TOFF[t]:TOFF[t] + ROWS[t]], ident)
                    if t == 0 and last_of:
                        used_up(ins, last_of)
                full(ins, key)

            for l in range(DEPTH):
                for t in range(3):
                    pe.wait_ge(xn_ready, norm_no(l, 0, t))
                    turn(("h", l, t), xn[:, t, :], ROWS[t])
                for what, *n_ in FRONT:
                    if what == "za":
                        t, = n_
                        r = ROWS[t]
                        wait_out(pe, ("h", l, t))
                        key = ("za", l, t)
                        wait_room(pe, key)
                        v = pair(key, r)
                        for c in range(2):
                            for k in range(KD):
                                wk = ("in", l, c, k // 4)
                                weights(wk)
                                ins = mm_(v[:, 512 * c:512 * c + 512], hT[:, k, TOFF[t]:TOFF[t] + r], slot(wk, 4, 512)[:, k % 4, :],
                                          start=(k == 0), stop=(k == KD - 1))
                                if t == 2 and k % 4 == 3 and not (c == 1 and k == KD - 1):
                                    used_up(ins, wk)
                        full(ins, key)
                    elif what == "zc":
                        t, = n_
                        r = ROWS[t]
                        key = ("zc", l, t)
                        wait_room(pe, key)
                        wk = ("in", l, 2, 0)
                        weights(wk)
                        for k in range(KD):
                            ins = mm_(pair(key, r)[:, 0:IN_W - S3], hT[:, k, TOFF[t]:TOFF[t] + r], slot(wk, 8, IN_W - S3)[:, k, :],
                                      start=(k == 0), stop=(k == KD - 1))
                        full(ins, key)
                    elif what == "tc":
                        key = ("tc", l)
                        wait_room(pe, key)
                        pe.wait_ge(loaded_cache, CACHES_IN)
                        v = pair(key)
                        tr(v[:, 0:P], kc[:, l, :], ident)
                        ins = tr(v[:, P:2 * P], ckvc[:, l, :], ident)
                        full(ins, key)
                    elif what == "tq":
                        t, = n_
                        r = ROWS[t]
                        key = ("tq", l, t)
                        pe.wait_ge(rows_ready, 3 * l + t + 1)
                        wait_room(pe, key)
                        v = pair(key)
                        for i in range(4):
                            ins = tr(v[:, i * P:i * P + r], qa[0:r, t % 2, i * P:(i + 1) * P], ident[0:r, 0:r])
                            if t == 1 and i == 0:
                                used_up(ins, ("in", l, 1, 1))
                            elif t == 2 and i == 0:
                                used_up(ins, ("in", l, 2, 0))
                        tr(v[:, 4 * P:4 * P + r], ka[0:r, t, :], ident[0:r, 0:r])
                        for i in range(2):
                            tr(v[:, (5 + i) * P:(5 + i) * P + r], cqn[0:r, t % 2, i * P:(i + 1) * P], ident[0:r, 0:r])
                        full(tr(v[:, 7 * P:7 * P + r], ckv[0:r, t, :], ident[0:r, 0:r]), key)
                    elif what == "item":
                        i, = n_
                        kind, t = ITEMS[i]
                        key = ("item", l, i)
                        if kind == "k" and t == 2:
                            wait_out(pe, ("tc", l))
                        else:
                            wait_out(pe, ("tq", l, t if kind == "q" else min(t, 2)))
                        wait_room(pe, key)
                        if kind == "q":
                            weights(("uq", l))
                            r = ROWS[t]
                            for c0, w in ((0, 512), (512, 256)):
                                for k in range(2):
                                    ins = mm_(pair(key, r)[:, c0:c0 + w], cqT[:, k, TOFF[t]:TOFF[t] + r],
                                              slot(("uq", l), 2, 768)[:, k, c0:c0 + w], start=(k == 0), stop=(k == 1))
                        else:
                            if i == 0:
                                pe.wait_ge(ukv_ready, 16 * (l + 1))
                            r = KROWS[t]
                            for c0 in (0, 512):
                                ins = mm_(pair(key, r)[:, c0:c0 + 512], ckvT[:, KOFF[t]:KOFF[t] + r],
                                          w_ukv[:, c0:c0 + 512], start=True, stop=True)
                        full(ins, key)
                    else:
                        i, = n_
                        kind, t = ITEMS[i]
                        r = ROWS[t] if kind == "q" else KROWS[t]
                        key = ("titem", l, i)
                        pe.wait_ge(item_ready, len(ITEMS) * l + i + 1)
                        wait_room(pe, key)
                        for h in range(HEADS):
                            ins = tr(pair(key, QK)[:, h * P:h * P + r], qkb[0:r, i % 2, h * QK:(h + 1) * QK], ident[0:r, 0:r])
                            if i == len(ITEMS) - 1 and h == 0:
                                used_up(ins, ("uq", l))
                        full(ins, key)
                for g in range(STEPS):
                    if g < len(GROUPS):
                        typ, t, hg = GROUPS[g]
                        r = ROWS[t]
                        k0 = KOFF[KEYS_OF[t][0]]
                        nk = sum(KROWS[KEYS_OF[t][0]:KEYS_OF[t][1]])
                        key = ("s", l, g)
                        if g == 0:
                            for n in range(3):
                                wait_out(pe, ("tq", l, n))
                        for n in NEEDS.get(g, ()):
                            wait_out(pe, ("titem", l, n))
                        wait_room(pe, key)
                        v = pair(key, r)
                        for h4 in range(4):
                            if typ == "a":
                                q, kk = qTa[64 * hg:64 * hg + 64, h4, TOFF[t]:TOFF[t] + r], kTa[64 * hg:64 * hg + 64, k0:k0 + nk]
                            else:
                                h = 4 * hg + h4
                                q, kk = qTb[0:QK, h, TOFF[t]:TOFF[t] + r], kTb[0:QK, h, k0:k0 + nk]
                            ins = mm_(v[:, 256 * h4:256 * h4 + nk], q, kk, start=True, stop=True)
                        full(ins, key)
                    if 1 <= g <= len(GROUPS):
                        typ, t, hg = GROUPS[g - 1]
                        r, b = ROWS[t], (g - 1) % 2
                        key = ("p", l, g - 1)
                        pe.wait_ge(exp_ready, len(GROUPS) * l + g)
                        wait_room(pe, key)
                        v = pair(key).rearrange("p (h k c) -> p h k c", h=4, k=2)
                        for h4 in range(4):
                            for k, kt in enumerate(range(*KEYS_OF[t])):
                                kr_ = KROWS[kt]
                                ins = tr(v[0:kr_, h4, k, 0:r], sp_[0:r, b, h4, P * k:P * k + kr_], ident[0:r, 0:r])
                        full(ins, key)
                    if g >= 2:
                        typ, t, hg = GROUPS[g - 2]
                        r, b = ROWS[t], (g - 2) % 2
                        key = ("o", l, g - 2)
                        wait_out(pe, ("p", l, g - 2))
                        wait_room(pe, key)
                        kts = list(range(*KEYS_OF[t]))
                        for h4 in range(4):
                            for k, kt in enumerate(kts):
                                kr_ = KROWS[kt]
                                if typ == "b":
                                    h = 4 * hg + h4
                                    val = vb[0:kr_, kt, h * VD:(h + 1) * VD]
                                elif kt == 2:
                                    val = vc[:, l, 64 * hg:64 * hg + 64]
                                else:
                                    val = v_sb[0:kr_, min(kt, 2), 64 * hg:64 * hg + 64]
                                ins = mm_(pair(key, r)[:, 64 * h4:64 * h4 + 64], pT[0:kr_, b, h4, P * k:P * k + r], val,
                                          start=(k == 0), stop=(k == len(kts) - 1))
                        full(ins, key)
                    if g in TO_STEP:
                        t = TO_STEP.index(g)
                        for n, (_, tile, _) in enumerate(GROUPS):
                            if tile == t:
                                wait_out(pe, ("o", l, n))
                        turn(("to", l, t), xn[:, t, :], ROWS[t])
                for t in range(3):
                    wait_out(pe, ("to", l, t))

                for d in range(KD + 1):
                    if d < KD:
                        key = ("wo", l, d)
                        wait_room(pe, key)
                        for k in range(KD):
                            wk = ("wo", l, d // 4, k // 4)
                            weights(wk)
                            ins = mm_(pair(key)[:, 0:TOK], slot(wk, 4, 512)[:, k % 4, (d % 4) * P:(d % 4 + 1) * P], hT[:, k, :],
                                      start=(k == 0), stop=(k == KD - 1))
                            if d % 4 == 3 and k == 3:
                                used_up(ins, wk)
                        full(ins, key)
                    if d >= 1:
                        turn_back(("ty", l, d - 1), yT[:, 0, (d - 1) % 2, :], ("wo", l, d - 1),
                                  last_of=("wo", l, d // 4 - 1, 1) if d % 4 == 0 else None)
                for t in range(3):
                    pe.wait_ge(xn_ready, norm_no(l, 1, t))
                    turn(("hf", l, t), xn[:, t, :], ROWS[t])
                for t in range(3):
                    wait_out(pe, ("hf", l, t))
                if l == 0:
                    pe.wait_ge(tok_ready, 3)
                    for n, (kind, i, *rest) in enumerate(DENSE):
                        hi, lo = w_hi[n % DENSE_PAIRS], w_lo[n % DENSE_PAIRS]
                        if kind != "down":
                            hi, lo = (w[:, :].rearrange("p (k c) -> p k c", k=KD) for w in (hi, lo))
                            key = (kind, i)
                            wait_room(pe, key)
                            pe.wait_ge(lo_ready, n + 1)
                            for f in range(2):
                                for k in range(KD):
                                    for m, (w, x) in enumerate(((hi, hT_hi), (hi, hT_lo), (lo, hT_hi))):
                                        ins = mm_(pair(key)[:, 512 * f:512 * f + TOK], w[:, k, f * P:(f + 1) * P], x[:, k, :],
                                                  start=(k == 0 and m == 0), stop=(k == KD - 1 and m == 2))
                            full(ins, key)
                            continue
                        g = rest[0]
                        hi, lo = (w[:, :].rearrange("p (k c) -> p k c", k=4) for w in (hi, lo))
                        if g == 0:
                            for h in range(2):
                                wait_room(pe, ("dn", i, h))
                        pe.wait_ge(dense_act, min(DCH, 2 * g + 2))
                        pe.wait_ge(lo_ready, n + 1)
                        last = min(4, FT - 4 * g) - 1
                        for k in range(last + 1):
                            for d in range(4):
                                for m, (w, x) in enumerate(((hi, aT_hi), (hi, aT_lo), (lo, aT_hi))):
                                    kk = 4 * g + k
                                    ins = mm_(pair(("dn", i, d // 2))[:, 512 * (d % 2):512 * (d % 2) + TOK], w[:, k, d * P:(d + 1) * P],
                                              x[:, kk, :], start=(kk == 0 and m == 0), stop=(kk == FT - 1 and m == 2))
                                if kk == FT - 1 and d % 2 == 1:
                                    full(ins, ("dn", i, d // 2))
                        if g < 5:
                            ins.then_inc(pair_used, 1)
                        else:
                            for d in range(4 * i, 4 * i + 4):
                                turn_back(("tz", d), yT[:, d // 2 % 2, d % 2, :], ("dn", i, d // 2 % 2))

            key = ("router",)
            wait_room(pe, key)
            for t in range(3):
                r = ROWS[t]
                for k in range(KD):
                    ins = mm_(pair(key, r)[:, NE * t:NE * t + NE], hT[:, k, TOFF[t]:TOFF[t] + r], wr[:, k, :],
                              start=(k == 0), stop=(k == KD - 1))
            full(ins, key)
            key = ("pos",)
            wait_room(pe, key)
            pe.wait_ge(pair_diff, 1)
            for t in range(3):
                r = ROWS[t]
                for u in range(t + 1):
                    lhs = C("upper", r)[:, 0:r] if u == t else C("ones")[:, 0:r]
                    mm_(pair(key, r)[:, NE * t:NE * t + NE], lhs, member[0:ROWS[u], u, :], start=(u == 0), stop=(u == t))
            for u in range(3):
                ins = mm_(pair(key, 1)[:, NE * 3:NE * 4], C("ones", ROWS[u])[:, 0:1], member[0:ROWS[u], u, :],
                          start=(u == 0), stop=(u == 2))
            full(ins, key)

            pe.wait_ge(plan_ready, 1)
            rounds = pe.value_load(nround[0:1, 0:1], min_val=1, max_val=ROUNDS)
            PARTS = ((0, 0), (0, 1), (1, 0))

            def gather(count):
                pe.wait_ge(pick_ready, count)
                for k in range(KD):
                    for t in range(3):
                        for m, x in enumerate((xn_hi, xn_lo)):
                            ins = mm_(ps[:, k // 4, (k % 4) * P:(k % 4 + 1) * P], x[0:ROWS[t], t, k * P:(k + 1) * P],
                                      pick[0:ROWS[t], t, :], start=(t == 0 and m == 0), stop=(t == 2 and m == 1))
                ins.then_inc(gathered, 1)

            def scatter(t, done, first_inc=None):
                for h in range(2):
                    for m, y in enumerate((y_hi, y_lo)):
                        ins = mm_(ps[0:ROWS[t], SC_BANKS[t] + h, :], pickT[:, TOFF[t]:TOFF[t] + ROWS[t]],
                                  y[:, 512 * h:512 * h + 512], start=(m == 0), stop=(m == 1))
                        if first_inc is not None and h == 0 and m == 0:
                            ins.then_inc(first_inc, 1)
                ins.then_inc(done, 1)

            pe.wait_ge(tok_ready, 6)
            gather(1)
            with pe.Fori(0, rounds) as r_:
                with pe.Fori(0, NE) as e:
                    j = pe.snap(r_ * NE + e)

                    def wait_unit(u):
                        pe.wait_ge(lo_ready, j * len(EXPERT) + (ND + u + 1))

                    def gate_up(c, parts=(0, 1)):
                        q = c % 2
                        if c >= 2:
                            pe.wait_ge(gu_free[q], j * 3 + c // 2)
                        for m in parts:
                            for k in range(KD):
                                u = unit[("gate", "up")[m], c, k // 4]
                                if k % 4 == 0:
                                    wait_unit(u)
                                w = [x[u % MOE_PAIRS][:, 0:4 * WIDTH[c]].rearrange("p (k c) -> p k c", k=4) for x in (w_hi, w_lo)]
                                for n, (wp, xp) in enumerate(PARTS):
                                    ins = mm_(ps[:, 2 * (1 - q) + m, 0:WIDTH[c]], (xg_hi, xg_lo)[xp][:, k, :], w[wp][:, k % 4, :],
                                              start=(k == 0 and n == 0), stop=(k == KD - 1 and n == 2))
                                if k % 4 == 3 and not (m == 1 and k == KD - 1):
                                    ins.then_inc(pair_used, 1)
                        if 1 in parts:
                            ins.then_inc(gu_full[q], 1)

                    def turn_chunk(c):
                        b, w = c % 2, WIDTH[c] // P
                        pe.wait_ge(gu_free[b], j * 3 + (c // 2 + 1))
                        if c == 1:
                            pe.wait_ge(pickT_free, j + 1)
                        if c >= 2:
                            pe.wait_ge(aT_free, j * CHUNKS + (c - 1))
                        for k in range(w):
                            ins = tr(ps[:, 5 if b == 0 else 4, k * P:(k + 1) * P], act_m[:, b, k * P:(k + 1) * P], ident)
                        ins.then_inc(aT_full, 1)

                    def down(c):
                        b, n = c % 2, WIDTH[c] // P // 2
                        pe.wait_ge(aT_free, j * CHUNKS + (c + 1))
                        for k in range(2 * n):
                            u = unit["down", c, k // n]
                            if k % n == 0:
                                wait_unit(u)
                            w = [x[u % MOE_PAIRS][:, 0:n * D].rearrange("p (k c) -> p k c", k=n) for x in (w_hi, w_lo)]
                            first, last = (c == 0 and k == 0), (c == CHUNKS - 1 and k == 2 * n - 1)
                            for h in range(2):
                                for i, (wp, xp) in enumerate(PARTS):
                                    ins = mm_(ps[:, 6 + h, :], (am_hi, am_lo)[xp][:, b, k, :], w[wp][:, k % n, 512 * h:512 * h + 512],
                                              start=(first and i == 0), stop=(last and i == 2))
                                    if c + 2 < CHUNKS and k == 0 and h == 0 and i == 0:
                                        ins.then_inc(pair_used, 1)
                            if k % n == n - 1:
                                ins.then_inc(y_full if last else pair_used, 1)

                    pe.wait_ge(xg_ready, j + 1)
                    gate_up(0, (0,))
                    pe.wait_ge(y_free, j + 1)
                    scatter(0, sc_full)
                    scatter(1, sc_full)
                    gate_up(0, (1,))
                    pe.wait_ge(sc_free, j * 3 + 2)
                    scatter(2, sc_full, pair_used)
                    gate_up(1)
                    pe.wait_ge(sc_free, j * 3 + 3)
                    for t in range(3):
                        ins = tr(ps[:, 4, TOFF[t]:TOFF[t] + ROWS[t]], pick[0:ROWS[t], t, :].bitcast(F32), ident[0:ROWS[t], 0:ROWS[t]])
                        if t == 0:
                            ins.then_inc(pair_used, 1)
                    for t in range(3):
                        ins = mm_(ps[:, 4, TOK:TOK + 1], pick[0:ROWS[t], t, :].bitcast(F32), gcol[0:ROWS[t], t:t + 1],
                                  start=(t == 0), stop=(t == 2))
                    ins.then_inc(pickT_full, 1)
                    turn_chunk(0)
                    for c in range(2, CHUNKS):
                        gate_up(c)
                        down(c - 2)
                        turn_chunk(c - 1)
                    pe.wait_ge(gu_free[1], j * 3 + 3)
                    gather(j + 2)
                    turn_chunk(CHUNKS - 1)
                    down(CHUNKS - 2)
                    down(CHUNKS - 1)
            pe.wait_ge(y_free, rounds * NE + 1)
            pe.wait_ge(xg_ready, rounds * NE + 1)
            for t in range(3):
                if t == 2:
                    pe.wait_ge(moe_done, 2)
                scatter(t, last_full)


_INS = ["x_prompt", "x_sample", "cache_swa_k", "cache_swa_v", "cache_mla_ckv", "cache_mla_krope", "ln_attn", "w_in",
        "a_q_norm", "a_k_norm", "a_sinks", "b_cq_norm", "b_w_uq", "b_ckv_norm", "b_w_ukv", "b_qn_norm", "b_qr_norm",
        "b_kn_norm", "b_kr_norm", "w_o", "ln_ffn", "ffn_w_gate", "ffn_w_up", "ffn_w_down", "moe_router", "moe_w_gate",
        "moe_w_up", "moe_w_down"]
_OUTS = [("y_p", (1, SEQ, D)), ("y_s", (1, DEC, D)), ("k_p", (DEPTH, 1, WINDOW, KVH, HD)), ("v_p", (DEPTH, 1, WINDOW, KVH, HD)),
         ("ckv_p", (DEPTH, 1, SEQ, KL)), ("kr_p", (DEPTH, 1, SEQ, ROPE)), ("k_s", (DEPTH, 1, DEC, KVH, HD)),
         ("v_s", (DEPTH, 1, DEC, KVH, HD)), ("ckv_s", (DEPTH, 1, DEC, KL)), ("kr_s", (DEPTH, 1, DEC, ROPE))]


def shape_constants():
    import numpy as np

    out = np.zeros((P, CONST_W), np.float32)

    def put(name, v):
        at, w = CONST[name]
        out[:, at:at + w] = v

    row = np.arange(P)
    put("ident", np.eye(P))
    put("upper", row[:, None] < row[None, :])
    put("ones", 1.0)
    put("iota", row[None, :])
    for w, c_name, s_name in ((HD, "c64", "s64"), (ROPE, "c32", "s32")):
        half = w // 2
        inv = np.float32(10000.0) ** (-(np.arange(half, dtype=np.float32) / np.float32(half)))
        for tile in range(2):
            ang = (row + P * tile).astype(np.float32)[:, None] * inv[None, :]
            c, s = np.cos(ang), np.sin(ang)
            at = CONST[c_name][0] + tile * w
            out[:, at:at + w] = np.concatenate([c, c], 1)
            at = CONST[s_name][0] + tile * w
            out[:, at:at + w] = np.concatenate([-s, s], 1)
    q, k = row[:, None] // CHUNK, np.arange(2 * P)[None, :] // CHUNK
    put("mask0", np.where(k[:, :P] <= q, 0.0, -1e30))
    q = q + P // CHUNK
    put("mask1a", np.where((k <= q) & (k >= q - WINDOW // CHUNK), 0.0, -1e30))
    put("mask1b", np.where(k <= q, 0.0, -1e30))
    put("inv_a", np.array([1 / HD] * 10 + [1 / QL, 1 / KL, 1 / ROPE], np.float32)[None, :])
    put("inv_b", np.array([1 / NOPE] * 8 + [1 / ROPE] * 8, np.float32)[None, :])
    put("eps", EPS)
    return out


def kernel(**inputs):
    import numpy as _np
    import concourse.bacc as _bacc
    from concourse.bass_utils import run_bass_kernel_spmd as _run

    nc = _bacc.Bacc("TRN2", target_bir_lowering=False, num_devices=1)
    arrays, a, out = {}, {}, {}
    for name in _INS:
        v = _np.ascontiguousarray(inputs[name])
        arrays[f"in_{name}"] = v
        a[name] = nc.dram_tensor(f"in_{name}", v.shape, mybir.dt.from_np(v.dtype), kind="ExternalInput").ap()
    arrays["shape_consts"] = shape_constants()
    consts = nc.dram_tensor("shape_consts", (P, CONST_W), F32, kind="ExternalInput").ap()
    for name, shape in _OUTS:
        out[name] = nc.dram_tensor(f"out_{name}", shape, F32, kind="ExternalOutput").ap()
    build(nc, a, out, consts)
    r = _run(nc, [arrays], core_ids=[0])
    return tuple(r.results[0][f"out_{name}"] for name, _ in _OUTS)
```
